# Optimizing a Trainium2 kernel written in Bass

```python
import jax, jax.numpy as jnp
from jax import lax
import numpy as np

D_MODEL = 1024
BATCH = 1
SEQ = 512
DEPTH = 2

GRID_W = 64
CTX_LEN = 256
EPS = 1e-6
N_HEADS = 8
N_KV_HEADS = 2
GQA_GROUP = N_HEADS // N_KV_HEADS
HEAD_DIM = 64
ATTN_WIDTH = N_HEADS * HEAD_DIM
KV_WIDTH = N_KV_HEADS * HEAD_DIM
ATTN_SCALE = HEAD_DIM ** -0.5
ROPE_THETA = 10000.0
ROPE_PAIRS_PER_AXIS = HEAD_DIM // 4
Q_BLOCK = 128
CONV_A_WIDTH = D_MODEL // 2
CONV_A_K = 31
EVEN_IN = ATTN_WIDTH + 2 * KV_WIDTH + 2 * CONV_A_WIDTH
EVEN_SPLITS = (ATTN_WIDTH, ATTN_WIDTH + KV_WIDTH, ATTN_WIDTH + 2 * KV_WIDTH,
               ATTN_WIDTH + 2 * KV_WIDTH + CONV_A_WIDTH)
EVEN_OUT = ATTN_WIDTH + CONV_A_WIDTH
SC_WIDTH = D_MODEL
SC_K = 3
N_EXPERTS = 16
N_GROUPS = 4
EXPERTS_PER_GROUP = N_EXPERTS // N_GROUPS
TOP_K = 2
D_EXPERT = 512
MOE_BLOCK = 256
N_EVEN = (DEPTH + 1) // 2
N_ODD = DEPTH // 2
LAST_ATTN_LAYER = (DEPTH - 1) - ((DEPTH - 1) % 2)

kernel_name = "hybrid_dit_conformer_gqa_shortconv_moe"

def rms_norm(x, g):
    xf = x.astype(jnp.float32)
    y = xf * lax.rsqrt(jnp.mean(xf * xf, axis=-1, keepdims=True) + EPS)
    return (y * g.astype(jnp.float32)).astype(x.dtype)

def layer_norm(x, g, b):
    xf = x.astype(jnp.float32)
    mu = jnp.mean(xf, axis=-1, keepdims=True)
    var = jnp.mean(jnp.square(xf - mu), axis=-1, keepdims=True)
    y = (xf - mu) * lax.rsqrt(var + EPS)
    return (y * g.astype(jnp.float32) + b.astype(jnp.float32)).astype(x.dtype)

def modulate(h, shift, scale):
    return h * (1 + scale) + shift

def depthwise_conv(x, w, pad):
    return lax.conv_general_dilated(x, w[:, None, :], window_strides=(1,), padding=[(pad, pad)],
                                    dimension_numbers=("NWC", "WIO", "NWC"),
                                    feature_group_count=x.shape[-1])

def axial_rope_tables(n_tokens):
    rows = n_tokens // GRID_W
    row = jnp.repeat(jnp.arange(rows, dtype=jnp.float32), GRID_W)
    col = jnp.tile(jnp.arange(GRID_W, dtype=jnp.float32), rows)
    inv = ROPE_THETA ** (-jnp.arange(ROPE_PAIRS_PER_AXIS, dtype=jnp.float32) / ROPE_PAIRS_PER_AXIS)
    ang = jnp.concatenate([row[:, None] * inv, col[:, None] * inv], axis=-1)
    return jnp.cos(ang), jnp.sin(ang)

def apply_rope(x, cos, sin):
    bshape = (1, cos.shape[0]) + (1,) * (x.ndim - 3) + (cos.shape[1],)
    cs, sn = cos.reshape(bshape), sin.reshape(bshape)
    xf = x.astype(jnp.float32).reshape(x.shape[:-1] + (HEAD_DIM // 2, 2))
    x1, x2 = xf[..., 0], xf[..., 1]
    out = jnp.stack([x1 * cs - x2 * sn, x1 * sn + x2 * cs], axis=-1)
    return out.reshape(x.shape).astype(x.dtype)

def gqa_attend(q, k, v):
    s = jnp.einsum("bqhgd,bkhd->bhgqk", q * ATTN_SCALE, k).astype(jnp.float32)
    p = jax.nn.softmax(s, axis=-1).astype(v.dtype)
    return jnp.einsum("bhgqk,bkhd->bqhgd", p, v)

def split_even(p, q_g, k_g):
    b, l, _ = p.shape
    q, k, v, a, a_gate = jnp.split(p, EVEN_SPLITS, axis=-1)
    q = rms_norm(q.reshape(b, l, N_KV_HEADS, GQA_GROUP, HEAD_DIM), q_g)
    k = rms_norm(k.reshape(b, l, N_KV_HEADS, HEAD_DIM), k_g)
    v = v.reshape(b, l, N_KV_HEADS, HEAD_DIM)
    return q, k, v, a * jax.nn.sigmoid(a_gate)

def conformer_conv(a, dw_w, dw_b, ln_g, ln_b):
    y = depthwise_conv(a, dw_w, CONV_A_K // 2) + dw_b
    return jax.nn.silu(layer_norm(y, ln_g, ln_b))

def even_mixer(hx, hz, w_in, q_g, k_g, dw_w, dw_b, ln_g, ln_b, w_out, cos, sin, ctx_out):
    b, s, _ = hx.shape
    qx, kx, vx, ax = split_even(hx @ w_in, q_g, k_g)
    qx = apply_rope(qx, cos, sin)
    kx = apply_rope(kx, cos, sin)
    if ctx_out:
        qz, kz, vz, az = split_even(hz @ w_in, q_g, k_g)
    else:
        kz, vz = jnp.split(hz @ w_in[:, ATTN_WIDTH:ATTN_WIDTH + 2 * KV_WIDTH], 2, axis=-1)
        kz = rms_norm(kz.reshape(b, -1, N_KV_HEADS, HEAD_DIM), k_g)
        vz = vz.reshape(b, -1, N_KV_HEADS, HEAD_DIM)
    k_all = jnp.concatenate([kx, kz], axis=1)
    v_all = jnp.concatenate([vx, vz], axis=1)
    n_blk = s // Q_BLOCK
    q_blocks = qx.reshape(b, n_blk, Q_BLOCK, N_KV_HEADS, GQA_GROUP, HEAD_DIM).swapaxes(0, 1)
    attn_x = lax.map(lambda qb: gqa_attend(qb, k_all, v_all), q_blocks)
    attn_x = attn_x.swapaxes(0, 1).reshape(b, s, ATTN_WIDTH)
    ox = jnp.concatenate([attn_x, conformer_conv(ax, dw_w, dw_b, ln_g, ln_b)], axis=-1) @ w_out
    if not ctx_out:
        return ox, None
    attn_z = gqa_attend(qz, kz, vz).reshape(b, -1, ATTN_WIDTH)
    oz = jnp.concatenate([attn_z, conformer_conv(az, dw_w, dw_b, ln_g, ln_b)], axis=-1) @ w_out
    return ox, oz

def short_conv_mixer(h, w_in, conv_w, w_out):
    gb, gc, v = jnp.split(h @ w_in, 3, axis=-1)
    return (gb * depthwise_conv(gc * v, conv_w, SC_K // 2)) @ w_out

def route(h, router_w, router_bias):
    aff = jax.nn.sigmoid((h @ router_w).astype(jnp.float32))
    sel = (aff + router_bias.astype(jnp.float32)).reshape(-1, N_GROUPS, EXPERTS_PER_GROUP)
    grp_score = lax.top_k(sel, 2)[0].sum(-1)
    grp = jnp.argmax(grp_score, axis=-1)
    sel_in = jnp.take_along_axis(sel, grp[:, None, None], axis=1)[:, 0]
    _, local = lax.top_k(sel_in, TOP_K)
    e_idx = (grp[:, None] * EXPERTS_PER_GROUP + local).astype(jnp.int32)
    w = jnp.take_along_axis(aff, e_idx, axis=1)
    return e_idx, w / w.sum(-1, keepdims=True)

def moe_ffn(h, router_w, router_bias, w_gate, w_up, w_down):
    n_tok = h.shape[0]
    n_assign = n_tok * TOP_K
    e_idx, e_w = route(h, router_w, router_bias)
    flat_e = e_idx.reshape(-1)
    order = jnp.argsort(flat_e)
    counts = jnp.bincount(flat_e, length=N_EXPERTS).astype(jnp.int32)
    padded = (counts + MOE_BLOCK - 1) // MOE_BLOCK * MOE_BLOCK
    starts = jnp.cumsum(counts) - counts
    pad_ends = jnp.cumsum(padded)
    pad_starts = pad_ends - padded
    sorted_e = flat_e[order]
    dest_sorted = pad_starts[sorted_e] + jnp.arange(n_assign, dtype=jnp.int32) - starts[sorted_e]
    dest = jnp.zeros((n_assign,), jnp.int32).at[order].set(dest_sorted.astype(jnp.int32))
    n_blocks = -(-n_assign // MOE_BLOCK) + N_EXPERTS
    n_rows = n_blocks * MOE_BLOCK
    row_token = jnp.full((n_rows,), n_tok, jnp.int32).at[dest].set(
        jnp.arange(n_assign, dtype=jnp.int32) // TOP_K)
    block_e = jnp.minimum(jnp.searchsorted(pad_ends, jnp.arange(n_blocks, dtype=jnp.int32) * MOE_BLOCK,
                                           side="right"), N_EXPERTS - 1)

    def expert_block(args):
        tok, e = args
        xb = jnp.take(h, tok, axis=0, mode="fill", fill_value=0)
        return (jax.nn.silu(xb @ w_gate[e]) * (xb @ w_up[e])) @ w_down[e]

    out = lax.map(expert_block, (row_token.reshape(n_blocks, MOE_BLOCK), block_e)).reshape(n_rows, -1)
    y = out[dest].reshape(n_tok, TOP_K, -1) * e_w[..., None].astype(h.dtype)
    return y.sum(axis=1)

def setup_inputs(seed: int = 0) -> dict:
    key = jax.random.key(seed)
    ks = jax.random.split(key, 24)
    D = D_MODEL

    def nrm(k, shape, scale):
        return jax.random.normal(k, shape, jnp.float32) * scale

    return {
        "x": nrm(ks[0], (BATCH, SEQ, D), 1.0),
        "c": nrm(ks[1], (BATCH, D), 1.0),
        "ctx": nrm(ks[2], (BATCH, CTX_LEN, D), 1.0),
        "c_ctx": nrm(ks[3], (D,), 1.0),
        "w_mod": nrm(ks[4], (DEPTH, D, 6 * D), 0.5 * D ** -0.5),
        "b_mod": nrm(ks[5], (DEPTH, 6 * D), 0.02),
        "norm_mix_g": 1.0 + nrm(ks[6], (DEPTH, D), 0.02),
        "norm_ffn_g": 1.0 + nrm(ks[7], (DEPTH, D), 0.02),
        "ev_w_in": nrm(ks[8], (N_EVEN, D, EVEN_IN), D ** -0.5),
        "ev_q_norm_g": 1.0 + nrm(ks[9], (N_EVEN, HEAD_DIM), 0.02),
        "ev_k_norm_g": 1.0 + nrm(ks[10], (N_EVEN, HEAD_DIM), 0.02),
        "ev_dw_w": nrm(ks[11], (N_EVEN, CONV_A_K, CONV_A_WIDTH), CONV_A_K ** -0.5),
        "ev_dw_b": nrm(ks[12], (N_EVEN, CONV_A_WIDTH), 0.02),
        "ev_ln_g": 1.0 + nrm(ks[13], (N_EVEN, CONV_A_WIDTH), 0.02),
        "ev_ln_b": nrm(ks[14], (N_EVEN, CONV_A_WIDTH), 0.02),
        "ev_w_out": nrm(ks[15], (N_EVEN, EVEN_OUT, D), EVEN_OUT ** -0.5),
        "od_w_in": nrm(ks[16], (N_ODD, D, 3 * SC_WIDTH), D ** -0.5),
        "od_conv_w": nrm(ks[17], (N_ODD, SC_K, SC_WIDTH), SC_K ** -0.5),
        "od_w_out": nrm(ks[18], (N_ODD, SC_WIDTH, D), SC_WIDTH ** -0.5),
        "router_w": nrm(ks[19], (D, N_EXPERTS), D ** -0.5),
        "router_bias": nrm(ks[20], (N_EXPERTS,), 0.01),
        "moe_w_gate": nrm(ks[21], (DEPTH, N_EXPERTS, D, D_EXPERT), D ** -0.5),
        "moe_w_up": nrm(ks[22], (DEPTH, N_EXPERTS, D, D_EXPERT), D ** -0.5),
        "moe_w_down": nrm(ks[23], (DEPTH, N_EXPERTS, D_EXPERT, D), D_EXPERT ** -0.5),
    }

def reference(x, c, ctx, c_ctx, w_mod, b_mod, norm_mix_g, norm_ffn_g, ev_w_in, ev_q_norm_g,
              ev_k_norm_g, ev_dw_w, ev_dw_b, ev_ln_g, ev_ln_b, ev_w_out, od_w_in, od_conv_w,
              od_w_out, router_w, router_bias, moe_w_gate, moe_w_up, moe_w_down):
    b, s, d = x.shape
    cos, sin = axial_rope_tables(s)
    z = ctx
    c_act = jax.nn.silu(c)
    cz_act = jax.nn.silu(c_ctx)
    n_lat = b * s
    for l in range(DEPTH):
        i = l // 2
        is_attn = l % 2 == 0
        ctx_in = l <= LAST_ATTN_LAYER
        ctx_out = l < LAST_ATTN_LAYER
        mx = jnp.split(c_act @ w_mod[l] + b_mod[l], 6, axis=-1)
        hx = modulate(rms_norm(x, norm_mix_g[l]), mx[0][:, None], mx[1][:, None])
        hz = None
        if ctx_in:
            mz = jnp.split(cz_act @ w_mod[l] + b_mod[l], 6, axis=-1)
            hz = modulate(rms_norm(z, norm_mix_g[l]), mz[0], mz[1])
        if is_attn:
            ox, oz = even_mixer(hx, hz, ev_w_in[i], ev_q_norm_g[i], ev_k_norm_g[i], ev_dw_w[i],
                                ev_dw_b[i], ev_ln_g[i], ev_ln_b[i], ev_w_out[i], cos, sin, ctx_out)
        else:
            ox = short_conv_mixer(hx, od_w_in[i], od_conv_w[i], od_w_out[i])
            oz = short_conv_mixer(hz, od_w_in[i], od_conv_w[i], od_w_out[i]) if ctx_out else None
        x = x + mx[2][:, None] * ox
        hx = modulate(rms_norm(x, norm_ffn_g[l]), mx[3][:, None], mx[4][:, None])
        if ctx_out:
            z = z + mz[2] * oz
            hz = modulate(rms_norm(z, norm_ffn_g[l]), mz[3], mz[4])
            tokens = jnp.concatenate([hx.reshape(-1, d), hz.reshape(-1, d)], axis=0)
        else:
            tokens = hx.reshape(-1, d)
        y = moe_ffn(tokens, router_w, router_bias, moe_w_gate[l], moe_w_up[l], moe_w_down[l])
        x = x + mx[5][:, None] * y[:n_lat].reshape(b, s, d)
        if ctx_out:
            z = z + mz[5] * y[n_lat:].reshape(z.shape)
    return x


_drawn_inputs = setup_inputs


def setup_inputs(seed=0):
    import zlib

    import numpy as np

    out = dict(_drawn_inputs(seed))
    spreads = {}
    factors = {'ev_q_norm_g': 16.617,
     'ev_k_norm_g': 15.792,
     'ev_dw_b': 3.205,
     'ev_ln_g': 9.936,
     'ev_ln_b': 21.508,
     'norm_ffn_g': 3.238}
    for name, (base, spread) in spreads.items():
        noise = np.random.default_rng([zlib.crc32(name.encode()), seed]).standard_normal(out[name].shape)
        drawn = base * np.exp(spread * noise) if base else spread * noise
        out[name] = __import__('jax').numpy.asarray(drawn.astype(out[name].dtype))
    for name, factor in factors.items():
        out[name] = (out[name] * factor).astype(out[name].dtype)
    return out
```

```python
from contextlib import ExitStack

import numpy as np

import concourse.bass as bass
from concourse import mybir

F32 = mybir.dt.float32
I32 = mybir.dt.int32
ALU = mybir.AluOpType
ACT = mybir.ActivationFunctionType
AX_X = mybir.AxisListType.X

P = 128
D = 1024
KD = D // P
SEQ = 512
TT = SEQ // P
CTX = 256
CT = CTX // P
KT = TT + CT
HEADS, KVH, HD = 8, 2, 64
PAIRS = HEADS // 2
GRID_W = 64
CONV_K, CONV_C = 31, 512
PAD = CONV_K // 2
APAD = SEQ + 2 * PAD
SC_K = 3
NE, NG, EPG = 16, 4, 4
FE = 512
BLK = 64
MAXB = SEQ * 2 // BLK + NE
NB = MAXB + 1
NIDX = 4096
EPS = 1e-6
RING = 6
NBANK = 4

WITH_A = [(0, 6), (0, 7), (0, 8), (0, 9)]
WITH_AG = [(1, 0), (1, 1), (1, 2), (1, 3)]
WITH_Q = [(1, 6), (1, 7), (1, 8), (1, 9)]
GATES = [[(l, 4), (l, 5), (l, 10), (l, 11)] for l in range(2)]

CONSTS = {}


def build_consts():
    p = np.arange(P)
    parts = []

    def add(name, a):
        a = np.asarray(a, np.float32).reshape(P, -1)
        at = sum(x.shape[1] for x in parts)
        CONSTS[name] = (at, at + a.shape[1])
        parts.append(a)

    add("ident", np.eye(P))
    add("ones", np.ones((P, P)))
    add("before", p[:, None] < p[None, :])
    add("sel_both", np.stack([p % 32 == 0, p % 32 == 1], 1))
    add("sel_x", np.repeat((p % 32 == 0)[:, None], P, 1))
    add("ident_twice", np.repeat(np.eye(P)[:, :24], 2, 1))
    add("slot_of_col", np.tile(p % BLK, (P, 1)))
    add("block_id", np.tile(np.arange(NB), (P, 1)))
    add("half", p // BLK)
    add("full_blocks", np.tile(np.arange(1, SEQ // BLK) * BLK, (P, 1)))
    add("group_key", np.tile(NG - np.arange(NG), (P, 1)))
    add("expert_key", np.tile(NE - np.arange(NE), (P, 1)))
    add("expert_before", np.tile((np.arange(NE)[None, :] < np.arange(NE + 1)[:, None]).ravel(), (P, 1)))
    token = np.arange(TT)[None, :, None] * P + p[:, None, None] + np.zeros((1, 1, 2))
    add("token", token)
    add("out_row", token + SEQ * np.arange(2)[None, None, :] - NIDX)
    add("minus_half", np.full((P, 1), -0.5))
    t = np.arange(SEQ)
    inv = (np.float32(10000.0) ** (-np.arange(HD // 4, dtype=np.float32) / np.float32(HD // 4))).astype(np.float32)
    ang = np.concatenate([(t // GRID_W).astype(np.float32)[:, None] * inv,
                          (t % GRID_W).astype(np.float32)[:, None] * inv], -1).astype(np.float32)
    for name, f in (("cos", np.cos), ("sin", np.sin)):
        add(name, f(ang.astype(np.float64)).reshape(TT, P, HD // 2).transpose(1, 0, 2))
    return np.ascontiguousarray(np.concatenate(parts, 1))


def plan_units():
    order = [("mod", 0, c) for c in range(4)] + [("kv",), ("a",)]
    order += [("mod",) + m for m in WITH_A] + [("ag",)] + [("mod",) + m for m in WITH_AG]
    order += [("q",)] + [("mod",) + m for m in WITH_Q] + [("mod",) + m for m in GATES[0]] + [("wo", 0), ("wo", 1)]
    return order


def plan_units_odd():
    return ([("gc", 0), ("v", 0), ("gb", 0), ("mod", 1, 4), ("mod", 1, 5), ("gc", 1), ("v", 1), ("gb", 1),
             ("mod", 1, 10), ("mod", 1, 11), ("ow", 0), ("ow", 1)])


def plan_groups():
    g = [("params",), ("taps",)]
    for c in range(4):
        g += [("mod", 0, c), ("fin", 0, c)]
    g += [("norm", "ctx", j) for j in range(KD)] + [("norm", "mix0", j) for j in range(KD)]
    g += [("kvz", t) for t in range(CT)] + [("kvx", t) for t in range(TT)]
    for i in range(4):
        g += [("a", i), ("mod",) + WITH_A[i], ("fin",) + WITH_A[i]]
    for i in range(4):
        g += [("ag", i), ("mod",) + WITH_AG[i], ("fin",) + WITH_AG[i]]
    g += [("kT", v, h) for v in range(KVH) for h in range(2)]
    for i in range(4):
        g += [("q", i), ("mod",) + WITH_Q[i], ("fin",) + WITH_Q[i]]
    g += [("qT", i) for i in range(PAIRS)]
    for s in range(8):
        for u in range(4):
            g += [("PT", s, u, 0), ("PT", s, u, 1)]
        g += [("pv", s)]
    g += [("mu",), ("var",)]
    for m in GATES[0]:
        g += [("mod",) + m, ("fin",) + m]
    g += [("out", 0, h, t) for h in range(2) for t in range(TT)]
    g += [("norm", "ffn0", j) for j in range(KD)] + [("route", 0, k) for k in range(3)]
    g += [("norm", "mix1", j) for j in range(KD)]
    for h in range(2):
        for i in range(4):
            g += [(w, h * 4 + i) for w in ("gc", "v", "gb")]
        for m in GATES[1][2 * h:2 * h + 2]:
            g += [("mod",) + m, ("fin",) + m]
    g += [("out", 1, h, t) for h in range(2) for t in range(TT)]
    g += [("norm", "ffn1", j) for j in range(KD)] + [("route", 1, k) for k in range(3)]
    return g


GROUPS = plan_groups()
GROUP_AT = {name: n for n, name in enumerate(GROUPS)}
assert len(GROUP_AT) == len(GROUPS)


def hybrid_backbone_kernel(nc, x, c, ctx, c_ctx, w_mod, b_mod, norm_mix_g, norm_ffn_g, ev_w_in,
                           ev_q_norm_g, ev_k_norm_g, ev_dw_w, ev_dw_b, ev_ln_g, ev_ln_b, ev_w_out,
                           od_w_in, od_conv_w, od_w_out, router_w, router_bias, moe_w_gate, moe_w_up,
                           moe_w_down, consts, out):
    stack = ExitStack()
    with stack:
        def sb(name, shape, dt=F32):
            return stack.enter_context(nc.sbuf_tensor(name, shape, dt))

        def sem(name):
            return stack.enter_context(nc.semaphore(name))

        ring = sb("ring", [P, RING, KD, 512])
        xs = sb("xs", [P, TT, D])
        hT_cat = sb("hT_cat", [P, KD, SEQ])
        big = sb("big", [P, 4096])
        mid = sb("mid", [P, 4096])
        qT = sb("qT", [P, PAIRS, SEQ])
        kv_buf = sb("kv_buf", [P, 3 * KT * P])
        cact = sb("cact", [P, KD, 32])
        b_rows = sb("b_rows", [P, 512])
        prob = sb("prob", [P, 2, KT * P])
        apad = sb("apad", [P, 4, APAD])
        cst = sb("cst", [P, consts.shape[1]])
        modrow = sb("modrow", [P, 512])
        params = sb("params", [P, 44])
        taps = sb("taps", [P, KD, 34])
        modcol = sb("modcol", [P, 2, 12, 4, 2])
        mod_a = sb("mod_a", [P, 5, KD])
        stats = sb("stats", [P, 4, KT])
        qkg = sb("qkg", [P, 2, HD])
        head_stats = sb("head_stats", [P, 4, 32])
        softm = sb("softm", [P, 4, 2])
        bias_r = sb("bias_r", [P, NE])
        small = sb("small", [P, 4])
        block_start = sb("block_start", [P, NE + 1], I32)
        route_w = sb("route_w", [P, KD, NE])
        rowid = sb("rowid", [P, 3, NB])
        row_i = sb("row_i", [P, 2, NB], I32)
        cur_idx = sb("cur_idx", [P, 2, 1], I32)
        tick = sb("tick", [P, 1])

        xhat = big[:, 0:4096].rearrange("p (t d) -> p t d", t=TT)
        ctx_x = kv_buf[:, 0:CT * D].rearrange("p (t d) -> p t d", t=CT)
        kT2 = kv_buf[:, 0:KVH * KT * P].rearrange("p (v k) -> p v k", v=KVH)
        vtok = kv_buf[:, KVH * KT * P:].rearrange("p (t d) -> p t d", t=KT)
        PT = [[v.rearrange("p (k q) -> p k q", k=KT) for v in pair] for pair in
              ((big[:, 0:1536], big[:, 1536:3072]),
               (hT_cat[:, 4:7, :].rearrange("p a b -> p (a b)"), mid[:, 0:1536]))]
        junk = mid[:, 0:D]
        gate_mix = qT[:, 0:2, :].rearrange("p a b -> p (a b)")
        gate_ffn = qT[:, 2, :]
        mT = xhat.rearrange("p t (j q) -> p (t j) q", q=512)
        hzT = mid[:, 0:2048].rearrange("p (j t) -> p j t", j=KD)
        ctx_hat = mid[:, 2048:4096].rearrange("p (t d) -> p t d", t=CT)
        qtok = mid[:, 0:2048].rearrange("p (t d) -> p t d", t=TT)
        ktok = prob[:, 0, :].rearrange("p (t d) -> p t d", t=KT)
        qtmp = prob[:, 1, :]
        conv_y = mid[:, 2048:4096].rearrange("p (t d) -> p t d", t=4)
        staging = qT[:, 0:2, :].rearrange("p a b -> p (a b)")
        craw = qT[:, 2, 0:16].rearrange("p (s k) -> p s k", s=2)
        gc_sb = [mid[:, 0:512], mid[:, 512:1024]]
        u_pad = [mid[:, 1024 + 520 * i:1024 + 520 * i + SEQ + 2] for i in range(2)]
        sc_y = [mid[:, 2560:3072], mid[:, 3072:3584]]
        work = apad[:, :, :].rearrange("p a b -> p (a b)")
        hg_raw = work[:, 0:512]
        hgT = work[:, 512:1024].rearrange("p (j s) -> p j s", j=KD)
        silu_g = work[:, 1024:1280]
        act_sb = work[:, 1280:1536]
        actT = work[:, 1536:1792].rearrange("p (j s) -> p j s", j=2)
        y_blk = prob[:, 0, 0:512]
        y_in = [big[:, 0:2048].rearrange("p (k d) -> p k d", k=2), big[:, 2048:4096].rearrange("p (k d) -> p k d", k=2)]
        rt = work
        rt_at = [0]

        def rtmp(*shape):
            n = int(np.prod(shape))
            a = rt[:, rt_at[0]:rt_at[0] + n]
            rt_at[0] += n
            if len(shape) == 1:
                return a
            names = "abcd"[:len(shape)]
            return a.rearrange(f"p ({' '.join(names)}) -> p {' '.join(names)}", **dict(zip(names[1:], shape[1:])))

        aff, sel, selm, oh1, oh2 = (rtmp(TT, NE) for _ in range(5))
        r16, picked, base16 = (rtmp(TT, NE) for _ in range(3))
        g_a, g_b, g_c, g_d = (rtmp(TT, NG) for _ in range(4))
        r4, w_sum = rtmp(TT, 1), rtmp(TT, 1)
        before16, total16 = rtmp(TT, NE), rtmp(TT, NE)
        count16, nblk16 = rtmp(NE), rtmp(NE)
        cmp16 = rtmp(NE, SEQ // BLK - 1)
        start_cmp = rtmp(NE + 1, NE)
        start_f = rtmp(NE + 1)
        pos2, st2, full2, slot2, blk2, w2 = (rtmp(TT, 2) for _ in range(6))
        cmp2 = rtmp(TT * 2, SEQ // BLK - 1)
        assert rt_at[0] <= 4 * APAD
        oh_slot = mid[:, 0:1024].rearrange("p (n s) -> p n s", s=P)
        oh_blk = mid[:, 1024:1024 + 8 * NB].rearrange("p (n b) -> p n b", b=NB)
        val_blk = mid[:, 1536:1536 + 24 * NB].rearrange("p (n v b) -> p n v b", v=3, b=NB)

        def const(name):
            a, b = CONSTS[name]
            return cst[:, a:b]

        ident = const("ident")

        psum = [stack.enter_context(nc.psum_tensor(f"bank{i}", [P, 512], F32)) for i in range(4)]
        score_ps = [stack.enter_context(nc.psum_tensor(f"scores{i}", [P, 1024], F32)) for i in range(2)]
        gate_ps, up_ps, hg_dve_ps, at_ps = psum
        hg_act_ps = score_ps[1][:, 0:2 * P]
        y_ps = score_ps[0][:, 0:512]

        xhat_d = nc.dram_tensor("xhat_d", [SEQ * 2, 512], F32).ap()
        y_d = [nc.dram_tensor(f"y_d{l}", [SEQ * 4, 512], F32).ap() for l in range(2)]

        unit_in = [sem(f"unit_in{s}") for s in range(RING)]
        consts_in, x_in, ctx_in, c_in, rows_in, bmod_in, qkg_in, router_in = (
            sem(n) for n in ("consts_in", "x_in", "ctx_in", "c_in", "rows_in", "bmod_in", "qkg_in", "router_in"))
        zeroed = sem("zeroed")
        cact_ready = sem("cact_ready")
        acc_done = sem("acc_done")
        bank_read = {}
        modrow_ready = sem("modrow_ready")
        modcol_ready = [sem(f"modcol_ready{i}") for i in range(4)]
        gates_ready = sem("gates_ready")
        dve_step, act_step, pool_step = sem("dve_step"), sem("act_step"), sem("pool_step")
        MOD_OF = {"ctx": 0, "mix0": 0, "ffn0": 1, "mix1": 2, "ffn1": 3}
        norms = ("ctx", "mix0", "ffn0", "mix1", "ffn1")
        ssq_ready = {n: sem(f"ssq_{n}") for n in norms}
        rstd_ready = {n: sem(f"rstd_{n}") for n in norms}
        xhat_ready = {n: sem(f"xhat_{n}") for n in norms}
        hT_even = {n: sem(f"hT_even_{n}") for n in norms}
        hT_odd = {n: sem(f"hT_odd_{n}") for n in norms}
        kv_ready = sem("kv_ready")
        k_ssq, k_rstd, q_ssq, q_rstd = sem("k_ssq"), sem("k_rstd"), sem("q_ssq"), sem("q_rstd")
        k_roped, q_roped, q_ready = sem("k_roped"), sem("q_roped"), sem("q_ready")
        kT_ready, qT_ready = sem("kT_ready"), sem("qT_ready")
        a_ready, ag_ready, glu_ready = sem("a_ready"), sem("ag_ready"), sem("glu_ready")
        scores_done, max_ready, exp_ready, prob_ready = (
            sem(n) for n in ("scores_done", "max_ready", "exp_ready", "prob_ready"))
        PT_ready, attn_ready = sem("PT_ready"), sem("attn_ready")
        tap_done = sem("tap_done")
        centred, sq_ready, var_ready, ln_rstd, ln_done, cat_ready = (
            sem(n) for n in ("centred", "sq_ready", "var_ready", "ln_rstd", "ln_done", "cat_ready"))
        x_new = [sem(f"x_new{l}") for l in range(2)]
        xhat_stored = [sem(f"xhat_stored{l}") for l in range(2)]
        aff_ready = [sem(f"aff_ready{l}") for l in range(2)]
        mask_ready = [sem(f"mask_ready{l}") for l in range(2)]
        table_in = [sem(f"table_in{l}") for l in range(2)]
        route_ready = [sem(f"route_ready{l}") for l in range(2)]
        idx_ready = [sem(f"idx_ready{l}") for l in range(2)]
        hg_in = [sem(f"hg_in{l}") for l in range(2)]
        hg_turned = [sem(f"hg_turned{l}") for l in range(2)]
        hgT_dve = [sem(f"hgT_dve{l}") for l in range(2)]
        hgT_act = [sem(f"hgT_act{l}") for l in range(2)]
        gate_done = [sem(f"gate_done{l}") for l in range(2)]
        up_done = [sem(f"up_done{l}") for l in range(2)]
        silu_ready = [sem(f"silu_ready{l}") for l in range(2)]
        act_ready = [sem(f"act_ready{l}") for l in range(2)]
        act_turned = [sem(f"act_turned{l}") for l in range(2)]
        actT_ready = [sem(f"actT_ready{l}") for l in range(2)]
        down_done = [sem(f"down_done{l}") for l in range(2)]
        y_read = [sem(f"y_read{l}") for l in range(2)]
        y_free = [sem(f"y_free{l}") for l in range(2)]
        ticked = [sem(f"ticked{l}") for l in range(2)]
        yin = [[sem(f"yin{l}_{i}") for i in range(2)] for l in range(2)]
        y_added = [sem(f"y_added{l}") for l in range(2)]
        gc_ready, u_ready, mT_ready = sem("gc_ready"), sem("u_ready"), sem("mT_ready")
        out_done = sem("out_done")

        unit_slot, unit_count, unit_order, loads = {}, {}, [], [0] * RING
        prev_owner = [None] * RING
        unit_prev = {}

        def place(name, slot):
            loads[slot] += 1
            unit_slot[name], unit_count[name] = slot, loads[slot] * 16
            unit_prev[name] = prev_owner[slot]
            prev_owner[slot] = name
            unit_order.append(name)

        even_units = plan_units()
        for n, name in enumerate(even_units):
            place(name, n % RING)
        moe_base = []
        moe_base.append(list(loads))
        for e in range(NE):
            for k, w in enumerate(("wg", "wu", "wd")):
                place((w, 0, e), (3 * e + k) % RING)
        odd_units = plan_units_odd()
        for n, name in enumerate(odd_units):
            place(name, n % RING)
        moe_base.append(list(loads))
        for e in range(NE):
            for k, w in enumerate(("wg", "wu", "wd")):
                place((w, 1, e), (3 * e + k) % RING)
        unit_last = {("kv",): ("kvx", TT - 1), ("a",): ("a", 3), ("ag",): ("ag", 3), ("q",): ("q", TT - 1)}
        for name in even_units + odd_units:
            if name[0] == "mod":
                unit_last[name] = name
            elif name[0] in ("wo", "ow"):
                unit_last[name] = ("out", 0 if name[0] == "wo" else 1, name[1], TT - 1)
            elif len(name) == 2:
                unit_last[name] = (name[0], 4 * name[1] + 3)

        wmod_v = [w_mod[l].rearrange("(p k) n -> p k n", k=KD) for l in range(2)]
        win_v = ev_w_in[0].rearrange("(k p) n -> p k n", p=P)
        wout_v = ev_w_out[0].rearrange("(k p) n -> p k n", p=P)
        oin_v = od_w_in[0].rearrange("(k p) n -> p k n", p=P)
        oout_v = od_w_out[0].rearrange("(k p) n -> p k n", p=P)
        kv_at = HEADS * HD
        a_at = kv_at + 2 * KVH * HD
        wg_v = moe_w_gate.rearrange("l e (k p) n -> (l e) p k n", p=P)
        wu_v = moe_w_up.rearrange("l e (k p) n -> (l e) p k n", p=P)
        wd_v = moe_w_down.rearrange("l e (k p) n -> (l e) p k n", p=P)

        def unit_source(name):
            w = name[0]
            if w == "mod":
                return wmod_v[name[1]][:, :, name[2] * 512:(name[2] + 1) * 512]
            if w == "kv":
                return win_v[:, :, kv_at:a_at]
            if w == "a":
                return win_v[:, :, a_at:a_at + 512]
            if w == "ag":
                return win_v[:, :, a_at + 512:a_at + 1024]
            if w == "q":
                return win_v[:, :, 0:512]
            if w == "wo":
                return wout_v[:, :, name[1] * 512:(name[1] + 1) * 512]
            if w == "ow":
                return oout_v[:, :, name[1] * 512:(name[1] + 1) * 512]
            at = {"gb": 0, "gc": D, "v": 2 * D}[w] + name[1] * 512
            return oin_v[:, :, at:at + 512]

        def unit(name):
            return ring[:, unit_slot[name]]

        def expert_view(slot, w):
            u = ring[:, slot]
            return u.rearrange("p k n -> p (k n)").rearrange("p (k n) -> p k n", n=D) if w == "wd" else u

        def bank(name):
            return psum[GROUP_AT[name] % NBANK]

        block = stack.enter_context(nc.Block())

        @block.sync
        def _(sp):
            def load_dense(name):
                prev = unit_prev[name]
                if prev in unit_last:
                    sp.wait_ge(acc_done, GROUP_AT[unit_last[prev]] + 1)
                src = unit_source(name)
                dst = unit(name)
                if name[0] == "kv":
                    dst = dst[:, :, 0:256]
                sp.dma_start(dst, src).then_inc(unit_in[unit_slot[name]], 16)

            def load_expert(l, e, par):
                for k, v in enumerate((wg_v, wu_v, wd_v)):
                    slot = 3 * par + k
                    src = v[bass.ds(e + l * NE, 1)].rearrange("o p k n -> (o p) k n")
                    sp.dma_start(expert_view(slot, "wd" if k == 2 else "wg"), src).then_inc(unit_in[slot], 16)

            def load_experts(l, units_before):
                for par in range(2):
                    for k, w in enumerate(("wg", "wu", "wd")):
                        prev = unit_prev[(w, l, par)]
                        sp.wait_ge(acc_done, GROUP_AT[unit_last[prev]] + 1)
                    load_expert(l, par, par)
                sp.wait_ge(route_ready[l], 1)
                with sp.Fori(1, NE // 2) as i:
                    for par in range(2):
                        end = sp.value_load(block_start[0:1, bass.ds(i * 2 + (par - 1), 1)], min_val=1, max_val=MAXB)
                        sp.wait_ge(down_done[l], end)
                        load_expert(l, i * 2 + par, par)
                total = sp.value_load(block_start[0:1, NE:NE + 1], min_val=NE, max_val=MAXB)
                sp.wait_ge(down_done[l], total)

            for name in even_units:
                load_dense(name)
            load_experts(0, len(even_units))
            for name in odd_units:
                load_dense(name)
            load_experts(1, len(odd_units))
            for t in range(TT):
                sp.wait_ge(y_added[1], t + 1)
                sp.dma_start(out[0, t * P:(t + 1) * P, :], xs[:, t, :]).then_inc(out_done, 16)
            sp.wait_ge(out_done, 16 * TT)

        @block.scalar
        def _(act):
            steps = [0]

            def link(ins):
                steps[0] += 1
                ins.then_inc(act_step, 1)
                act.wait_ge(act_step, steps[0])

            def acc_wait(name):
                act.wait_ge(acc_done, GROUP_AT[name] + 1)

            act.dma_start(cst[:, :], consts).then_inc(consts_in, 16)
            act.dma_start(craw[:, 0, :], c.rearrange("o (p k) -> (o p) k", k=KD)).then_inc(c_in, 16)
            act.dma_start(craw[:, 1, :], c_ctx.rearrange("(p k) -> p k", k=KD)).then_inc(c_in, 16)
            act.wait_ge(zeroed, 1)
            act.dma_start(b_rows[0:24, :], b_mod.rearrange("l (c n) -> (l c) n", n=512)).then_inc(bmod_in, 16)
            act.dma_start(staging[0:16, 0:P], norm_mix_g.rearrange("l (j p) -> (l j) p", p=P)).then_inc(rows_in, 16)
            act.dma_start(staging[16:32, 0:P], norm_ffn_g.rearrange("l (j p) -> (l j) p", p=P)).then_inc(rows_in, 16)
            for k, v in enumerate((ev_dw_b, ev_ln_g, ev_ln_b)):
                act.dma_start(staging[32 + 4 * k:36 + 4 * k, 0:P], v.rearrange("o (j p) -> (o j) p", p=P)).then_inc(rows_in, 16)
            act.dma_start(ctx_x, ctx[0].rearrange("(t p) d -> p t d", p=P)).then_inc(ctx_in, 16)
            act.dma_start(xs[:, :, :], x[0].rearrange("(t p) d -> p t d", p=P)).then_inc(x_in, 16)
            act.dma_start(hT_cat[0:CONV_K, 0, :], ev_dw_w[0]).then_inc(rows_in, 16)
            act.dma_start(hT_cat[CONV_K:CONV_K + SC_K, 0:2, :], od_conv_w[0].rearrange("k (a n) -> k a n", a=2)).then_inc(rows_in, 16)
            act.dma_start(qkg[:, 0, :], ev_q_norm_g.to_broadcast([P, HD])).then_inc(qkg_in, 16)
            act.dma_start(qkg[:, 1, :], ev_k_norm_g.to_broadcast([P, HD])).then_inc(qkg_in, 16)
            act.dma_start(route_w[:, :, :], router_w.rearrange("(k p) n -> p k n", p=P)).then_inc(router_in, 16)
            act.dma_start(bias_r[:, :], router_bias.rearrange("(o n) -> o n", o=1).to_broadcast([P, NE])).then_inc(router_in, 16)

            act.wait_ge(c_in, 32)
            for s in range(2):
                act.activation(cact[:, :, s], craw[:, s, :], ACT.Silu).then_inc(cact_ready, 1)

            mods = [0]

            def modrow_copy(l, c):
                acc_wait(("mod", l, c))
                if mods[0]:
                    act.wait_ge(acc_done, last_fin[0] + 1)
                act.activation(modrow[:, :], bank(("mod", l, c))[:, :], ACT.Copy).then_inc(modrow_ready, 1)
                mods[0] += 1
                bank_read[("mod", l, c)] = (modrow_ready, mods[0])
                last_fin[0] = GROUP_AT[("fin", l, c)]

            last_fin = [0]

            squared = []

            def squares(norm, src, tiles, wait):
                first = TT if norm == "ctx" else 0
                for t in range(tiles):
                    wait(t)
                    if squared:
                        act.wait_ge(*squared[-1])
                    act.activation(junk, src[:, t, :], ACT.Square,
                                   accum_out=stats[:, 0, first + t:first + t + 1]).then_inc(ssq_ready[norm], 1)
                    squared.append((ssq_ready[norm], t + 1))

            squares("ctx", ctx_x, CT, lambda t: act.wait_ge(ctx_in, 16))

            def modulate(norm, dst, n, scale, shift, chunks):
                act.wait_ge(modcol_ready[MOD_OF[norm]], 1)
                for j in chunks:
                    g = ("norm", norm, j)
                    acc_wait(g)
                    act.activation(dst[:, j, :], bank(g)[:, 0:n], ACT.Identity, bias=shift(j),
                                   scale=scale(j)).then_inc(hT_even[norm], 1)
                    bank_read[g] = (hT_even[norm], j // 2 + 1)

            def shift_of(l, which, s):
                return lambda j: modcol[:, l, 2 * which + j // 4, j % 4, s:s + 1]

            for c_ in range(4):
                modrow_copy(0, c_)
                if c_ == 1:
                    squares("mix0", xs, TT, lambda t: act.wait_ge(x_in, 16))
            modulate("ctx", hzT, CTX, lambda j: mod_a[:, 4, j:j + 1], shift_of(0, 0, 1), range(0, KD, 2))
            modulate("mix0", hT_cat, SEQ, lambda j: mod_a[:, 0, j:j + 1], shift_of(0, 0, 0), range(0, KD, 2))

            for t in range(KT):
                tile = ("kvz", t) if t < CT else ("kvx", t - CT)
                at = TT + t if t < CT else t - CT
                acc_wait(tile)
                act.activation(ktok[:, at, :], bank(tile)[:, 0:P], ACT.Copy).then_inc(kv_ready, 1)
                act.activation(vtok[:, at, :], bank(tile)[:, P:2 * P], ACT.Copy).then_inc(kv_ready, 1)
                bank_read[tile] = (kv_ready, 2 * t + 2)
            for i in range(4):
                acc_wait(("a", i))
                act.activation(apad[:, i, PAD:PAD + SEQ], bank(("a", i))[:, :], ACT.Copy).then_inc(a_ready, 1)
                bank_read[("a", i)] = (a_ready, i + 1)
                modrow_copy(*WITH_A[i])
            for i in range(4):
                acc_wait(("ag", i))
                if i >= 2:
                    act.wait_ge(glu_ready, i - 1)
                act.activation(qT[:, i % 2, :], bank(("ag", i))[:, :], ACT.Sigmoid).then_inc(ag_ready, 1)
                bank_read[("ag", i)] = (ag_ready, i + 1)
                modrow_copy(*WITH_AG[i])
            for v in range(KVH):
                for h in range(2):
                    g = ("kT", v, h)
                    acc_wait(g)
                    act.activation(kT2[:, v, h * 384:(h + 1) * 384], bank(g)[:, 0:384], ACT.Copy).then_inc(kT_ready, 1)
                    bank_read[g] = (kT_ready, 2 * v + h + 1)
            for t in range(TT):
                acc_wait(("q", t))
                act.activation(qtok[:, t, :], bank(("q", t))[:, :], ACT.Copy).then_inc(q_ready, 1)
                bank_read[("q", t)] = (q_ready, t + 1)
                modrow_copy(*WITH_Q[t])
            for i in range(PAIRS):
                acc_wait(("qT", i))
                act.activation(qT[:, i, :], bank(("qT", i))[:, :], ACT.Copy).then_inc(qT_ready, 1)
                bank_read[("qT", i)] = (qT_ready, i + 1)


            def exps(n):
                act.wait_ge(max_ready, n + 1)
                if n >= 2:
                    acc_wait(("PT", (n - 2) // 4, (n - 2) % 4, 1))
                act.activation(prob[:, n % 2, :], score_ps[n % 2][:, 0:KT * P], ACT.Exp, bias=softm[:, 0, n % 2:n % 2 + 1],
                               scale=HD ** -0.5, accum_out=softm[:, 1, n % 2:n % 2 + 1]).then_inc(exp_ready, 1)

            exps(0)
            for s in range(8):
                for u in range(4):
                    n = 4 * s + u
                    if n + 1 < 32:
                        exps(n + 1)
                    hh, qt = u // 2, u % 2
                    for g3 in range(2):
                        g = ("PT", s, u, g3)
                        acc_wait(g)
                        if s >= 2:
                            acc_wait(("pv", s - 2))
                        act.activation(PT[s % 2][hh][:, 3 * g3:3 * g3 + 3, qt * P:(qt + 1) * P],
                                       bank(g)[:, 0:384].rearrange("p (k q) -> p k q", k=3),
                                       ACT.Copy).then_inc(PT_ready, 1)
                        bank_read[g] = (PT_ready, 2 * n + g3 + 1)
                acc_wait(("pv", s))
                act.activation(hT_cat[:, s // 2, (s % 2) * 256:(s % 2 + 1) * 256], bank(("pv", s))[:, 0:256],
                               ACT.Copy).then_inc(attn_ready, 1)
                bank_read[("pv", s)] = (attn_ready, s + 1)

            for m in GATES[0]:
                modrow_copy(*m)
            for i in range(4):
                act.wait_ge(ln_done, i + 1)
                act.activation(hT_cat[:, 4 + i, :], conv_y[:, i, :], ACT.Silu, bias=params[:, 40 + i:41 + i],
                               scale=params[:, 36 + i:37 + i]).then_inc(cat_ready, 1)

            def ffn(l):
                norm = f"ffn{l}"
                squares(norm, xs, TT, lambda t: act.wait_ge(x_new[l], TT + t + 1))
                for t in range(TT):
                    act.wait_ge(xhat_ready[norm], t + 1)
                    act.dma_start(xhat_d[t * 2 * P:(t + 1) * 2 * P, :].rearrange("(p h) n -> p (h n)", h=2),
                                  xhat[:, t, :]).then_inc(xhat_stored[l], 16)
                modulate(norm, hT_cat, SEQ, lambda j: mod_a[:, 1 + 2 * l, j:j + 1], shift_of(l, 3, 0), range(0, KD, 2))
                acc_wait(("route", l, 0))
                act.activation(aff.rearrange("p a b -> p (a b)"), bank(("route", l, 0))[:, 0:TT * NE],
                               ACT.Sigmoid).then_inc(aff_ready[l], 1)
                bank_read[("route", l, 0)] = (aff_ready[l], 1)

                def turn_in():
                    for j in (2, 3, 6, 7):
                        at = (j % 4 - 2) * P + (j // 4) * BLK
                        act.activation(hgT[:, j, :], hg_act_ps[:, at:at + BLK], ACT.Identity,
                                       bias=shift_of(l, 3, 0)(j), scale=mod_a[:, 1 + 2 * l, j:j + 1]).then_inc(hgT_act[l], 1)

                act.wait_ge(route_ready[l], 1)
                total = act.value_load(block_start[0:1, NE:NE + 1], min_val=NE, max_val=MAXB)
                act.wait_ge(hg_turned[l], 1)
                turn_in()
                with act.Fori(0, total) as b:
                    act.wait_ge(gate_done[l], b + 1)
                    act.activation(silu_g, gate_ps[:, 0:256], ACT.Silu).then_inc(silu_ready[l], 1)
                    act.wait_ge(hg_turned[l], b + 2)
                    act.wait_ge(up_done[l], b + 1)
                    turn_in()
                act.wait_ge(y_free[l], total * 16 + 16)
                for t in range(TT):
                    if t >= 2:
                        act.wait_ge(y_added[l], t - 1)
                    for k in range(2):
                        rows = y_d[l][(k * SEQ + t * P) * 2:(k * SEQ + (t + 1) * P) * 2, :].rearrange("(p h) n -> p (h n)", h=2)
                        act.dma_start(y_in[t % 2][:, k, :], rows).then_inc(yin[l][t % 2], 16)

            ffn(0)

            squares("mix1", xs, TT, lambda t: act.wait_ge(y_added[0], TT))
            modulate("mix1", hT_cat, SEQ, lambda j: mod_a[:, 2, j:j + 1], shift_of(1, 0, 0), range(0, KD, 2))
            for h in range(2):
                for i in range(4):
                    m = 4 * h + i
                    acc_wait(("gc", m))
                    if m >= 2:
                        act.wait_ge(u_ready, m - 1)
                    act.activation(gc_sb[m % 2], bank(("gc", m))[:, :], ACT.Copy).then_inc(gc_ready, 1)
                    bank_read[("gc", m)] = (gc_ready, m + 1)
                for m_ in GATES[1][2 * h:2 * h + 2]:
                    modrow_copy(*m_)
            ffn(1)

        @block.vector
        def _(dve):
            steps = [0]

            def link(ins):
                steps[0] += 1
                ins.then_inc(dve_step, 1)
                dve.wait_ge(dve_step, steps[0])

            def acc_wait(name):
                dve.wait_ge(acc_done, GROUP_AT[name] + 1)

            V = nc.vector
            V.memset(b_rows[:, :], 0.0)
            V.memset(staging[:, 0:P], 0.0)
            V.memset(cact[:, :, :].rearrange("p k m -> p (k m)"), 0.0)
            V.memset(apad[:, :, 0:PAD], 0.0)
            V.memset(apad[:, :, PAD + SEQ:APAD], 0.0)
            for l in range(2):
                V.memset(small[:, l:l + 1], 0.0).then_inc(y_read[l], 1)
                V.memset(small[:, 2 + l:3 + l], 0.0).then_inc(ticked[l], 1)
            V.memset(hT_cat[0:34, 1, :], 0.0).then_inc(zeroed, 1)

            acc_wait(("params",))
            link(V.tensor_copy(params[:, :], bank(("params",))[:, 0:44]))
            bank_read[("params",)] = (dve_step, steps[0])
            acc_wait(("taps",))
            link(V.tensor_copy(taps[:, :, :], bank(("taps",))[:, 0:KD * 34].rearrange("p (j k) -> p j k", j=KD)))
            bank_read[("taps",)] = (dve_step, steps[0])

            gates = [0]

            def fin(l, c):
                g = ("fin", l, c)
                acc_wait(g)
                if c in (4, 5, 10, 11):
                    gates[0] += 1
                    bank_read[g] = (gates_ready, gates[0])
                if c in (4, 5):
                    V.tensor_copy(gate_mix[:, (c - 4) * 512:(c - 3) * 512], bank(g)[:, :]).then_inc(gates_ready, 1)
                elif c in (10, 11):
                    h = c - 10
                    V.tensor_copy(gate_ffn[h * 64:(h + 1) * 64, :], bank(g)[h * 64:(h + 1) * 64, :]).then_inc(gates_ready, 1)
                else:
                    link(V.tensor_copy(modcol[:, l, c, :, :], bank(g)[:, 0:8].rearrange("p (j s) -> p j s", s=2)))
                    bank_read[g] = (dve_step, steps[0])
                if c in (3, 9):
                    first = c - 1
                    gcol = (0 if c == 3 else 16) + 8 * l
                    at = 2 * l + (0 if c == 3 else 1)
                    for s in range(1 if (l, c) == (0, 3) else 0, -1, -1):
                        ins = V.scalar_tensor_tensor(out=mod_a[:, 4 if s else at, :].rearrange("p (h j) -> p h j", h=2),
                                                     in0=modcol[:, l, first:first + 2, :, s], scalar=1.0,
                                                     in1=params[:, gcol:gcol + 8].rearrange("p (h j) -> p h j", h=2),
                                                     op0=ALU.add, op1=ALU.mult)
                    ins.then_inc(modcol_ready[at], 1)

            def normalise(norm, src, tiles):
                dst = xhat if norm != "ctx" else ctx_hat
                dve.wait_ge(rstd_ready[norm], 1)
                for t in range(tiles):
                    V.tensor_scalar(dst[:, t, :], src[:, t, :], stats[:, 1 if norm != "ctx" else 2, t:t + 1], None,
                                    ALU.mult).then_inc(xhat_ready[norm], 1)

            def modulate(norm, dst, n, scale, shift):
                dve.wait_ge(modcol_ready[MOD_OF[norm]], 1)
                for j in range(1, KD, 2):
                    g = ("norm", norm, j)
                    acc_wait(g)
                    V.tensor_scalar(dst[:, j, :], bank(g)[:, 0:n], scale(j), shift(j), ALU.mult,
                                    ALU.add).then_inc(hT_odd[norm], 1)
                    bank_read[g] = (hT_odd[norm], j // 2 + 1)

            def shift_of(l, which, s):
                return lambda j: modcol[:, l, 2 * which + j // 4, j % 4, s:s + 1]

            normalise("ctx", ctx_x, CT)
            for c_ in range(3):
                fin(0, c_)
            normalise("mix0", xs, TT)
            fin(0, 3)
            modulate("ctx", hzT, CTX, lambda j: mod_a[:, 4, j:j + 1], shift_of(0, 0, 1))
            modulate("mix0", hT_cat, SEQ, lambda j: mod_a[:, 0, j:j + 1], shift_of(0, 0, 0))

            def head_norm(v, tmp, n, nh, g, stat, ssq, rstd, count):
                link(V.tensor_tensor(tmp, v, v, ALU.mult))
                V.tensor_reduce(head_stats[:, stat, 0:n * nh], tmp.rearrange("p (m d) -> p m d", d=HD), AX_X,
                                ALU.add).then_inc(ssq, 1)
                dve.wait_ge(rstd, count)
                v3 = v.rearrange("p (m d) -> p m d", d=HD)
                link(V.tensor_tensor(v3, v3, head_stats[:, stat, 0:n * nh].unsqueeze(2).to_broadcast([P, n * nh, HD]), ALU.mult))
                link(V.tensor_tensor(v3, v3, qkg[:, g, :].unsqueeze(1).to_broadcast([P, n * nh, HD]), ALU.mult))

            def rope(v, tmp, tile, nh, done):
                x12 = v.rearrange("p (h i two) -> p two h i", h=nh, two=2)
                half = nh * HD // 2
                t1 = tmp[:, 0:half].rearrange("p (h i) -> p h i", h=nh)
                t2 = tmp[:, half:2 * half].rearrange("p (h i) -> p h i", h=nh)
                cs = const("cos")[:, tile * 32:(tile + 1) * 32].unsqueeze(1).to_broadcast([P, nh, 32])
                sn = const("sin")[:, tile * 32:(tile + 1) * 32].unsqueeze(1).to_broadcast([P, nh, 32])
                x1, x2 = x12[:, 0], x12[:, 1]
                V.tensor_tensor(t1, x1, sn, ALU.mult)
                link(V.tensor_tensor(t2, x2, sn, ALU.mult))
                V.tensor_tensor(x1, x1, cs, ALU.mult)
                link(V.tensor_tensor(x2, x2, cs, ALU.mult))
                link(V.tensor_tensor(x2, x2, t1, ALU.add))
                V.tensor_tensor(x1, x1, t2, ALU.subtract).then_inc(done, 1)

            dve.wait_ge(kv_ready, 2 * KT)
            dve.wait_ge(qkg_in, 32)
            head_norm(ktok.rearrange("p t d -> p (t d)"), qtmp, KT, KVH, 1, 0, k_ssq, k_rstd, 1)
            for t in range(TT):
                rope(ktok[:, t, :], qtmp[:, t * P:(t + 1) * P], t, KVH, k_roped)

            for m in WITH_A:
                fin(*m)
            for i in range(4):
                dve.wait_ge(ag_ready, i + 1)
                a_in = apad[:, i, PAD:PAD + SEQ]
                V.tensor_tensor(a_in, a_in, qT[:, i % 2, :], ALU.mult).then_inc(glu_ready, 1)
                fin(*WITH_AG[i])

            tap_list = [(k, i) for k in range(CONV_K) for i in range(4)]
            tap_at = [0]

            def conv(n):
                for k, i in tap_list[tap_at[0]:tap_at[0] + n]:
                    src = apad[:, i, k:k + SEQ]
                    w = taps[:, i, k:k + 1]
                    if k == 0:
                        dve.wait_ge(glu_ready, 4)
                        ins = V.tensor_scalar(conv_y[:, i, :], src, w, params[:, 32 + i:33 + i], ALU.mult, ALU.add)
                    else:
                        dve.wait_ge(tap_done, 4 * (k - 1) + i + 1)
                        ins = V.scalar_tensor_tensor(out=conv_y[:, i, :], in0=src, scalar=w, in1=conv_y[:, i, :],
                                                     op0=ALU.mult, op1=ALU.add)
                    ins.then_inc(tap_done, 1)
                tap_at[0] += n

            conv(12)
            for t in range(TT):
                dve.wait_ge(q_ready, t + 1)
                head_norm(qtok[:, t, :], qtmp[:, 0:512], 1, HEADS, 0, 1, q_ssq, q_rstd, t + 1)
                rope(qtok[:, t, :], qtmp[:, 0:512], t, HEADS, q_roped)
                fin(*WITH_Q[t])
                conv(6)

            def row_max(n):
                dve.wait_ge(scores_done, n + 1)
                link(V.tensor_reduce(softm[:, 2, n % 2:n % 2 + 1], score_ps[n % 2][:, 0:KT * P], AX_X, ALU.max))
                V.tensor_scalar(softm[:, 0, n % 2:n % 2 + 1], softm[:, 2, n % 2:n % 2 + 1], -HD ** -0.5, None,
                                ALU.mult).then_inc(max_ready, 1)

            row_max(0)
            for s in range(8):
                for u in range(4):
                    n = 4 * s + u
                    if n + 1 < 32:
                        row_max(n + 1)
                    dve.wait_ge(exp_ready, n + 1)
                    link(V.reciprocal(softm[:, 3, n % 2:n % 2 + 1], softm[:, 1, n % 2:n % 2 + 1]))
                    V.tensor_scalar(prob[:, n % 2, :], prob[:, n % 2, :], softm[:, 3, n % 2:n % 2 + 1], None,
                                    ALU.mult).then_inc(prob_ready, 1)
                    conv(3)
            conv(len(tap_list) - tap_at[0])

            dve.wait_ge(tap_done, len(tap_list))
            acc_wait(("mu",))
            for i in range(4):
                V.scalar_tensor_tensor(out=conv_y[:, i, :], in0=bank(("mu",))[:, :], scalar=-1.0 / CONV_C,
                                       in1=conv_y[:, i, :], op0=ALU.mult, op1=ALU.add).then_inc(centred, 1)
            bank_read[("mu",)] = (centred, 4)
            for i in range(4):
                dve.wait_ge(centred, i + 1)
                V.tensor_tensor(apad[:, i, 0:SEQ], conv_y[:, i, :], conv_y[:, i, :], ALU.mult).then_inc(sq_ready, 1)
            acc_wait(("var",))
            V.tensor_scalar(gc_sb[0], bank(("var",))[:, :], 1.0 / CONV_C, EPS, ALU.mult, ALU.add).then_inc(var_ready, 1)
            bank_read[("var",)] = (var_ready, 1)
            dve.wait_ge(ln_rstd, 1)
            for i in range(4):
                V.tensor_tensor(conv_y[:, i, :], conv_y[:, i, :], gc_sb[1], ALU.mult).then_inc(ln_done, 1)

            def mixer_out(l):
                for h in range(2):
                    for t in range(TT):
                        g = ("out", l, h, t)
                        tmp = prob[:, 0, 0:512] if t % 2 else prob[:, 1, 0:512]
                        acc_wait(g)
                        link(V.tensor_tensor(tmp, bank(g)[:, :], gate_mix[:, h * 512:(h + 1) * 512], ALU.mult))
                        bank_read[g] = (dve_step, steps[0])
                        xh = xs[:, t, h * 512:(h + 1) * 512]
                        V.tensor_tensor(xh, xh, tmp, ALU.add).then_inc(x_new[l], 1)

            def route(l):
                key = const("expert_key").unsqueeze(1).to_broadcast([P, TT, NE])
                gkey = const("group_key").unsqueeze(1).to_broadcast([P, TT, NG])

                def b16(v):
                    return v.to_broadcast([P, TT, NE])

                dve.wait_ge(aff_ready[l], 1)
                link(V.tensor_tensor(sel, aff, bias_r[:, :].unsqueeze(1).to_broadcast([P, TT, NE]), ALU.add))
                s4 = sel.rearrange("p t (g k) -> p t g k", g=NG)
                e = [s4[:, :, :, k] for k in range(EPG)]
                V.tensor_tensor(g_a, e[0], e[1], ALU.max)
                V.tensor_tensor(g_b, e[0], e[1], ALU.min)
                V.tensor_tensor(g_c, e[2], e[3], ALU.max)
                link(V.tensor_tensor(g_d, e[2], e[3], ALU.min))
                link(V.tensor_tensor(g_b, g_b, g_d, ALU.max))
                link(V.tensor_tensor(g_d, g_a, g_c, ALU.min))
                link(V.tensor_tensor(g_b, g_b, g_d, ALU.max))
                link(V.tensor_tensor(g_a, g_a, g_c, ALU.max))
                link(V.tensor_tensor(g_a, g_a, g_b, ALU.add))
                link(V.tensor_reduce(r4, g_a, AX_X, ALU.max))
                link(V.tensor_tensor(g_b, g_a, r4.to_broadcast([P, TT, NG]), ALU.is_equal))
                link(V.tensor_tensor(g_b, g_b, gkey, ALU.mult))
                link(V.tensor_reduce(r4, g_b, AX_X, ALU.max))
                link(V.tensor_tensor(g_b, g_b, r4.to_broadcast([P, TT, NG]), ALU.is_equal))
                link(V.tensor_scalar(g_c, g_b, 1e30, -1e30, ALU.mult, ALU.add))
                m4 = selm.rearrange("p t (g k) -> p t g k", g=NG)
                link(V.tensor_tensor(m4, s4, g_b.unsqueeze(3).to_broadcast([P, TT, NG, EPG]), ALU.mult))
                link(V.tensor_tensor(m4, m4, g_c.unsqueeze(3).to_broadcast([P, TT, NG, EPG]), ALU.add))
                for n, oh in enumerate((oh1, oh2)):
                    link(V.tensor_reduce(r4, selm, AX_X, ALU.max))
                    link(V.tensor_tensor(r16, selm, b16(r4), ALU.is_equal))
                    link(V.tensor_tensor(r16, r16, key, ALU.mult))
                    link(V.tensor_reduce(r4, r16, AX_X, ALU.max))
                    link(V.tensor_tensor(oh, r16, b16(r4), ALU.is_equal))
                    if n == 0:
                        link(V.scalar_tensor_tensor(out=selm, in0=oh, scalar=-3e38, in1=selm, op0=ALU.mult, op1=ALU.add))
                V.tensor_tensor(picked, oh1, oh2, ALU.add).then_inc(mask_ready[l], 1)
                for n, oh in enumerate((oh1, oh2)):
                    link(V.tensor_tensor(r16, oh, aff, ALU.mult))
                    link(V.tensor_reduce(w2[:, :, n:n + 1], r16, AX_X, ALU.add))
                link(V.tensor_tensor(w_sum, w2[:, :, 0:1], w2[:, :, 1:2], ALU.add))
                link(V.reciprocal(w_sum, w_sum))
                link(V.tensor_tensor(w2, w2, w_sum.to_broadcast([P, TT, 2]), ALU.mult))
                g = ("route", l, 1)
                acc_wait(g)
                V.tensor_copy(before16, bank(g)[:, 0:TT * NE].rearrange("p (t e) -> p t e", e=NE))
                link(V.tensor_copy(total16, bank(g)[:, TT * NE:2 * TT * NE].rearrange("p (t e) -> p t e", e=NE)))
                bank_read[g] = (dve_step, steps[0])
                for t in range(1, TT):
                    link(V.tensor_tensor(before16[:, t, :], before16[:, t, :], total16[:, t - 1, :], ALU.add))
                    link(V.tensor_tensor(total16[:, t, :], total16[:, t, :], total16[:, t - 1, :], ALU.add))
                fb = const("full_blocks")
                link(V.tensor_tensor(cmp16, total16[:, TT - 1, :].unsqueeze(2).to_broadcast([P, NE, SEQ // BLK - 1]),
                                     fb.unsqueeze(1).to_broadcast([P, NE, SEQ // BLK - 1]), ALU.is_gt))
                link(V.tensor_reduce(nblk16, cmp16, AX_X, ALU.add))
                link(V.tensor_scalar(nblk16, nblk16, 1.0, None, ALU.add))
                link(V.tensor_tensor(start_cmp, nblk16.unsqueeze(1).to_broadcast([P, NE + 1, NE]),
                                     const("expert_before").rearrange("p (a b) -> p a b", b=NE), ALU.mult))
                link(V.tensor_reduce(start_f, start_cmp, AX_X, ALU.add))
                link(V.tensor_copy(block_start[:, :], start_f))
                for n, oh in enumerate((oh1, oh2)):
                    link(V.tensor_tensor(r16, oh, before16, ALU.mult))
                    link(V.tensor_reduce(pos2[:, :, n:n + 1], r16, AX_X, ALU.add))
                    link(V.tensor_tensor(r16, oh, start_f[:, 0:NE].unsqueeze(1).to_broadcast([P, TT, NE]), ALU.mult))
                    link(V.tensor_reduce(st2[:, :, n:n + 1], r16, AX_X, ALU.add))
                flat = lambda v: v.rearrange("p a b -> p (a b)")
                link(V.tensor_tensor(cmp2, flat(pos2).unsqueeze(2).to_broadcast([P, 2 * TT, SEQ // BLK - 1]),
                                     fb.unsqueeze(1).to_broadcast([P, 2 * TT, SEQ // BLK - 1]), ALU.is_ge))
                link(V.tensor_reduce(flat(full2), cmp2, AX_X, ALU.add))
                link(V.tensor_tensor(blk2, st2, full2, ALU.add))
                link(V.scalar_tensor_tensor(out=slot2, in0=full2, scalar=-float(BLK), in1=pos2, op0=ALU.mult, op1=ALU.add))
                V.tensor_tensor(oh_slot, flat(slot2).unsqueeze(2).to_broadcast([P, 2 * TT, P]),
                                const("slot_of_col").unsqueeze(1).to_broadcast([P, 2 * TT, P]), ALU.is_equal)
                link(V.tensor_tensor(oh_blk, flat(blk2).unsqueeze(2).to_broadcast([P, 2 * TT, NB]),
                                     const("block_id").unsqueeze(1).to_broadcast([P, 2 * TT, NB]), ALU.is_equal))
                for n, v in enumerate((const("token"), const("out_row"), flat(w2))):
                    V.tensor_tensor(val_blk[:, :, n, :], oh_blk, v.unsqueeze(2).to_broadcast([P, 2 * TT, NB]),
                                    ALU.mult).then_inc(table_in[l], 1)
                g = ("route", l, 2)
                acc_wait(g)
                tab = bank(g)[:, 0:3 * NB].rearrange("p (v b) -> p v b", v=3)
                V.tensor_scalar(rowid[:, 0, :], tab[:, 0, :], 2.0, const("half"), ALU.mult, ALU.add)
                V.tensor_scalar(rowid[:, 1, :], tab[:, 1, :], float(NIDX), 2.0, ALU.add, ALU.mult)
                link(V.tensor_copy(rowid[:, 2, :], tab[:, 2, :]))
                bank_read[g] = (dve_step, steps[0])
                link(V.tensor_scalar(rowid[:, 1, :], rowid[:, 1, :], const("half"), None, ALU.add))
                link(V.tensor_copy(row_i[:, 0, :], rowid[:, 0, :]))
                V.tensor_copy(row_i[:, 1, :], rowid[:, 1, :]).then_inc(route_ready[l], 1)

            def ffn(l):
                norm = f"ffn{l}"
                normalise(norm, xs, TT)
                modulate(norm, hT_cat, SEQ, lambda j: mod_a[:, 1 + 2 * l, j:j + 1], shift_of(l, 3, 0))
                if l == 0:
                    dve.wait_ge(router_in, 32)
                route(l)

                def turn_in():
                    for j in (0, 1, 4, 5):
                        at = j % 4 * P + (j // 4) * BLK
                        V.tensor_scalar(hgT[:, j, :], hg_dve_ps[:, at:at + BLK], mod_a[:, 1 + 2 * l, j:j + 1],
                                        shift_of(l, 3, 0)(j), ALU.mult, ALU.add).then_inc(hgT_dve[l], 1)

                dve.wait_ge(route_ready[l], 1)
                total = dve.value_load(block_start[0:1, NE:NE + 1], min_val=NE, max_val=MAXB)
                dve.wait_ge(hg_turned[l], 1)
                turn_in()
                with dve.Fori(0, total) as b:
                    dve.wait_ge(silu_ready[l], b + 1)
                    dve.wait_ge(up_done[l], b + 1)
                    V.tensor_tensor(act_sb, silu_g, up_ps[:, 0:256], ALU.mult).then_inc(act_ready[l], 1)
                    dve.wait_ge(act_turned[l], b + 1)
                    V.tensor_copy(actT, at_ps[:, 0:256].rearrange("p (j s) -> p j s", j=2)).then_inc(actT_ready[l], 1)
                    dve.wait_ge(hg_turned[l], b + 2)
                    turn_in()
                    dve.wait_ge(down_done[l], b + 1)
                    dve.wait_ge(y_free[l], b * 16 + 16)
                    V.scalar_tensor_tensor(out=y_blk, in0=y_ps, scalar=rowid[:, 2, bass.ds(b, 1)], in1=gate_ffn[:, :],
                                           op0=ALU.mult, op1=ALU.mult).then_inc(y_read[l], 1)
                for t in range(TT):
                    i = t % 2
                    dve.wait_ge(yin[l][i], 32 * (t // 2 + 1))
                    link(V.tensor_tensor(xs[:, t, :], xs[:, t, :], y_in[i][:, 0, :], ALU.add))
                    V.tensor_tensor(xs[:, t, :], xs[:, t, :], y_in[i][:, 1, :], ALU.add).then_inc(y_added[l], 1)

            for m in GATES[0]:
                fin(*m)
            dve.wait_ge(gates_ready, 4)
            mixer_out(0)
            ffn(0)

            normalise("mix1", xs, TT)
            modulate("mix1", hT_cat, SEQ, lambda j: mod_a[:, 2, j:j + 1], shift_of(1, 0, 0))
            for u in u_pad:
                V.memset(u[:, 0:1], 0.0)
                link(V.memset(u[:, SEQ + 1:SEQ + 2], 0.0))
            for h in range(2):
                for i in range(4):
                    m = 4 * h + i
                    up, y = u_pad[m % 2], sc_y[m % 2]
                    dve.wait_ge(gc_ready, m + 1)
                    acc_wait(("v", m))
                    V.tensor_tensor(up[:, 1:SEQ + 1], gc_sb[m % 2], bank(("v", m))[:, :], ALU.mult).then_inc(u_ready, 1)
                    bank_read[("v", m)] = (u_ready, m + 1)
                    dve.wait_ge(u_ready, m + 1)
                    link(V.tensor_scalar(y, up[:, 0:SEQ], taps[:, m, 31:32], None, ALU.mult))
                    for k in range(1, SC_K):
                        link(V.scalar_tensor_tensor(out=y, in0=up[:, k:k + SEQ], scalar=taps[:, m, 31 + k:32 + k], in1=y,
                                                    op0=ALU.mult, op1=ALU.add))
                    acc_wait(("gb", m))
                    V.tensor_tensor(mT[:, m, :], y, bank(("gb", m))[:, :], ALU.mult).then_inc(mT_ready, 1)
                    bank_read[("gb", m)] = (mT_ready, m + 1)
                for m_ in GATES[1][2 * h:2 * h + 2]:
                    fin(*m_)
            dve.wait_ge(gates_ready, 8)
            mixer_out(1)
            ffn(1)

        @block.gpsimd
        def _(pool):
            G = nc.gpsimd
            pool.wait_ge(zeroed, 1)
            pool.wait_ge(consts_in, 16)
            half = const("minus_half")
            steps = [0]

            def passed(l, n):
                pool.wait_ge(ticked[l], n)
                G.tensor_tensor(tick[:, :], half, half, ALU.add).then_inc(ticked[l], 1)

            def link(ins):
                steps[0] += 1
                ins.then_inc(pool_step, 1)
                pool.wait_ge(pool_step, steps[0])

            def rsqrt(dst, src, n, scale):
                link(G.tensor_scalar(dst, src, scale, EPS, ALU.mult, ALU.add))
                return G.tensor_tensor(dst, dst, half.to_broadcast([P, n]), ALU.pow)

            def norm_rstd(norm, tiles):
                pool.wait_ge(ssq_ready[norm], tiles)
                row, first = (2, TT) if norm == "ctx" else (1, 0)
                rsqrt(stats[:, row, 0:tiles], stats[:, 0, first:first + tiles], tiles, 1.0 / D).then_inc(rstd_ready[norm], 1)

            norm_rstd("ctx", CT)
            norm_rstd("mix0", TT)
            pool.wait_ge(k_ssq, 1)
            rsqrt(head_stats[:, 0, 0:KT * KVH], head_stats[:, 0, 0:KT * KVH], KT * KVH, 1.0 / HD).then_inc(k_rstd, 1)
            for t in range(TT):
                pool.wait_ge(q_ssq, t + 1)
                rsqrt(head_stats[:, 1, 0:HEADS], head_stats[:, 1, 0:HEADS], HEADS, 1.0 / HD).then_inc(q_rstd, 1)
            pool.wait_ge(var_ready, 1)
            G.tensor_tensor(gc_sb[1], gc_sb[0], half.to_broadcast([P, SEQ]), ALU.pow).then_inc(ln_rstd, 1)

            def ffn(l):
                norm_rstd(f"ffn{l}", TT)
                pool.wait_ge(route_ready[l], 1)
                total = pool.value_load(block_start[0:1, NE:NE + 1], min_val=NE, max_val=MAXB)
                pool.wait_ge(xhat_stored[l], 16 * TT)

                def gather(b, count):
                    G.tensor_copy(cur_idx[:, 0, :], row_i[:, 0, bass.ds(b, 1)]).then_inc(idx_ready[l], 1)
                    pool.wait_ge(idx_ready[l], count)
                    passed(l, count)
                    G.indirect_dma_start(out=hg_raw, out_offset=None, in_=xhat_d,
                                         in_offset=bass.IndirectOffsetOnAxis(ap=cur_idx[:, 0, :], axis=0),
                                         bounds_check=2 * SEQ - 1, oob_is_err=False).then_inc(hg_in[l], 16)

                def scatter(b, count, reads):
                    G.tensor_copy(cur_idx[:, 1, :], row_i[:, 1, bass.ds(b, 1)]).then_inc(idx_ready[l], 1)
                    pool.wait_ge(idx_ready[l], count)
                    pool.wait_ge(y_read[l], reads)
                    passed(l, count)
                    G.indirect_dma_start(out=y_d[l], out_offset=bass.IndirectOffsetOnAxis(ap=cur_idx[:, 1, :], axis=0),
                                         in_=y_blk, in_offset=None, bounds_check=4 * SEQ - 1,
                                         oob_is_err=False).then_inc(y_free[l], 16)

                gather(0, 1)
                scatter(NB - 1, 2, 1)
                with pool.Fori(0, total) as b:
                    pool.wait_ge(hg_turned[l], b + 1)
                    gather(b + 1, b * 2 + 3)
                    pool.wait_ge(y_free[l], b * 16 + 16)
                    scatter(b, b * 2 + 4, b + 2)

            ffn(0)
            norm_rstd("mix1", TT)
            ffn(1)

        @block.tensor
        def _(pe):
            T = nc.tensor
            at = [0]

            def open_group(name):
                n = at[0]
                assert GROUPS[n] == name, (GROUPS[n], name)
                at[0] += 1
                if n >= NBANK:
                    pe.wait_ge(*bank_read[GROUPS[n - NBANK]])
                return psum[n % NBANK]

            def unit_wait(name):
                pe.wait_ge(unit_in[unit_slot[name]], unit_count[name])
                return unit(name)

            def close(mm):
                mm.then_inc(acc_done, 1)

            pe.wait_ge(consts_in, 16)
            pe.wait_ge(zeroed, 1)
            pe.wait_ge(rows_in, 16 * 7)
            ps = open_group(("params",))
            close(T.transpose(ps[:, 0:44], staging[0:44, 0:P], ident[0:44, 0:44]))
            ps = open_group(("taps",))
            for j in range(KD):
                mm = T.transpose(ps[:, j * 34:(j + 1) * 34], hT_cat[0:34, j // 4, (j % 4) * P:(j % 4 + 1) * P], ident[0:34, 0:34])
            close(mm)

            mods = [0]

            def mod_rows(l, c):
                ps = open_group(("mod", l, c))
                w = unit_wait(("mod", l, c))
                if not mods[0]:
                    pe.wait_ge(cact_ready, 2)
                    pe.wait_ge(bmod_in, 16)
                for k in range(KD):
                    q = k % 4
                    T.matmul(ps[32 * q:32 * q + 32, :], cact[:, k, :], w[:, k, :], start=(k < 4), stop=(k >= 4 and q != 0))
                mm = T.matmul(ps[0:2, :], const("ident_twice")[:, 2 * (12 * l + c):2 * (12 * l + c) + 2], b_rows[:, :], start=False, stop=True)
                close(mm)

            def mod_fin(l, c):
                mods[0] += 1
                ps = open_group(("fin", l, c))
                pe.wait_ge(modrow_ready, mods[0])
                if c in (4, 5):
                    mm = T.matmul(ps[:, :], const("sel_x"), modrow[:, :], start=True, stop=True)
                elif c in (10, 11):
                    h = c - 10
                    mm = T.matmul(ps[h * 64:(h + 1) * 64, :], const("sel_x")[:, 0:64], modrow[:, :], start=True, stop=True)
                else:
                    for j in range(4):
                        mm = T.matmul(ps[:, 2 * j:2 * j + 2], modrow[:, j * P:(j + 1) * P], const("sel_both"), start=True, stop=True)
                close(mm)

            def norm_turn(norm, src, tiles):
                pe.wait_ge(xhat_ready[norm], tiles)
                for j in range(KD):
                    ps = open_group(("norm", norm, j))
                    for t in range(tiles):
                        mm = T.transpose(ps[:, t * P:(t + 1) * P], src[:, t, j * P:(j + 1) * P], ident)
                    close(mm)

            for c_ in range(4):
                mod_rows(0, c_)
                mod_fin(0, c_)
            norm_turn("ctx", ctx_hat, CT)
            norm_turn("mix0", xhat, TT)
            def hT_wait(norm):
                pe.wait_ge(hT_even[norm], KD // 2)
                pe.wait_ge(hT_odd[norm], KD // 2)


            def tokens_out(name, lhs, t, w, n):
                ps = open_group(name)
                for k in range(KD):
                    mm = T.matmul(ps[:, 0:n], lhs[:, k, t * P:(t + 1) * P], w[:, k, 0:n], start=(k == 0), stop=(k == KD - 1))
                close(mm)

            def channels_out(name, i, w):
                ps = open_group(name)
                for k in range(KD):
                    mm = T.matmul(ps[:, :], w[:, k, i * P:(i + 1) * P], hT_cat[:, k, :], start=(k == 0), stop=(k == KD - 1))
                close(mm)

            w = unit_wait(("kv",))
            hT_wait("ctx")
            for t in range(CT):
                tokens_out(("kvz", t), hzT, t, w, 256)
            hT_wait("mix0")
            for t in range(TT):
                tokens_out(("kvx", t), hT_cat, t, w, 256)
            w = unit_wait(("a",))
            for i in range(4):
                channels_out(("a", i), i, w)
                mod_rows(*WITH_A[i])
                mod_fin(*WITH_A[i])
            w = unit_wait(("ag",))
            for i in range(4):
                channels_out(("ag", i), i, w)
                mod_rows(*WITH_AG[i])
                mod_fin(*WITH_AG[i])
            for v in range(KVH):
                for h in range(2):
                    ps = open_group(("kT", v, h))
                    pe.wait_ge(k_roped, TT)
                    for t in range(3):
                        for half in range(2):
                            mm = T.matmul(ps[half * 64:(half + 1) * 64, t * P:(t + 1) * P], ktok[:, 3 * h + t, v * HD:(v + 1) * HD],
                                          ident, start=True, stop=True)
                    close(mm)
            w = unit_wait(("q",))
            for t in range(TT):
                tokens_out(("q", t), hT_cat, t, w, 512)
                mod_rows(*WITH_Q[t])
                mod_fin(*WITH_Q[t])
            for i in range(PAIRS):
                ps = open_group(("qT", i))
                pe.wait_ge(q_roped, TT)
                for t in range(TT):
                    mm = T.transpose(ps[:, t * P:(t + 1) * P], qtok[:, t, i * P:(i + 1) * P], ident)
                close(mm)

            def scores(n):
                s, u = n // 4, n % 4
                pair, qt = s // 2, (s % 2) * 2 + u % 2
                r = slice((u // 2) * 64, (u // 2) * 64 + 64)
                pe.wait_ge(qT_ready, pair + 1)
                if n >= 2:
                    pe.wait_ge(exp_ready, n - 1)
                for a, b in ((0, 512), (512, KT * P)):
                    mm = T.matmul(score_ps[n % 2][:, a:b], qT[r, pair, qt * P:(qt + 1) * P], kT2[r, pair // 2, a:b],
                                  start=True, stop=True)
                mm.then_inc(scores_done, 1)

            pe.wait_ge(kT_ready, 2 * KVH)
            scores(0)
            for s in range(8):
                for u in range(4):
                    n = 4 * s + u
                    if n + 1 < 32:
                        scores(n + 1)
                    pe.wait_ge(prob_ready, n + 1)
                    for g3 in range(2):
                        ps = open_group(("PT", s, u, g3))
                        for k in range(3):
                            mm = T.transpose(ps[:, k * P:(k + 1) * P], prob[:, n % 2, (3 * g3 + k) * P:(3 * g3 + k + 1) * P], ident)
                        close(mm)
                ps = open_group(("pv", s))
                pe.wait_ge(PT_ready, 8 * s + 8)
                kvh = s // 4
                for k in range(KT):
                    for hh in range(2):
                        mm = T.matmul(ps[hh * 64:(hh + 1) * 64, 0:256], vtok[:, k, kvh * HD:(kvh + 1) * HD], PT[s % 2][hh][:, k, :],
                                      start=(k == 0), stop=(k == KT - 1))
                close(mm)

            for name, src, ready in ((("mu",), conv_y, (tap_done, 4 * CONV_K)), (("var",), apad[:, :, 0:SEQ], (sq_ready, 4))):
                ps = open_group(name)
                pe.wait_ge(*ready)
                for i in range(4):
                    mm = T.matmul(ps[:, :], const("ones"), src[:, i, :], start=(i == 0), stop=(i == 3))
                close(mm)

            for m in GATES[0]:
                mod_rows(*m)
                mod_fin(*m)

            def mixer_out(l, lhs, unit_name):
                for h in range(2):
                    w = unit_wait((unit_name, h))
                    for t in range(TT):
                        ps = open_group(("out", l, h, t))
                        for k in range(KD):
                            mm = T.matmul(ps[:, :], lhs[:, k, t * P:(t + 1) * P], w[:, k, :], start=(k == 0), stop=(k == KD - 1))
                        close(mm)

            def ffn(l):
                norm_turn(f"ffn{l}", xhat, TT)
                ps = open_group(("route", l, 0))
                hT_wait(f"ffn{l}")
                if l == 0:
                    pe.wait_ge(router_in, 32)
                for t in range(TT):
                    for k in range(KD):
                        mm = T.matmul(ps[:, t * NE:(t + 1) * NE], hT_cat[:, k, t * P:(t + 1) * P], route_w[:, k, :],
                                      start=(k == 0), stop=(k == KD - 1))
                close(mm)
                ps = open_group(("route", l, 1))
                pe.wait_ge(mask_ready[l], 1)
                rows = picked.rearrange("p t e -> p (t e)")
                T.matmul(ps[:, 0:TT * NE], const("before"), rows, start=True, stop=True)
                close(T.matmul(ps[:, TT * NE:2 * TT * NE], const("ones"), rows, start=True, stop=True))
                ps = open_group(("route", l, 2))
                pe.wait_ge(table_in[l], 3)
                for n in range(2 * TT):
                    mm = T.matmul(ps[:, 0:3 * NB], oh_slot[:, n, :], val_blk[:, n, :, :].rearrange("p v b -> p (v b)"),
                                  start=(n == 0), stop=(n == 2 * TT - 1))
                close(mm)

                pe.wait_ge(route_ready[l], 1)

                def turn(count):
                    pe.wait_ge(hg_in[l], count * 16)
                    for j in range(4):
                        mm = T.transpose((hg_dve_ps, hg_act_ps)[j // 2][:, j % 2 * P:(j % 2 + 1) * P], hg_raw[:, j * P:(j + 1) * P], ident)
                    mm.then_inc(hg_turned[l], 1)

                turn(1)

                def block_of(b, i, par):
                    def landed(k):
                        slot = 3 * par + k
                        pe.wait_ge(unit_in[slot], i * 16 + (moe_base[l][slot] + 1) * 16)
                        return expert_view(slot, "wd" if k == 2 else "wg")

                    pe.wait_ge(hgT_dve[l], b * 4 + 4)
                    pe.wait_ge(hgT_act[l], b * 4 + 4)
                    for n, ps, done in ((0, gate_ps, gate_done[l]), (1, up_ps, up_done[l])):
                        w = landed(n)
                        for k in range(KD):
                            for h in range(2):
                                mm = T.matmul(ps[h * BLK:(h + 1) * BLK, 0:256], hgT[:, k, :], w[:, k, h * 256:(h + 1) * 256],
                                              start=(k == 0), stop=(k == KD - 1))
                        mm.then_inc(done, 1)
                    turn(b + 2)
                    pe.wait_ge(act_ready[l], b + 1)
                    for j in range(2):
                        mm = T.transpose(at_ps[:, j * P:(j + 1) * P], act_sb[:, j * P:(j + 1) * P], ident)
                    mm.then_inc(act_turned[l], 1)
                    pe.wait_ge(actT_ready[l], b + 1)
                    pe.wait_ge(y_read[l], b + 1)
                    wd = landed(2)
                    for k in range(4):
                        for h in range(2):
                            mm = T.matmul(y_ps[h * BLK:(h + 1) * BLK, :], actT[:, k % 2, (k // 2) * BLK:(k // 2 + 1) * BLK],
                                          wd[:, k, h * 512:(h + 1) * 512], start=(k == 0), stop=(k == 3))
                    mm.then_inc(down_done[l], 1)

                with pe.Fori(0, NE // 2) as i:
                    for par in range(2):
                        first = pe.value_load(block_start[0:1, bass.ds(i * 2 + par, 1)], min_val=0, max_val=MAXB)
                        end = pe.value_load(block_start[0:1, bass.ds(i * 2 + par + 1, 1)], min_val=1, max_val=MAXB)
                        with pe.Fori(first, end) as b:
                            block_of(b, i, par)
                total = pe.value_load(block_start[0:1, NE:NE + 1], min_val=NE, max_val=MAXB)
                pe.wait_ge(y_read[l], total + 1)
                pe.wait_ge(hgT_dve[l], total * 4 + 4)
                pe.wait_ge(hgT_act[l], total * 4 + 4)

            pe.wait_ge(attn_ready, 8)
            pe.wait_ge(cat_ready, 4)
            mixer_out(0, hT_cat, "wo")
            ffn(0)

            norm_turn("mix1", xhat, TT)
            hT_wait("mix1")
            for h in range(2):
                w = {n: unit_wait((n, h)) for n in ("gc", "v", "gb")}
                for i in range(4):
                    for n in ("gc", "v", "gb"):
                        ps = open_group((n, 4 * h + i))
                        for k in range(KD):
                            mm = T.matmul(ps[:, :], w[n][:, k, i * P:(i + 1) * P], hT_cat[:, k, :], start=(k == 0), stop=(k == KD - 1))
                        close(mm)
                for m in GATES[1][2 * h:2 * h + 2]:
                    mod_rows(*m)
                    mod_fin(*m)
            pe.wait_ge(mT_ready, KD)
            mixer_out(1, mT, "ow")
            ffn(1)
            assert at[0] == len(GROUPS)


_INS = ["x", "c", "ctx", "c_ctx", "w_mod", "b_mod", "norm_mix_g", "norm_ffn_g", "ev_w_in", "ev_q_norm_g", "ev_k_norm_g",
        "ev_dw_w", "ev_dw_b", "ev_ln_g", "ev_ln_b", "ev_w_out", "od_w_in", "od_conv_w", "od_w_out", "router_w",
        "router_bias", "moe_w_gate", "moe_w_up", "moe_w_down"]


def kernel(**inputs):
    import concourse.bacc as bacc
    from concourse.bass_utils import run_bass_kernel_spmd

    nc = bacc.Bacc("TRN2", target_bir_lowering=False, num_devices=1)
    arrays, args = {}, []
    values = {name: np.ascontiguousarray(inputs[name]) for name in _INS}
    values["consts"] = build_consts()
    for name, a in values.items():
        arrays[f"in_{name}"] = a
        args.append(nc.dram_tensor(f"in_{name}", a.shape, mybir.dt.from_np(a.dtype), kind="ExternalInput").ap())
    out = nc.dram_tensor("out_x", (1, SEQ, D), F32, kind="ExternalOutput").ap()
    hybrid_backbone_kernel(nc, *args, out)
    r = run_bass_kernel_spmd(nc, [arrays], core_ids=[0])
    return r.results[0]["out_x"]
```

```python
from contextlib import ExitStack

import numpy as np

import concourse.bass as bass
from concourse import mybir

F32 = mybir.dt.float32
I32 = mybir.dt.int32
ALU = mybir.AluOpType
ACT = mybir.ActivationFunctionType
AX_X = mybir.AxisListType.X

P = 128
D = 1024
KD = D // P
SEQ = 512
TT = SEQ // P
CTX = 256
CT = CTX // P
KT = TT + CT
HEADS, KVH, HD = 8, 2, 64
PAIRS = HEADS // 2
GRID_W = 64
CONV_K, CONV_C = 31, 512
PAD = CONV_K // 2
APAD = SEQ + 2 * PAD
SC_K = 3
NE, NG, EPG = 16, 4, 4
FE = 512
BLK = 64
MAXB = SEQ * 2 // BLK + NE
NB = MAXB + 3
NIDX = 4096
EPS = 1e-6
RING = 6
NBANK = 4

WITH_A = [(0, 6), (0, 7), (0, 8), (0, 9)]
WITH_AG = [(1, 0), (1, 1), (1, 2), (1, 3)]
WITH_Q = [(1, 6), (1, 7), (1, 8), (1, 9)]
GATES = [[(l, 4), (l, 5), (l, 10), (l, 11)] for l in range(2)]

CONSTS = {}


def build_consts():
    p = np.arange(P)
    parts = []

    def add(name, a):
        a = np.asarray(a, np.float32).reshape(P, -1)
        at = sum(x.shape[1] for x in parts)
        CONSTS[name] = (at, at + a.shape[1])
        parts.append(a)

    add("ident", np.eye(P))
    add("ones", np.ones((P, P)))
    add("before", p[:, None] < p[None, :])
    add("sel_both", np.stack([p % 32 == 0, p % 32 == 1], 1))
    add("sel_x", np.repeat((p % 32 == 0)[:, None], P, 1))
    add("sel_expert", p[:, None] % 32 == np.arange(NE)[None, :])
    add("slot_of_col", np.tile(p % BLK, (P, 1)))
    add("block_id", np.tile(np.arange(NB), (P, 1)))
    add("half", p // BLK)
    add("full_blocks", np.tile(np.arange(1, SEQ // BLK) * BLK, (P, 1)))
    add("group_key", np.tile(NG - np.arange(NG), (P, 1)))
    add("expert_key", np.tile(NE - np.arange(NE), (P, 1)))
    add("expert_before", np.tile((np.arange(NE)[None, :] < np.arange(NE + 1)[:, None]).ravel(), (P, 1)))
    token = np.arange(TT)[None, :, None] * P + p[:, None, None] + np.zeros((1, 1, 2))
    add("token", token)
    add("out_row", token + SEQ * np.arange(2)[None, None, :] - NIDX)
    add("minus_half", np.full((P, 1), -0.5))
    t = np.arange(SEQ)
    inv = (np.float32(10000.0) ** (-np.arange(HD // 4, dtype=np.float32) / np.float32(HD // 4))).astype(np.float32)
    ang = np.concatenate([(t // GRID_W).astype(np.float32)[:, None] * inv,
                          (t % GRID_W).astype(np.float32)[:, None] * inv], -1).astype(np.float32)
    for name, f in (("cos", np.cos), ("sin", np.sin)):
        add(name, f(ang.astype(np.float64)).reshape(TT, P, HD // 2).transpose(1, 0, 2))
    return np.ascontiguousarray(np.concatenate(parts, 1))


def plan_units():
    order = [("mod", 0, c) for c in range(4)] + [("kv",), ("a",)]
    order += [("mod",) + m for m in WITH_A] + [("ag",)] + [("mod",) + m for m in WITH_AG]
    order += [("q",)] + [("mod",) + m for m in WITH_Q] + [("mod",) + m for m in GATES[0]] + [("wo", 0), ("wo", 1)]
    return order


def plan_units_odd():
    return ([("gc", 0), ("v", 0), ("gb", 0), ("mod", 1, 4), ("mod", 1, 5), ("gc", 1), ("v", 1), ("gb", 1),
             ("mod", 1, 10), ("mod", 1, 11), ("ow", 0), ("ow", 1)])


def plan_groups():
    g = [("params",), ("taps",), ("bias",)]
    for c in range(4):
        g += [("mod", 0, c), ("fin", 0, c)]
    g += [("norm", "ctx", j) for j in range(KD)] + [("norm", "mix0", j) for j in range(KD)]
    g += [("kvz", t) for t in range(CT)] + [("kvx", t) for t in range(TT)]
    last = None
    for w, units in (("a", WITH_A), ("ag", WITH_AG), ("q", WITH_Q)):
        if w == "q":
            g += [("kT", v, h) for v in range(KVH) for h in range(2)]
        for i in range(4):
            g += [(w, i)] + ([("fin",) + last] if last else []) + [("mod",) + units[i]]
            last = units[i]
    g += [("fin",) + last]
    g += [("qT", i) for i in range(PAIRS)]
    for s in range(8):
        for u in range(4):
            g += [("PT", s, u, 0), ("PT", s, u, 1)]
        g += [("pv", s)]
    g += [("mu",)]
    for n, m in enumerate(GATES[0]):
        g += [("mod",) + m, ("fin",) + m] + [("var",)] * (n == 1)
    g += [("ln_rstd",)]
    g += [("out", 0, h, t) for h in range(2) for t in range(TT)]
    g += [("norm", "ffn0", j) for j in range(KD)] + [("route", 0, k) for k in range(4)]
    g += [("norm", "mix1", j) for j in range(KD)]
    for h in range(2):
        for i in range(4):
            g += [(w, h * 4 + i) for w in ("gc", "v", "gb")]
        for m in GATES[1][2 * h:2 * h + 2]:
            g += [("mod",) + m, ("fin",) + m]
    g += [("out", 1, h, t) for h in range(2) for t in range(TT)]
    g += [("norm", "ffn1", j) for j in range(KD)] + [("route", 1, k) for k in range(4)]
    return g


GROUPS = plan_groups()
GROUP_AT = {name: n for n, name in enumerate(GROUPS)}
assert len(GROUP_AT) == len(GROUPS)


def hybrid_backbone_kernel(nc, x, c, ctx, c_ctx, w_mod, b_mod, norm_mix_g, norm_ffn_g, ev_w_in,
                           ev_q_norm_g, ev_k_norm_g, ev_dw_w, ev_dw_b, ev_ln_g, ev_ln_b, ev_w_out,
                           od_w_in, od_conv_w, od_w_out, router_w, router_bias, moe_w_gate, moe_w_up,
                           moe_w_down, consts, out):
    stack = ExitStack()
    with stack:
        def sb(name, shape, dt=F32):
            return stack.enter_context(nc.sbuf_tensor(name, shape, dt))

        def sem(name):
            return stack.enter_context(nc.semaphore(name))

        ring = sb("ring", [P, RING, KD, 512])
        xs = sb("xs", [P, TT, D])
        hT_cat = sb("hT_cat", [P, KD, SEQ])
        big = sb("big", [P, 4096])
        mid = sb("mid", [P, 4096])
        qT = sb("qT", [P, PAIRS, SEQ])
        kv_buf = sb("kv_buf", [P, 3 * KT * P])
        cact = sb("cact", [P, KD, 32])
        b_rows = sb("b_rows", [P, 512])
        prob = sb("prob", [P, 2, KT * P])
        apad = sb("apad", [P, 4, APAD])
        cst = sb("cst", [P, consts.shape[1]])
        modrow = sb("modrow", [P, 512])
        params = sb("params", [P, 44])
        taps = sb("taps", [P, KD, 34])
        modcol = sb("modcol", [P, 2, 12, 4, 2])
        mod_a = sb("mod_a", [P, 5, KD])
        stats = sb("stats", [P, 4, KT])
        qkg = sb("qkg", [P, 2, HD])
        head_stats = sb("head_stats", [P, 4, 32])
        softm = sb("softm", [P, 4, 2])
        bias_r = sb("bias_r", [P, NE])
        small = sb("small", [P, 4])
        block_start = sb("block_start", [P, NE + 1], I32)
        route_w = sb("route_w", [P, KD, 32])
        bias_col = sb("bias_col", [P, 4, 24])
        ln_col = sb("ln_col", [P, 2, TT])
        rowid = sb("rowid", [P, 3, NB])
        row_i = sb("row_i", [P, 2, NB], I32)
        cur_idx = sb("cur_idx", [P, 2, 1], I32)
        tick = sb("tick", [P, 1])

        xhat = big[:, 0:4096].rearrange("p (t d) -> p t d", t=TT)
        ctx_x = kv_buf[:, 0:CT * D].rearrange("p (t d) -> p t d", t=CT)
        kT2 = kv_buf[:, 0:KVH * KT * P].rearrange("p (v k) -> p v k", v=KVH)
        vtok = kv_buf[:, KVH * KT * P:].rearrange("p (t d) -> p t d", t=KT)
        PT = [[v.rearrange("p (k q) -> p k q", k=KT) for v in pair] for pair in
              ((big[:, 0:1536], big[:, 1536:3072]),
               (hT_cat[:, 4:7, :].rearrange("p a b -> p (a b)"), mid[:, 0:1536]))]
        junk = mid[:, 0:D]
        gate_mix = qT[:, 0:2, :].rearrange("p a b -> p (a b)")
        gate_ffn = qT[:, 2, :]
        mT = xhat.rearrange("p t (j q) -> p (t j) q", q=512)
        hzT = mid[:, 0:2048].rearrange("p (j t) -> p j t", j=KD)
        ctx_hat = mid[:, 2048:4096].rearrange("p (t d) -> p t d", t=CT)
        qtok = mid[:, 0:2048].rearrange("p (t d) -> p t d", t=TT)
        ktok = prob[:, 0, :].rearrange("p (t d) -> p t d", t=KT)
        qtmp = prob[:, 1, :]
        conv_y = mid[:, 2048:4096].rearrange("p (t d) -> p t d", t=4)
        staging = qT[:, 0:2, :].rearrange("p a b -> p (a b)")
        craw = qT[:, 2, 0:16].rearrange("p (s k) -> p s k", s=2)
        gc_sb = [mid[:, 0:512], mid[:, 512:1024]]
        u_pad = [mid[:, 1024 + 520 * i:1024 + 520 * i + SEQ + 2] for i in range(2)]
        sc_y = [mid[:, 2560:3072], mid[:, 3072:3584]]
        work = apad[:, :, :].rearrange("p a b -> p (a b)")
        hg_raw = hT_cat[:, 0, :]
        hg_next = work[:, 0:512]
        hgT = work[:, 512:1024].rearrange("p (j s) -> p j s", j=KD)
        silu_g = work[:, 1024:1280]
        act_sb = work[:, 1280:1536]
        actT = work[:, 1536:1792].rearrange("p (j s) -> p j s", j=2)
        y_blk = prob[:, 0, 0:512]
        y_out = kv_buf[:, 0:512]
        y_in = [big[:, 0:2048].rearrange("p (k d) -> p k d", k=2), big[:, 2048:4096].rearrange("p (k d) -> p k d", k=2)]
        router_rows = prob[:, 1, 0:512]
        rt = work
        rt_at = [0]

        def rtmp(*shape):
            n = int(np.prod(shape))
            a = rt[:, rt_at[0]:rt_at[0] + n]
            rt_at[0] += n
            if len(shape) == 1:
                return a
            names = "abcd"[:len(shape)]
            return a.rearrange(f"p ({' '.join(names)}) -> p {' '.join(names)}", **dict(zip(names[1:], shape[1:])))

        aff, sel, selm, oh1, oh2 = (rtmp(TT, NE) for _ in range(5))
        r16, picked, base16 = (rtmp(TT, NE) for _ in range(3))
        g_a, g_b, g_c, g_d = (rtmp(TT, NG) for _ in range(4))
        r4, w_sum = rtmp(TT, 1), rtmp(TT, 1)
        before16, total16 = rtmp(TT, NE), rtmp(TT, NE)
        count16, nblk16 = rtmp(NE), rtmp(NE)
        cmp16 = rtmp(NE, SEQ // BLK - 1)
        start_cmp = rtmp(NE + 1, NE)
        start_f = rtmp(NE + 1)
        pos2, st2, full2, slot2, blk2, w2 = (rtmp(TT, 2) for _ in range(6))
        cmp2 = rtmp(TT * 2, SEQ // BLK - 1)
        assert rt_at[0] <= 4 * APAD
        oh_slot = mid[:, 0:1024].rearrange("p (n s) -> p n s", s=P)
        oh_blk = mid[:, 1024:1024 + 8 * NB].rearrange("p (n b) -> p n b", b=NB)
        val_blk = mid[:, 1536:1536 + 24 * NB].rearrange("p (n v b) -> p n v b", v=3, b=NB)

        def const(name):
            a, b = CONSTS[name]
            return cst[:, a:b]

        ident = const("ident")

        psum = [stack.enter_context(nc.psum_tensor(f"bank{i}", [P, 512], F32)) for i in range(4)]
        score_ps = [stack.enter_context(nc.psum_tensor(f"scores{i}", [P, 1024], F32)) for i in range(2)]
        gate_ps, up_ps, hg_dve_ps, at_ps = psum
        hg_act_ps = score_ps[1][:, 0:2 * P]
        y_ps = score_ps[0][:, 0:512]

        xhat_d = nc.dram_tensor("xhat_d", [SEQ * 2, 512], F32).ap()
        y_d = [nc.dram_tensor(f"y_d{l}", [SEQ * 4, 512], F32).ap() for l in range(2)]

        unit_in = [sem(f"unit_in{s}") for s in range(RING)]
        consts_in, x_in, ctx_in, c_in, rows_in, bmod_in, qkg_in, router_in = (
            sem(n) for n in ("consts_in", "x_in", "ctx_in", "c_in", "rows_in", "bmod_in", "qkg_in", "router_in"))
        zeroed = sem("zeroed")
        cact_ready = sem("cact_ready")
        acc_done = sem("acc_done")
        bank_read = {}
        modrow_ready = sem("modrow_ready")
        modcol_ready = [sem(f"modcol_ready{i}") for i in range(4)]
        gates_ready = sem("gates_ready")
        dve_step, act_step, pool_step = sem("dve_step"), sem("act_step"), sem("pool_step")
        MOD_OF = {"ctx": 0, "mix0": 0, "ffn0": 1, "mix1": 2, "ffn1": 3}
        norms = ("ctx", "mix0", "ffn0", "mix1", "ffn1")
        ssq_ready = {n: sem(f"ssq_{n}") for n in norms}
        rstd_ready = {n: sem(f"rstd_{n}") for n in norms}
        xhat_ready = {n: sem(f"xhat_{n}") for n in norms}
        hT_even = {n: sem(f"hT_even_{n}") for n in norms}
        hT_odd = {n: sem(f"hT_odd_{n}") for n in norms}
        kv_ready = sem("kv_ready")
        k_ssq, k_rstd, q_ssq, q_rstd = sem("k_ssq"), sem("k_rstd"), sem("q_ssq"), sem("q_rstd")
        k_roped, q_roped, q_ready = sem("k_roped"), sem("q_roped"), sem("q_ready")
        kT_ready, qT_ready = sem("kT_ready"), sem("qT_ready")
        a_ready, ag_ready, glu_ready = sem("a_ready"), sem("ag_ready"), sem("glu_ready")
        scores_done, max_ready, exp_ready, prob_ready = (
            sem(n) for n in ("scores_done", "max_ready", "exp_ready", "prob_ready"))
        PT_ready, attn_ready = sem("PT_ready"), sem("attn_ready")
        tap_done = sem("tap_done")
        centred, sq_ready, var_ready, ln_rstd, diag_ready, ln_done, cat_ready = (
            sem(n) for n in ("centred", "sq_ready", "var_ready", "ln_rstd", "diag_ready", "ln_done", "cat_ready"))
        x_new = [sem(f"x_new{l}") for l in range(2)]
        xhat_stored = [sem(f"xhat_stored{l}") for l in range(2)]
        router_turned = [sem(f"router_turned{l}") for l in range(2)]
        aff_ready = [sem(f"aff_ready{l}") for l in range(2)]
        mask_ready = [sem(f"mask_ready{l}") for l in range(2)]
        table_in = [sem(f"table_in{l}") for l in range(2)]
        route_ready = [sem(f"route_ready{l}") for l in range(2)]
        idx_ready = [sem(f"idx_ready{l}") for l in range(2)]
        hg_in = [sem(f"hg_in{l}") for l in range(2)]
        hg_moved = [sem(f"hg_moved{l}") for l in range(2)]
        hg_turned = [sem(f"hg_turned{l}") for l in range(2)]
        hgT_dve = [sem(f"hgT_dve{l}") for l in range(2)]
        hgT_act = [sem(f"hgT_act{l}") for l in range(2)]
        gate_done = [sem(f"gate_done{l}") for l in range(2)]
        up_done = [sem(f"up_done{l}") for l in range(2)]
        silu_ready = [sem(f"silu_ready{l}") for l in range(2)]
        act_ready = [sem(f"act_ready{l}") for l in range(2)]
        act_turned = [sem(f"act_turned{l}") for l in range(2)]
        actT_ready = [sem(f"actT_ready{l}") for l in range(2)]
        down_done = [sem(f"down_done{l}") for l in range(2)]
        y_read = [sem(f"y_read{l}") for l in range(2)]
        y_moved = [sem(f"y_moved{l}") for l in range(2)]
        y_stored = [sem(f"y_stored{l}") for l in range(2)]
        ticked = [sem(f"ticked{l}") for l in range(2)]
        yin = [[sem(f"yin{l}_{i}") for i in range(2)] for l in range(2)]
        y_added = [sem(f"y_added{l}") for l in range(2)]
        gc_ready, u_ready, mT_ready = sem("gc_ready"), sem("u_ready"), sem("mT_ready")
        out_done = sem("out_done")

        unit_slot, unit_count, unit_order, loads = {}, {}, [], [0] * RING
        prev_owner = [None] * RING
        unit_prev = {}

        def place(name, slot):
            loads[slot] += 1
            unit_slot[name], unit_count[name] = slot, loads[slot] * 16
            unit_prev[name] = prev_owner[slot]
            prev_owner[slot] = name
            unit_order.append(name)

        even_units = plan_units()
        for n, name in enumerate(even_units):
            place(name, (n + 4) % RING)
        moe_base = []
        moe_base.append(list(loads))
        for e in range(NE):
            for k, w in enumerate(("wg", "wu", "wd")):
                place((w, 0, e), (3 * e + k) % RING)
        odd_units = plan_units_odd()
        for n, name in enumerate(odd_units):
            place(name, n % RING)
        moe_base.append(list(loads))
        for e in range(NE):
            for k, w in enumerate(("wg", "wu", "wd")):
                place((w, 1, e), (3 * e + k) % RING)
        unit_last = {("kv",): ("kvx", TT - 1), ("a",): ("a", 3), ("ag",): ("ag", 3), ("q",): ("q", TT - 1)}
        for name in even_units + odd_units:
            if name[0] == "mod":
                unit_last[name] = name
            elif name[0] in ("wo", "ow"):
                unit_last[name] = ("out", 0 if name[0] == "wo" else 1, name[1], TT - 1)
            elif len(name) == 2:
                unit_last[name] = (name[0], 4 * name[1] + 3)

        wmod_v = [w_mod[l].rearrange("(p k) n -> p k n", k=KD) for l in range(2)]
        win_v = ev_w_in[0].rearrange("(k p) n -> p k n", p=P)
        wout_v = ev_w_out[0].rearrange("(k p) n -> p k n", p=P)
        oin_v = od_w_in[0].rearrange("(k p) n -> p k n", p=P)
        oout_v = od_w_out[0].rearrange("(k p) n -> p k n", p=P)
        kv_at = HEADS * HD
        a_at = kv_at + 2 * KVH * HD
        wg_v = moe_w_gate.rearrange("l e (k p) n -> (l e) p k n", p=P)
        wu_v = moe_w_up.rearrange("l e (k p) n -> (l e) p k n", p=P)
        wd_v = moe_w_down.rearrange("l e (k p) n -> (l e) p k n", p=P)

        def unit_source(name):
            w = name[0]
            if w == "mod":
                return wmod_v[name[1]][:, :, name[2] * 512:(name[2] + 1) * 512]
            if w == "kv":
                return win_v[:, :, kv_at:a_at]
            if w == "a":
                return win_v[:, :, a_at:a_at + 512]
            if w == "ag":
                return win_v[:, :, a_at + 512:a_at + 1024]
            if w == "q":
                return win_v[:, :, 0:512]
            if w == "wo":
                return wout_v[:, :, name[1] * 512:(name[1] + 1) * 512]
            if w == "ow":
                return oout_v[:, :, name[1] * 512:(name[1] + 1) * 512]
            at = {"gb": 0, "gc": D, "v": 2 * D}[w] + name[1] * 512
            return oin_v[:, :, at:at + 512]

        def unit(name):
            return ring[:, unit_slot[name]]

        def expert_view(slot, w):
            u = ring[:, slot]
            return u.rearrange("p k n -> p (k n)").rearrange("p (k n) -> p k n", n=D) if w == "wd" else u

        def bank(name):
            return psum[GROUP_AT[name] % NBANK]

        block = stack.enter_context(nc.Block())

        @block.sync
        def _(sp):
            def load_dense(name):
                prev = unit_prev[name]
                if prev in unit_last:
                    sp.wait_ge(acc_done, GROUP_AT[unit_last[prev]] + 1)
                src = unit_source(name)
                dst = unit(name)
                if name[0] == "kv":
                    dst = dst[:, :, 0:256]
                sp.dma_start(dst, src).then_inc(unit_in[unit_slot[name]], 16)

            def load_third(l, e, par, k):
                slot = 3 * par + k
                src = (wg_v, wu_v, wd_v)[k][bass.ds(e + l * NE, 1)].rearrange("o p k n -> (o p) k n")
                sp.dma_start(expert_view(slot, "wd" if k == 2 else "wg"), src).then_inc(unit_in[slot], 16)

            def load_experts(l, next_units):
                for par in range(2):
                    for k, w in enumerate(("wg", "wu", "wd")):
                        prev = unit_prev[(w, l, par)]
                        sp.wait_ge(acc_done, GROUP_AT[unit_last[prev]] + 1)
                        load_third(l, par, par, k)
                sp.wait_ge(route_ready[l], 1)
                used = (gate_done[l], up_done[l], down_done[l])
                with sp.Fori(1, NE // 2) as i:
                    for par in range(2):
                        end = sp.value_load(block_start[0:1, bass.ds(i * 2 + (par - 1), 1)], min_val=1, max_val=MAXB)
                        for k in range(3):
                            sp.wait_ge(used[k], end)
                            load_third(l, i * 2 + par, par, k)
                end = sp.value_load(block_start[0:1, NE - 1:NE], min_val=NE - 1, max_val=MAXB)
                total = sp.value_load(block_start[0:1, NE:NE + 1], min_val=NE, max_val=MAXB)
                sp.wait_ge(down_done[l], end)
                for name in next_units[0:3]:
                    load_dense(name)
                sp.wait_ge(down_done[l], total)
                sp.wait_ge(y_stored[l], total * 16 + 16)
                for t in range(TT):
                    if t >= 2:
                        sp.wait_ge(y_added[l], t - 1)
                    for k in range(2):
                        rows = y_d[l][(k * SEQ + t * P) * 2:(k * SEQ + (t + 1) * P) * 2, :].rearrange("(p h) n -> p (h n)", h=2)
                        sp.dma_start(y_in[t % 2][:, k, :], rows).then_inc(yin[l][t % 2], 16)
                for name in next_units[3:]:
                    load_dense(name)

            sp.dma_start(cst[:, :], consts).then_inc(consts_in, 16)
            sp.dma_start(craw[:, 0, :], c.rearrange("o (p k) -> (o p) k", k=KD)).then_inc(c_in, 16)
            sp.dma_start(craw[:, 1, :], c_ctx.rearrange("(p k) -> p k", k=KD)).then_inc(c_in, 16)
            load_dense(even_units[0])
            sp.wait_ge(zeroed, 1)
            sp.dma_start(staging[0:16, 0:P], norm_mix_g.rearrange("l (j p) -> (l j) p", p=P)).then_inc(rows_in, 16)
            sp.dma_start(staging[16:32, 0:P], norm_ffn_g.rearrange("l (j p) -> (l j) p", p=P)).then_inc(rows_in, 16)
            for k, v in enumerate((ev_dw_b, ev_ln_g, ev_ln_b)):
                sp.dma_start(staging[32 + 4 * k:36 + 4 * k, 0:P], v.rearrange("o (j p) -> (o j) p", p=P)).then_inc(rows_in, 16)
            sp.dma_start(hT_cat[0:CONV_K, 0, :], ev_dw_w[0]).then_inc(rows_in, 16)
            sp.dma_start(hT_cat[CONV_K:CONV_K + SC_K, 0:2, :], od_conv_w[0].rearrange("k (a n) -> k a n", a=2)).then_inc(rows_in, 16)
            sp.dma_start(b_rows[0:24, :], b_mod.rearrange("l (c n) -> (l c) n", n=512)).then_inc(bmod_in, 16)
            for name in even_units[1:]:
                load_dense(name)
            load_experts(0, odd_units)
            load_experts(1, [])
            for t in range(TT):
                sp.wait_ge(y_added[1], t + 1)
                sp.dma_start(out[0, t * P:(t + 1) * P, :], xs[:, t, :]).then_inc(out_done, 16)
            sp.wait_ge(out_done, 16 * TT)

        @block.scalar
        def _(act):
            steps = [0]

            def link(ins):
                steps[0] += 1
                ins.then_inc(act_step, 1)
                act.wait_ge(act_step, steps[0])

            def acc_wait(name):
                act.wait_ge(acc_done, GROUP_AT[name] + 1)

            act.dma_start(xs[:, :, :], x[0].rearrange("(t p) d -> p t d", p=P)).then_inc(x_in, 16)
            act.dma_start(ctx_x, ctx[0].rearrange("(t p) d -> p t d", p=P)).then_inc(ctx_in, 16)
            act.dma_start(qkg[:, 0, :], ev_q_norm_g.to_broadcast([P, HD])).then_inc(qkg_in, 16)
            act.dma_start(qkg[:, 1, :], ev_k_norm_g.to_broadcast([P, HD])).then_inc(qkg_in, 16)
            act.wait_ge(zeroed, 1)
            act.dma_start(route_w[:, :, 0:NE], router_w.rearrange("(k p) n -> p k n", p=P)).then_inc(router_in, 16)
            act.dma_start(bias_r[:, :], router_bias.rearrange("(o n) -> o n", o=1).to_broadcast([P, NE])).then_inc(router_in, 16)

            act.wait_ge(c_in, 32)
            for s in range(2):
                act.activation(cact[:, :, s], craw[:, s, :], ACT.Silu).then_inc(cact_ready, 1)

            mods = [0]

            def modrow_copy(l, c):
                acc_wait(("mod", l, c))
                if mods[0]:
                    act.wait_ge(acc_done, last_fin[0] + 1)
                act.activation(modrow[:, :], bank(("mod", l, c))[:, :], ACT.Copy).then_inc(modrow_ready, 1)
                mods[0] += 1
                bank_read[("mod", l, c)] = (modrow_ready, mods[0])
                last_fin[0] = GROUP_AT[("fin", l, c)]

            last_fin = [0]

            squared = []

            def squares(norm, src, tiles, wait):
                first = TT if norm == "ctx" else 0
                for t in range(tiles):
                    wait(t)
                    if squared:
                        act.wait_ge(*squared[-1])
                    act.activation(junk, src[:, t, :], ACT.Square,
                                   accum_out=stats[:, 0, first + t:first + t + 1]).then_inc(ssq_ready[norm], 1)
                    squared.append((ssq_ready[norm], t + 1))

            squares("mix0", xs, TT, lambda t: act.wait_ge(x_in, 16))

            def modulate(norm, dst, n, scale, shift, chunks):
                act.wait_ge(modcol_ready[MOD_OF[norm]], 1)
                for j in chunks:
                    g = ("norm", norm, j)
                    acc_wait(g)
                    act.activation(dst[:, j, :], bank(g)[:, 0:n], ACT.Identity, bias=shift(j),
                                   scale=scale(j)).then_inc(hT_even[norm], 1)
                    bank_read[g] = (hT_even[norm], j // 2 + 1)

            def shift_of(l, which, s):
                return lambda j: modcol[:, l, 2 * which + j // 4, j % 4, s:s + 1]

            for c_ in range(4):
                modrow_copy(0, c_)
                if c_ == 1:
                    squares("ctx", ctx_x, CT, lambda t: act.wait_ge(ctx_in, 16))
            modulate("ctx", hzT, CTX, lambda j: mod_a[:, 4, j:j + 1], shift_of(0, 0, 1), range(0, KD, 2))
            modulate("mix0", hT_cat, SEQ, lambda j: mod_a[:, 0, j:j + 1], shift_of(0, 0, 0), range(0, KD, 2))

            for t in range(KT):
                tile = ("kvz", t) if t < CT else ("kvx", t - CT)
                at = TT + t if t < CT else t - CT
                acc_wait(tile)
                act.activation(ktok[:, at, :], bank(tile)[:, 0:P], ACT.Copy).then_inc(kv_ready, 1)
                act.activation(vtok[:, at, :], bank(tile)[:, P:2 * P], ACT.Copy).then_inc(kv_ready, 1)
                bank_read[tile] = (kv_ready, 2 * t + 2)
            for i in range(4):
                acc_wait(("a", i))
                act.activation(apad[:, i, PAD:PAD + SEQ], bank(("a", i))[:, :], ACT.Copy).then_inc(a_ready, 1)
                bank_read[("a", i)] = (a_ready, i + 1)
                modrow_copy(*WITH_A[i])
            for i in range(4):
                acc_wait(("ag", i))
                if i >= 2:
                    act.wait_ge(glu_ready, i - 1)
                act.activation(qT[:, i % 2, :], bank(("ag", i))[:, :], ACT.Sigmoid).then_inc(ag_ready, 1)
                bank_read[("ag", i)] = (ag_ready, i + 1)
                modrow_copy(*WITH_AG[i])
            for v in range(KVH):
                for h in range(2):
                    g = ("kT", v, h)
                    acc_wait(g)
                    act.activation(kT2[:, v, h * 384:(h + 1) * 384], bank(g)[:, 0:384], ACT.Copy).then_inc(kT_ready, 1)
                    bank_read[g] = (kT_ready, 2 * v + h + 1)
            for t in range(TT):
                acc_wait(("q", t))
                act.activation(qtok[:, t, :], bank(("q", t))[:, :], ACT.Copy).then_inc(q_ready, 1)
                bank_read[("q", t)] = (q_ready, t + 1)
                modrow_copy(*WITH_Q[t])
            for i in range(PAIRS):
                acc_wait(("qT", i))
                act.activation(qT[:, i, :], bank(("qT", i))[:, :], ACT.Copy).then_inc(qT_ready, 1)
                bank_read[("qT", i)] = (qT_ready, i + 1)


            def exps(n):
                act.wait_ge(max_ready, n + 1)
                if n >= 2:
                    acc_wait(("PT", (n - 2) // 4, (n - 2) % 4, 1))
                act.activation(prob[:, n % 2, :], score_ps[n % 2][:, 0:KT * P], ACT.Exp, bias=softm[:, 0, n % 2:n % 2 + 1],
                               scale=HD ** -0.5, accum_out=softm[:, 1, n % 2:n % 2 + 1]).then_inc(exp_ready, 1)

            exps(0)
            for s in range(8):
                for u in range(4):
                    n = 4 * s + u
                    if n + 1 < 32:
                        exps(n + 1)
                    hh, qt = u // 2, u % 2
                    for g3 in range(2):
                        g = ("PT", s, u, g3)
                        acc_wait(g)
                        if s >= 2:
                            acc_wait(("pv", s - 2))
                        act.activation(PT[s % 2][hh][:, 3 * g3:3 * g3 + 3, qt * P:(qt + 1) * P],
                                       bank(g)[:, 0:384].rearrange("p (k q) -> p k q", k=3),
                                       ACT.Copy).then_inc(PT_ready, 1)
                        bank_read[g] = (PT_ready, 2 * n + g3 + 1)
                acc_wait(("pv", s))
                act.activation(hT_cat[:, s // 2, (s % 2) * 256:(s % 2 + 1) * 256], bank(("pv", s))[:, 0:256],
                               ACT.Copy).then_inc(attn_ready, 1)
                bank_read[("pv", s)] = (attn_ready, s + 1)

            for m in GATES[0]:
                modrow_copy(*m)
            for i in range(4):
                act.wait_ge(ln_done, i + 1)
                act.activation(hT_cat[:, 4 + i, :], conv_y[:, i, :], ACT.Silu, bias=params[:, 40 + i:41 + i],
                               scale=params[:, 36 + i:37 + i]).then_inc(cat_ready, 1)

            def ffn(l):
                norm = f"ffn{l}"
                squares(norm, xs, TT, lambda t: act.wait_ge(x_new[l], TT + t + 1))
                for t in range(TT):
                    act.wait_ge(xhat_ready[norm], t + 1)
                    act.dma_start(xhat_d[t * 2 * P:(t + 1) * 2 * P, :].rearrange("(p h) n -> p (h n)", h=2),
                                  xhat[:, t, :]).then_inc(xhat_stored[l], 16)
                modulate(norm, hT_cat, SEQ, lambda j: mod_a[:, 1 + 2 * l, j:j + 1], shift_of(l, 3, 0), range(0, KD, 2))
                acc_wait(("route", l, 0))
                act.activation(router_rows, bank(("route", l, 0))[:, :], ACT.Copy).then_inc(router_turned[l], 1)
                bank_read[("route", l, 0)] = (router_turned[l], 1)
                acc_wait(("route", l, 1))
                act.activation(aff.rearrange("p a b -> p (a b)"), bank(("route", l, 1))[:, 0:TT * NE],
                               ACT.Sigmoid).then_inc(aff_ready[l], 1)
                bank_read[("route", l, 1)] = (aff_ready[l], 1)

                def turn_in():
                    for j in (2, 3, 6, 7):
                        at = (j % 4 - 2) * P + (j // 4) * BLK
                        act.activation(hgT[:, j, :], hg_act_ps[:, at:at + BLK], ACT.Identity,
                                       bias=shift_of(l, 3, 0)(j), scale=mod_a[:, 1 + 2 * l, j:j + 1]).then_inc(hgT_act[l], 1)

                act.wait_ge(route_ready[l], 1)
                total = act.value_load(block_start[0:1, NE:NE + 1], min_val=NE, max_val=MAXB)

                def move_on(b_plus_1):
                    act.wait_ge(hg_in[l], b_plus_1 * 16)
                    act.activation(hg_next, hg_raw, ACT.Copy).then_inc(hg_moved[l], 1)

                move_on(1)
                act.wait_ge(hg_turned[l], 1)
                turn_in()
                move_on(2)
                with act.Fori(0, total) as b:
                    act.wait_ge(gate_done[l], b + 1)
                    act.activation(silu_g, gate_ps[:, 0:256], ACT.Silu).then_inc(silu_ready[l], 1)
                    act.wait_ge(hg_turned[l], b + 2)
                    act.wait_ge(up_done[l], b + 1)
                    turn_in()
                    move_on(b + 3)

            ffn(0)

            squares("mix1", xs, TT, lambda t: act.wait_ge(y_added[0], t + 1))
            modulate("mix1", hT_cat, SEQ, lambda j: mod_a[:, 2, j:j + 1], shift_of(1, 0, 0), range(0, KD, 2))
            for h in range(2):
                for i in range(4):
                    m = 4 * h + i
                    acc_wait(("gc", m))
                    if m >= 2:
                        act.wait_ge(u_ready, m - 1)
                    act.activation(gc_sb[m % 2], bank(("gc", m))[:, :], ACT.Copy).then_inc(gc_ready, 1)
                    bank_read[("gc", m)] = (gc_ready, m + 1)
                for m_ in GATES[1][2 * h:2 * h + 2]:
                    modrow_copy(*m_)
            ffn(1)

        @block.vector
        def _(dve):
            steps = [0]

            def link(ins):
                steps[0] += 1
                ins.then_inc(dve_step, 1)
                dve.wait_ge(dve_step, steps[0])

            def acc_wait(name):
                dve.wait_ge(acc_done, GROUP_AT[name] + 1)

            V = nc.vector
            V.memset(b_rows[:, :], 0.0)
            V.memset(staging[:, 0:P], 0.0)
            V.memset(route_w[:, :, :].rearrange("p k m -> p (k m)"), 0.0)
            V.memset(cact[:, :, :].rearrange("p k m -> p (k m)"), 0.0)
            V.memset(apad[:, :, 0:PAD], 0.0)
            V.memset(apad[:, :, PAD + SEQ:APAD], 0.0)
            for l in range(2):
                V.memset(small[:, l:l + 1], 0.0).then_inc(y_read[l], 1)
                V.memset(small[:, 2 + l:3 + l], 0.0).then_inc(ticked[l], 1)
            V.memset(hT_cat[0:34, 1, :], 0.0).then_inc(zeroed, 1)

            acc_wait(("params",))
            link(V.tensor_copy(params[:, :], bank(("params",))[:, 0:44]))
            bank_read[("params",)] = (dve_step, steps[0])
            acc_wait(("taps",))
            link(V.tensor_copy(taps[:, :, :], bank(("taps",))[:, 0:KD * 34].rearrange("p (j k) -> p j k", j=KD)))
            bank_read[("taps",)] = (dve_step, steps[0])

            acc_wait(("bias",))
            link(V.tensor_copy(bias_col[:, :, :], bank(("bias",))[:, 0:4 * 24].rearrange("p (j c) -> p j c", j=4)))
            bank_read[("bias",)] = (dve_step, steps[0])

            gates = [0]

            def fin(l, c):
                g = ("fin", l, c)
                acc_wait(g)
                if c in (4, 5, 10, 11):
                    gates[0] += 1
                    bank_read[g] = (gates_ready, gates[0])
                if c in (4, 5):
                    V.tensor_copy(gate_mix[:, (c - 4) * 512:(c - 3) * 512], bank(g)[:, :]).then_inc(gates_ready, 1)
                elif c in (10, 11):
                    h = c - 10
                    V.tensor_copy(gate_ffn[h * 64:(h + 1) * 64, :], bank(g)[h * 64:(h + 1) * 64, :]).then_inc(gates_ready, 1)
                else:
                    link(V.tensor_tensor(modcol[:, l, c, :, :], bank(g)[:, 0:8].rearrange("p (j s) -> p j s", s=2),
                                         bias_col[:, :, 12 * l + c].unsqueeze(2).to_broadcast([P, 4, 2]), ALU.add))
                    bank_read[g] = (dve_step, steps[0])
                if c in (3, 9):
                    first = c - 1
                    gcol = (0 if c == 3 else 16) + 8 * l
                    at = 2 * l + (0 if c == 3 else 1)
                    for s in range(1 if (l, c) == (0, 3) else 0, -1, -1):
                        ins = V.scalar_tensor_tensor(out=mod_a[:, 4 if s else at, :].rearrange("p (h j) -> p h j", h=2),
                                                     in0=modcol[:, l, first:first + 2, :, s], scalar=1.0,
                                                     in1=params[:, gcol:gcol + 8].rearrange("p (h j) -> p h j", h=2),
                                                     op0=ALU.add, op1=ALU.mult)
                    ins.then_inc(modcol_ready[at], 1)

            def normalise(norm, src, tiles):
                dst = xhat if norm != "ctx" else ctx_hat
                for t in tiles:
                    dve.wait_ge(rstd_ready[norm], t + 1)
                    V.tensor_scalar(dst[:, t, :], src[:, t, :], stats[:, 1 if norm != "ctx" else 2, t:t + 1], None,
                                    ALU.mult).then_inc(xhat_ready[norm], 1)

            def modulate(norm, dst, n, scale, shift):
                dve.wait_ge(modcol_ready[MOD_OF[norm]], 1)
                for j in range(1, KD, 2):
                    g = ("norm", norm, j)
                    acc_wait(g)
                    V.tensor_scalar(dst[:, j, :], bank(g)[:, 0:n], scale(j), shift(j), ALU.mult,
                                    ALU.add).then_inc(hT_odd[norm], 1)
                    bank_read[g] = (hT_odd[norm], j // 2 + 1)

            def shift_of(l, which, s):
                return lambda j: modcol[:, l, 2 * which + j // 4, j % 4, s:s + 1]

            normalise("mix0", xs, range(TT))
            for c_ in range(3):
                fin(0, c_)
            normalise("ctx", ctx_x, range(CT))
            fin(0, 3)
            modulate("ctx", hzT, CTX, lambda j: mod_a[:, 4, j:j + 1], shift_of(0, 0, 1))
            modulate("mix0", hT_cat, SEQ, lambda j: mod_a[:, 0, j:j + 1], shift_of(0, 0, 0))

            def head_norm(v, tmp, n, nh, g, stat, ssq, rstd, count):
                link(V.tensor_tensor(tmp, v, v, ALU.mult))
                V.tensor_reduce(head_stats[:, stat, 0:n * nh], tmp.rearrange("p (m d) -> p m d", d=HD), AX_X,
                                ALU.add).then_inc(ssq, 1)
                dve.wait_ge(rstd, count)
                v3 = v.rearrange("p (m d) -> p m d", d=HD)
                link(V.tensor_tensor(v3, v3, head_stats[:, stat, 0:n * nh].unsqueeze(2).to_broadcast([P, n * nh, HD]), ALU.mult))
                link(V.tensor_tensor(v3, v3, qkg[:, g, :].unsqueeze(1).to_broadcast([P, n * nh, HD]), ALU.mult))

            def rope(v, tmp, tile, nh, done):
                x12 = v.rearrange("p (h i two) -> p two h i", h=nh, two=2)
                half = nh * HD // 2
                t1 = tmp[:, 0:half].rearrange("p (h i) -> p h i", h=nh)
                t2 = tmp[:, half:2 * half].rearrange("p (h i) -> p h i", h=nh)
                cs = const("cos")[:, tile * 32:(tile + 1) * 32].unsqueeze(1).to_broadcast([P, nh, 32])
                sn = const("sin")[:, tile * 32:(tile + 1) * 32].unsqueeze(1).to_broadcast([P, nh, 32])
                x1, x2 = x12[:, 0], x12[:, 1]
                V.tensor_tensor(t1, x1, sn, ALU.mult)
                link(V.tensor_tensor(t2, x2, sn, ALU.mult))
                V.tensor_tensor(x1, x1, cs, ALU.mult)
                link(V.tensor_tensor(x2, x2, cs, ALU.mult))
                link(V.tensor_tensor(x2, x2, t1, ALU.add))
                V.tensor_tensor(x1, x1, t2, ALU.subtract).then_inc(done, 1)

            dve.wait_ge(kv_ready, 2 * KT)
            dve.wait_ge(qkg_in, 32)
            head_norm(ktok.rearrange("p t d -> p (t d)"), qtmp, KT, KVH, 1, 0, k_ssq, k_rstd, 1)
            for t in range(TT):
                rope(ktok[:, t, :], qtmp[:, t * P:(t + 1) * P], t, KVH, k_roped)

            tap_list = [(k, i) for pair in ((0, 1), (2, 3)) for k in range(CONV_K) for i in pair]
            tap_at = [0]

            def conv(n):
                for k, i in tap_list[tap_at[0]:tap_at[0] + n]:
                    at = tap_at[0]
                    tap_at[0] += 1
                    src = apad[:, i, k:k + SEQ]
                    w = taps[:, i, k:k + 1]
                    if k == 0:
                        dve.wait_ge(glu_ready, i + 1)
                        ins = V.tensor_scalar(conv_y[:, i, :], src, w, params[:, 32 + i:33 + i], ALU.mult, ALU.add)
                    else:
                        dve.wait_ge(tap_done, at - 1)
                        ins = V.scalar_tensor_tensor(out=conv_y[:, i, :], in0=src, scalar=w, in1=conv_y[:, i, :],
                                                     op0=ALU.mult, op1=ALU.add)
                    ins.then_inc(tap_done, 1)

            for m in WITH_A[0:3]:
                fin(*m)
            for i in range(4):
                dve.wait_ge(ag_ready, i + 1)
                a_in = apad[:, i, PAD:PAD + SEQ]
                V.tensor_tensor(a_in, a_in, qT[:, i % 2, :], ALU.mult).then_inc(glu_ready, 1)
                fin(*([WITH_A[3]] + WITH_AG)[i])
                if i:
                    conv(8)

            for t in range(TT):
                fin(*([WITH_AG[3]] + WITH_Q)[t])
                dve.wait_ge(q_ready, t + 1)
                head_norm(qtok[:, t, :], qtmp[:, 0:512], 1, HEADS, 0, 1, q_ssq, q_rstd, t + 1)
                rope(qtok[:, t, :], qtmp[:, 0:512], t, HEADS, q_roped)
                if t < TT - 1:
                    conv(7)
            fin(*WITH_Q[3])

            def row_max(n):
                dve.wait_ge(scores_done, n + 1)
                link(V.tensor_reduce(softm[:, 2, n % 2:n % 2 + 1], score_ps[n % 2][:, 0:KT * P], AX_X, ALU.max))
                V.tensor_scalar(softm[:, 0, n % 2:n % 2 + 1], softm[:, 2, n % 2:n % 2 + 1], -HD ** -0.5, None,
                                ALU.mult).then_inc(max_ready, 1)

            row_max(0)
            for s in range(8):
                for u in range(4):
                    n = 4 * s + u
                    dve.wait_ge(exp_ready, n + 1)
                    link(V.reciprocal(softm[:, 3, n % 2:n % 2 + 1], softm[:, 1, n % 2:n % 2 + 1]))
                    V.tensor_scalar(prob[:, n % 2, :], prob[:, n % 2, :], softm[:, 3, n % 2:n % 2 + 1], None,
                                    ALU.mult).then_inc(prob_ready, 1)
                    if n + 1 < 32:
                        row_max(n + 1)
                    conv(3 if u < 3 else 2)
            conv(len(tap_list) - tap_at[0])

            dve.wait_ge(tap_done, len(tap_list))
            acc_wait(("mu",))
            for i in range(4):
                V.scalar_tensor_tensor(out=conv_y[:, i, :], in0=bank(("mu",))[:, :], scalar=-1.0 / CONV_C,
                                       in1=conv_y[:, i, :], op0=ALU.mult, op1=ALU.add).then_inc(centred, 1)
            bank_read[("mu",)] = (centred, 4)
            for i in range(4):
                dve.wait_ge(centred, i + 1)
                V.tensor_tensor(apad[:, i, 0:SEQ], conv_y[:, i, :], conv_y[:, i, :], ALU.mult).then_inc(sq_ready, 1)
            for m in GATES[0][0:2]:
                fin(*m)
            acc_wait(("var",))
            diag = gc_sb[0].rearrange("p (t q) -> p t q", t=TT)
            ident_t = ident.unsqueeze(1).to_broadcast([P, TT, P])
            link(V.tensor_tensor(diag, bank(("var",))[:, :].rearrange("p (t q) -> p t q", t=TT), ident_t, ALU.mult))
            bank_read[("var",)] = (dve_step, steps[0])
            V.tensor_reduce(ln_col[:, 0, :], diag, AX_X, ALU.add).then_inc(var_ready, 1)
            for m in GATES[0][2:3]:
                fin(*m)
            dve.wait_ge(ln_rstd, 1)
            V.tensor_tensor(diag, ident_t, ln_col[:, 1, :].unsqueeze(2).to_broadcast([P, TT, P]), ALU.mult).then_inc(diag_ready, 1)
            for m in GATES[0][3:4]:
                fin(*m)
            acc_wait(("ln_rstd",))
            for i in range(4):
                V.tensor_tensor(conv_y[:, i, :], conv_y[:, i, :], bank(("ln_rstd",))[:, :], ALU.mult).then_inc(ln_done, 1)
            bank_read[("ln_rstd",)] = (ln_done, 4)

            def mixer_out(l):
                for h in range(2):
                    for t in range(TT):
                        g = ("out", l, h, t)
                        tmp = prob[:, 0, 0:512] if t % 2 else prob[:, 1, 0:512]
                        acc_wait(g)
                        link(V.tensor_tensor(tmp, bank(g)[:, :], gate_mix[:, h * 512:(h + 1) * 512], ALU.mult))
                        bank_read[g] = (dve_step, steps[0])
                        xh = xs[:, t, h * 512:(h + 1) * 512]
                        V.tensor_tensor(xh, xh, tmp, ALU.add).then_inc(x_new[l], 1)
                        if l == 0 and h == 1 and t >= 1:
                            normalise("ffn0", xs, [t - 1])
                normalise(f"ffn{l}", xs, [TT - 1] if l == 0 else range(TT))

            def route(l):
                key = const("expert_key").unsqueeze(1).to_broadcast([P, TT, NE])
                gkey = const("group_key").unsqueeze(1).to_broadcast([P, TT, NG])

                def b16(v):
                    return v.to_broadcast([P, TT, NE])

                dve.wait_ge(aff_ready[l], 1)
                link(V.tensor_tensor(sel, aff, bias_r[:, :].unsqueeze(1).to_broadcast([P, TT, NE]), ALU.add))
                s4 = sel.rearrange("p t (g k) -> p t g k", g=NG)
                e = [s4[:, :, :, k] for k in range(EPG)]
                V.tensor_tensor(g_a, e[0], e[1], ALU.max)
                V.tensor_tensor(g_b, e[0], e[1], ALU.min)
                V.tensor_tensor(g_c, e[2], e[3], ALU.max)
                link(V.tensor_tensor(g_d, e[2], e[3], ALU.min))
                link(V.tensor_tensor(g_b, g_b, g_d, ALU.max))
                link(V.tensor_tensor(g_d, g_a, g_c, ALU.min))
                link(V.tensor_tensor(g_b, g_b, g_d, ALU.max))
                link(V.tensor_tensor(g_a, g_a, g_c, ALU.max))
                link(V.tensor_tensor(g_a, g_a, g_b, ALU.add))
                link(V.tensor_reduce(r4, g_a, AX_X, ALU.max))
                link(V.tensor_tensor(g_b, g_a, r4.to_broadcast([P, TT, NG]), ALU.is_equal))
                link(V.tensor_tensor(g_b, g_b, gkey, ALU.mult))
                link(V.tensor_reduce(r4, g_b, AX_X, ALU.max))
                link(V.tensor_tensor(g_b, g_b, r4.to_broadcast([P, TT, NG]), ALU.is_equal))
                link(V.tensor_scalar(g_c, g_b, 1e30, -1e30, ALU.mult, ALU.add))
                m4 = selm.rearrange("p t (g k) -> p t g k", g=NG)
                link(V.tensor_tensor(m4, s4, g_b.unsqueeze(3).to_broadcast([P, TT, NG, EPG]), ALU.mult))
                link(V.tensor_tensor(m4, m4, g_c.unsqueeze(3).to_broadcast([P, TT, NG, EPG]), ALU.add))
                for n, oh in enumerate((oh1, oh2)):
                    link(V.tensor_reduce(r4, selm, AX_X, ALU.max))
                    link(V.tensor_tensor(r16, selm, b16(r4), ALU.is_equal))
                    link(V.tensor_tensor(r16, r16, key, ALU.mult))
                    link(V.tensor_reduce(r4, r16, AX_X, ALU.max))
                    link(V.tensor_tensor(oh, r16, b16(r4), ALU.is_equal))
                    if n == 0:
                        link(V.scalar_tensor_tensor(out=selm, in0=oh, scalar=-3e38, in1=selm, op0=ALU.mult, op1=ALU.add))
                V.tensor_tensor(picked, oh1, oh2, ALU.add).then_inc(mask_ready[l], 1)
                for n, oh in enumerate((oh1, oh2)):
                    link(V.tensor_tensor(r16, oh, aff, ALU.mult))
                    link(V.tensor_reduce(w2[:, :, n:n + 1], r16, AX_X, ALU.add))
                link(V.tensor_tensor(w_sum, w2[:, :, 0:1], w2[:, :, 1:2], ALU.add))
                link(V.reciprocal(w_sum, w_sum))
                link(V.tensor_tensor(w2, w2, w_sum.to_broadcast([P, TT, 2]), ALU.mult))
                g = ("route", l, 2)
                acc_wait(g)
                V.tensor_copy(before16, bank(g)[:, 0:TT * NE].rearrange("p (t e) -> p t e", e=NE))
                link(V.tensor_copy(total16, bank(g)[:, TT * NE:2 * TT * NE].rearrange("p (t e) -> p t e", e=NE)))
                bank_read[g] = (dve_step, steps[0])
                for t in range(1, TT):
                    link(V.tensor_tensor(before16[:, t, :], before16[:, t, :], total16[:, t - 1, :], ALU.add))
                    link(V.tensor_tensor(total16[:, t, :], total16[:, t, :], total16[:, t - 1, :], ALU.add))
                fb = const("full_blocks")
                link(V.tensor_tensor(cmp16, total16[:, TT - 1, :].unsqueeze(2).to_broadcast([P, NE, SEQ // BLK - 1]),
                                     fb.unsqueeze(1).to_broadcast([P, NE, SEQ // BLK - 1]), ALU.is_gt))
                link(V.tensor_reduce(nblk16, cmp16, AX_X, ALU.add))
                link(V.tensor_scalar(nblk16, nblk16, 1.0, None, ALU.add))
                link(V.tensor_tensor(start_cmp, nblk16.unsqueeze(1).to_broadcast([P, NE + 1, NE]),
                                     const("expert_before").rearrange("p (a b) -> p a b", b=NE), ALU.mult))
                link(V.tensor_reduce(start_f, start_cmp, AX_X, ALU.add))
                link(V.tensor_copy(block_start[:, :], start_f))
                for n, oh in enumerate((oh1, oh2)):
                    link(V.tensor_tensor(r16, oh, before16, ALU.mult))
                    link(V.tensor_reduce(pos2[:, :, n:n + 1], r16, AX_X, ALU.add))
                    link(V.tensor_tensor(r16, oh, start_f[:, 0:NE].unsqueeze(1).to_broadcast([P, TT, NE]), ALU.mult))
                    link(V.tensor_reduce(st2[:, :, n:n + 1], r16, AX_X, ALU.add))
                flat = lambda v: v.rearrange("p a b -> p (a b)")
                link(V.tensor_tensor(cmp2, flat(pos2).unsqueeze(2).to_broadcast([P, 2 * TT, SEQ // BLK - 1]),
                                     fb.unsqueeze(1).to_broadcast([P, 2 * TT, SEQ // BLK - 1]), ALU.is_ge))
                link(V.tensor_reduce(flat(full2), cmp2, AX_X, ALU.add))
                link(V.tensor_tensor(blk2, st2, full2, ALU.add))
                link(V.scalar_tensor_tensor(out=slot2, in0=full2, scalar=-float(BLK), in1=pos2, op0=ALU.mult, op1=ALU.add))
                V.tensor_tensor(oh_slot, flat(slot2).unsqueeze(2).to_broadcast([P, 2 * TT, P]),
                                const("slot_of_col").unsqueeze(1).to_broadcast([P, 2 * TT, P]), ALU.is_equal)
                link(V.tensor_tensor(oh_blk, flat(blk2).unsqueeze(2).to_broadcast([P, 2 * TT, NB]),
                                     const("block_id").unsqueeze(1).to_broadcast([P, 2 * TT, NB]), ALU.is_equal))
                for n, v in enumerate((const("token"), const("out_row"), flat(w2))):
                    V.tensor_tensor(val_blk[:, :, n, :], oh_blk, v.unsqueeze(2).to_broadcast([P, 2 * TT, NB]),
                                    ALU.mult).then_inc(table_in[l], 1)
                g = ("route", l, 3)
                acc_wait(g)
                tab = bank(g)[:, 0:3 * NB].rearrange("p (v b) -> p v b", v=3)
                V.tensor_scalar(rowid[:, 0, :], tab[:, 0, :], 2.0, const("half"), ALU.mult, ALU.add)
                V.tensor_scalar(rowid[:, 1, :], tab[:, 1, :], float(NIDX), 2.0, ALU.add, ALU.mult)
                link(V.tensor_copy(rowid[:, 2, :], tab[:, 2, :]))
                bank_read[g] = (dve_step, steps[0])
                link(V.tensor_scalar(rowid[:, 1, :], rowid[:, 1, :], const("half"), None, ALU.add))
                link(V.tensor_copy(row_i[:, 0, :], rowid[:, 0, :]))
                V.tensor_copy(row_i[:, 1, :], rowid[:, 1, :]).then_inc(route_ready[l], 1)

            def ffn(l):
                norm = f"ffn{l}"
                modulate(norm, hT_cat, SEQ, lambda j: mod_a[:, 1 + 2 * l, j:j + 1], shift_of(l, 3, 0))
                if l == 0:
                    dve.wait_ge(router_in, 32)
                route(l)

                def turn_in():
                    for j in (0, 1, 4, 5):
                        at = j % 4 * P + (j // 4) * BLK
                        V.tensor_scalar(hgT[:, j, :], hg_dve_ps[:, at:at + BLK], mod_a[:, 1 + 2 * l, j:j + 1],
                                        shift_of(l, 3, 0)(j), ALU.mult, ALU.add).then_inc(hgT_dve[l], 1)

                dve.wait_ge(route_ready[l], 1)
                total = dve.value_load(block_start[0:1, NE:NE + 1], min_val=NE, max_val=MAXB)
                dve.wait_ge(hg_turned[l], 1)
                turn_in()
                with dve.Fori(0, total) as b:
                    dve.wait_ge(silu_ready[l], b + 1)
                    dve.wait_ge(up_done[l], b + 1)
                    V.tensor_tensor(act_sb, silu_g, up_ps[:, 0:256], ALU.mult).then_inc(act_ready[l], 1)
                    dve.wait_ge(act_turned[l], b + 1)
                    V.tensor_copy(actT, at_ps[:, 0:256].rearrange("p (j s) -> p j s", j=2)).then_inc(actT_ready[l], 1)
                    dve.wait_ge(hg_turned[l], b + 2)
                    turn_in()
                    dve.wait_ge(down_done[l], b + 1)
                    dve.wait_ge(y_moved[l], b + 1)
                    V.scalar_tensor_tensor(out=y_blk, in0=y_ps, scalar=rowid[:, 2, bass.ds(b, 1)], in1=gate_ffn[:, :],
                                           op0=ALU.mult, op1=ALU.mult).then_inc(y_read[l], 1)
                for t in range(TT):
                    i = t % 2
                    dve.wait_ge(yin[l][i], 32 * (t // 2 + 1))
                    link(V.tensor_tensor(xs[:, t, :], xs[:, t, :], y_in[i][:, 0, :], ALU.add))
                    V.tensor_tensor(xs[:, t, :], xs[:, t, :], y_in[i][:, 1, :], ALU.add).then_inc(y_added[l], 1)

            dve.wait_ge(gates_ready, 4)
            mixer_out(0)
            ffn(0)

            normalise("mix1", xs, range(TT))
            modulate("mix1", hT_cat, SEQ, lambda j: mod_a[:, 2, j:j + 1], shift_of(1, 0, 0))
            for u in u_pad:
                V.memset(u[:, 0:1], 0.0)
                link(V.memset(u[:, SEQ + 1:SEQ + 2], 0.0))
            for h in range(2):
                for i in range(4):
                    m = 4 * h + i
                    up, y = u_pad[m % 2], sc_y[m % 2]
                    dve.wait_ge(gc_ready, m + 1)
                    acc_wait(("v", m))
                    V.tensor_tensor(up[:, 1:SEQ + 1], gc_sb[m % 2], bank(("v", m))[:, :], ALU.mult).then_inc(u_ready, 1)
                    bank_read[("v", m)] = (u_ready, m + 1)
                    dve.wait_ge(u_ready, m + 1)
                    link(V.tensor_scalar(y, up[:, 0:SEQ], taps[:, m, 31:32], None, ALU.mult))
                    for k in range(1, SC_K):
                        link(V.scalar_tensor_tensor(out=y, in0=up[:, k:k + SEQ], scalar=taps[:, m, 31 + k:32 + k], in1=y,
                                                    op0=ALU.mult, op1=ALU.add))
                    acc_wait(("gb", m))
                    V.tensor_tensor(mT[:, m, :], y, bank(("gb", m))[:, :], ALU.mult).then_inc(mT_ready, 1)
                    bank_read[("gb", m)] = (mT_ready, m + 1)
                for m_ in GATES[1][2 * h:2 * h + 2]:
                    fin(*m_)
            dve.wait_ge(gates_ready, 8)
            mixer_out(1)
            ffn(1)

        @block.gpsimd
        def _(pool):
            G = nc.gpsimd
            pool.wait_ge(zeroed, 1)
            pool.wait_ge(consts_in, 16)
            half = const("minus_half")
            steps = [0]

            def passed(l, n):
                pool.wait_ge(ticked[l], n)
                G.tensor_tensor(tick[:, :], half, half, ALU.add).then_inc(ticked[l], 1)

            def link(ins):
                steps[0] += 1
                ins.then_inc(pool_step, 1)
                pool.wait_ge(pool_step, steps[0])

            def rsqrt(dst, src, n, scale):
                link(G.tensor_scalar(dst, src, scale, EPS, ALU.mult, ALU.add))
                return G.tensor_tensor(dst, dst, half.to_broadcast([P, n]), ALU.pow)

            def norm_rstd(norm, tiles):
                row, first = (2, TT) if norm == "ctx" else (1, 0)
                for t in range(tiles):
                    pool.wait_ge(ssq_ready[norm], t + 1)
                    rsqrt(stats[:, row, t:t + 1], stats[:, 0, first + t:first + t + 1], 1, 1.0 / D).then_inc(rstd_ready[norm], 1)

            norm_rstd("mix0", TT)
            norm_rstd("ctx", CT)
            pool.wait_ge(k_ssq, 1)
            rsqrt(head_stats[:, 0, 0:KT * KVH], head_stats[:, 0, 0:KT * KVH], KT * KVH, 1.0 / HD).then_inc(k_rstd, 1)
            for t in range(TT):
                pool.wait_ge(q_ssq, t + 1)
                rsqrt(head_stats[:, 1, 0:HEADS], head_stats[:, 1, 0:HEADS], HEADS, 1.0 / HD).then_inc(q_rstd, 1)
            pool.wait_ge(var_ready, 1)
            rsqrt(ln_col[:, 1, :], ln_col[:, 0, :], TT, 1.0 / CONV_C).then_inc(ln_rstd, 1)

            def ffn(l):
                norm_rstd(f"ffn{l}", TT)
                pool.wait_ge(route_ready[l], 1)
                total = pool.value_load(block_start[0:1, NE:NE + 1], min_val=NE, max_val=MAXB)
                pool.wait_ge(xhat_stored[l], 16 * TT)

                def gather(b, count):
                    G.tensor_copy(cur_idx[:, 0, :], row_i[:, 0, bass.ds(b, 1)]).then_inc(idx_ready[l], 1)
                    pool.wait_ge(idx_ready[l], count)
                    passed(l, count)
                    G.indirect_dma_start(out=hg_raw, out_offset=None, in_=xhat_d,
                                         in_offset=bass.IndirectOffsetOnAxis(ap=cur_idx[:, 0, :], axis=0),
                                         bounds_check=2 * SEQ - 1, oob_is_err=False).then_inc(hg_in[l], 16)

                def scatter(b, count, moved):
                    G.tensor_tensor(y_out, y_blk, const("ones")[:, 0:1].to_broadcast([P, 512]), ALU.mult).then_inc(y_moved[l], 1)
                    G.tensor_copy(cur_idx[:, 1, :], row_i[:, 1, bass.ds(b, 1)]).then_inc(idx_ready[l], 1)
                    pool.wait_ge(idx_ready[l], count)
                    pool.wait_ge(y_moved[l], moved)
                    passed(l, count)
                    G.indirect_dma_start(out=y_d[l], out_offset=bass.IndirectOffsetOnAxis(ap=cur_idx[:, 1, :], axis=0),
                                         in_=y_out, in_offset=None, bounds_check=4 * SEQ - 1,
                                         oob_is_err=False).then_inc(y_stored[l], 16)

                gather(0, 1)
                scatter(NB - 1, 2, 1)
                for n in range(1, 3):
                    pool.wait_ge(hg_moved[l], n)
                    gather(n, 2 + n)
                with pool.Fori(0, total) as b:
                    pool.wait_ge(hg_moved[l], b + 3)
                    gather(b + 3, b * 2 + 5)
                    pool.wait_ge(y_read[l], b + 2)
                    pool.wait_ge(y_stored[l], b * 16 + 16)
                    scatter(b, b * 2 + 6, b + 2)
                pool.wait_ge(hg_in[l], total * 16 + 48)
                passed(l, total * 2 + 5)

            ffn(0)
            norm_rstd("mix1", TT)
            ffn(1)

        @block.tensor
        def _(pe):
            T = nc.tensor
            at = [0]

            def open_group(name):
                n = at[0]
                assert GROUPS[n] == name, (GROUPS[n], name)
                at[0] += 1
                if n >= NBANK:
                    pe.wait_ge(*bank_read[GROUPS[n - NBANK]])
                return psum[n % NBANK]

            def unit_wait(name):
                pe.wait_ge(unit_in[unit_slot[name]], unit_count[name])
                return unit(name)

            def close(mm):
                mm.then_inc(acc_done, 1)

            pe.wait_ge(consts_in, 16)
            pe.wait_ge(zeroed, 1)
            pe.wait_ge(rows_in, 16 * 7)
            ps = open_group(("params",))
            close(T.transpose(ps[:, 0:44], staging[0:44, 0:P], ident[0:44, 0:44]))
            ps = open_group(("taps",))
            for j in range(KD):
                mm = T.transpose(ps[:, j * 34:(j + 1) * 34], hT_cat[0:34, j // 4, (j % 4) * P:(j % 4 + 1) * P], ident[0:34, 0:34])
            close(mm)

            ps = open_group(("bias",))
            pe.wait_ge(bmod_in, 16)
            for j in range(4):
                mm = T.transpose(ps[:, j * 24:(j + 1) * 24], b_rows[0:24, j * P:(j + 1) * P], ident[0:24, 0:24])
            close(mm)

            mods = [0]

            def mod_rows(l, c):
                ps = open_group(("mod", l, c))
                w = unit_wait(("mod", l, c))
                if not mods[0]:
                    pe.wait_ge(cact_ready, 2)
                for k in range(KD):
                    q = k % 4
                    mm = T.matmul(ps[32 * q:32 * q + 32, :], cact[:, k, :], w[:, k, :], start=(k < 4), stop=(k >= 4))
                close(mm)

            def mod_fin(l, c):
                mods[0] += 1
                ps = open_group(("fin", l, c))
                pe.wait_ge(modrow_ready, mods[0])
                bias_row = ident[:, 12 * l + c:12 * l + c + 1]
                if c in (4, 5):
                    T.matmul(ps[:, :], const("sel_x"), modrow[:, :], start=True, stop=False)
                    mm = T.matmul(ps[:, :], bias_row.to_broadcast([P, P]), b_rows[:, :], start=False, stop=True)
                elif c in (10, 11):
                    h = c - 10
                    T.matmul(ps[h * 64:(h + 1) * 64, :], const("sel_x")[:, 0:64], modrow[:, :], start=True, stop=False)
                    mm = T.matmul(ps[h * 64:(h + 1) * 64, :], bias_row.to_broadcast([P, 64]), b_rows[:, :], start=False, stop=True)
                else:
                    for j in range(4):
                        mm = T.matmul(ps[:, 2 * j:2 * j + 2], modrow[:, j * P:(j + 1) * P], const("sel_both"), start=True, stop=True)
                close(mm)

            def norm_turn(norm, src, tiles):
                pe.wait_ge(xhat_ready[norm], tiles)
                for j in range(KD):
                    ps = open_group(("norm", norm, j))
                    for t in range(tiles):
                        mm = T.transpose(ps[:, t * P:(t + 1) * P], src[:, t, j * P:(j + 1) * P], ident)
                    close(mm)

            for c_ in range(4):
                mod_rows(0, c_)
                mod_fin(0, c_)
            norm_turn("ctx", ctx_hat, CT)
            norm_turn("mix0", xhat, TT)
            def hT_wait(norm):
                pe.wait_ge(hT_even[norm], KD // 2)
                pe.wait_ge(hT_odd[norm], KD // 2)


            def tokens_out(name, lhs, t, w, n):
                ps = open_group(name)
                for k in range(KD):
                    mm = T.matmul(ps[:, 0:n], lhs[:, k, t * P:(t + 1) * P], w[:, k, 0:n], start=(k == 0), stop=(k == KD - 1))
                close(mm)

            def channels_out(name, i, w):
                ps = open_group(name)
                for k in range(KD):
                    mm = T.matmul(ps[:, :], w[:, k, i * P:(i + 1) * P], hT_cat[:, k, :], start=(k == 0), stop=(k == KD - 1))
                close(mm)

            w = unit_wait(("kv",))
            hT_wait("ctx")
            for t in range(CT):
                tokens_out(("kvz", t), hzT, t, w, 256)
            hT_wait("mix0")
            for t in range(TT):
                tokens_out(("kvx", t), hT_cat, t, w, 256)
            w = unit_wait(("a",))
            for i in range(4):
                channels_out(("a", i), i, w)
                if i:
                    mod_fin(*WITH_A[i - 1])
                mod_rows(*WITH_A[i])
            w = unit_wait(("ag",))
            for i in range(4):
                channels_out(("ag", i), i, w)
                mod_fin(*([WITH_A[3]] + WITH_AG)[i])
                mod_rows(*WITH_AG[i])
            for v in range(KVH):
                for h in range(2):
                    ps = open_group(("kT", v, h))
                    pe.wait_ge(k_roped, TT)
                    for t in range(3):
                        for half in range(2):
                            mm = T.matmul(ps[half * 64:(half + 1) * 64, t * P:(t + 1) * P], ktok[:, 3 * h + t, v * HD:(v + 1) * HD],
                                          ident, start=True, stop=True)
                    close(mm)
            w = unit_wait(("q",))
            for t in range(TT):
                tokens_out(("q", t), hT_cat, t, w, 512)
                mod_fin(*([WITH_AG[3]] + WITH_Q)[t])
                mod_rows(*WITH_Q[t])
            mod_fin(*WITH_Q[3])
            for i in range(PAIRS):
                ps = open_group(("qT", i))
                pe.wait_ge(q_roped, TT)
                for t in range(TT):
                    mm = T.transpose(ps[:, t * P:(t + 1) * P], qtok[:, t, i * P:(i + 1) * P], ident)
                close(mm)

            def scores(n):
                s, u = n // 4, n % 4
                pair, qt = s // 2, (s % 2) * 2 + u % 2
                r = slice((u // 2) * 64, (u // 2) * 64 + 64)
                pe.wait_ge(qT_ready, pair + 1)
                if n >= 2:
                    pe.wait_ge(exp_ready, n - 1)
                for a, b in ((0, 512), (512, KT * P)):
                    mm = T.matmul(score_ps[n % 2][:, a:b], qT[r, pair, qt * P:(qt + 1) * P], kT2[r, pair // 2, a:b],
                                  start=True, stop=True)
                mm.then_inc(scores_done, 1)

            pe.wait_ge(kT_ready, 2 * KVH)
            scores(0)
            for s in range(8):
                for u in range(4):
                    n = 4 * s + u
                    if n + 1 < 32:
                        scores(n + 1)
                    pe.wait_ge(prob_ready, n + 1)
                    for g3 in range(2):
                        ps = open_group(("PT", s, u, g3))
                        for k in range(3):
                            mm = T.transpose(ps[:, k * P:(k + 1) * P], prob[:, n % 2, (3 * g3 + k) * P:(3 * g3 + k + 1) * P], ident)
                        close(mm)
                ps = open_group(("pv", s))
                pe.wait_ge(PT_ready, 8 * s + 8)
                kvh = s // 4
                for k in range(KT):
                    for hh in range(2):
                        mm = T.matmul(ps[hh * 64:(hh + 1) * 64, 0:256], vtok[:, k, kvh * HD:(kvh + 1) * HD], PT[s % 2][hh][:, k, :],
                                      start=(k == 0), stop=(k == KT - 1))
                close(mm)

            def channel_sums(name, src, sem_, value):
                ps = open_group(name)
                pe.wait_ge(sem_, value)
                for i in range(4):
                    mm = T.matmul(ps[:, :], const("ones"), src[:, i, :], start=(i == 0), stop=(i == 3))
                close(mm)

            channel_sums(("mu",), conv_y, tap_done, 4 * CONV_K)
            for n, m in enumerate(GATES[0]):
                mod_rows(*m)
                mod_fin(*m)
                if n == 1:
                    channel_sums(("var",), apad[:, :, 0:SEQ], sq_ready, 4)
            ps = open_group(("ln_rstd",))
            pe.wait_ge(diag_ready, 1)
            close(T.matmul(ps[:, :], const("ones"), gc_sb[0], start=True, stop=True))

            def mixer_out(l, lhs, unit_name):
                for h in range(2):
                    w = unit_wait((unit_name, h))
                    for t in range(TT):
                        ps = open_group(("out", l, h, t))
                        for k in range(KD):
                            mm = T.matmul(ps[:, :], lhs[:, k, t * P:(t + 1) * P], w[:, k, :], start=(k == 0), stop=(k == KD - 1))
                        close(mm)

            def ffn(l):
                norm_turn(f"ffn{l}", xhat, TT)
                ps = open_group(("route", l, 0))
                hT_wait(f"ffn{l}")
                if l == 0:
                    pe.wait_ge(router_in, 32)
                for k in range(KD):
                    q = k % 4
                    mm = T.matmul(ps[32 * q:32 * q + 32, :], route_w[:, k, :], hT_cat[:, k, :], start=(k < 4), stop=(k >= 4))
                close(mm)
                ps = open_group(("route", l, 1))
                pe.wait_ge(router_turned[l], 1)
                for t in range(TT):
                    mm = T.matmul(ps[:, t * NE:(t + 1) * NE], router_rows[:, t * P:(t + 1) * P], const("sel_expert"),
                                  start=True, stop=True)
                close(mm)
                ps = open_group(("route", l, 2))
                pe.wait_ge(mask_ready[l], 1)
                rows = picked.rearrange("p t e -> p (t e)")
                T.matmul(ps[:, 0:TT * NE], const("before"), rows, start=True, stop=True)
                close(T.matmul(ps[:, TT * NE:2 * TT * NE], const("ones"), rows, start=True, stop=True))
                ps = open_group(("route", l, 3))
                pe.wait_ge(table_in[l], 3)
                for n in range(2 * TT):
                    mm = T.matmul(ps[:, 0:3 * NB], oh_slot[:, n, :], val_blk[:, n, :, :].rearrange("p v b -> p (v b)"),
                                  start=(n == 0), stop=(n == 2 * TT - 1))
                close(mm)

                pe.wait_ge(route_ready[l], 1)

                def turn(count):
                    pe.wait_ge(hg_moved[l], count)
                    for j in range(4):
                        mm = T.transpose((hg_dve_ps, hg_act_ps)[j // 2][:, j % 2 * P:(j % 2 + 1) * P], hg_next[:, j * P:(j + 1) * P], ident)
                    mm.then_inc(hg_turned[l], 1)

                turn(1)

                def block_of(b, i, par):
                    def landed(k):
                        slot = 3 * par + k
                        pe.wait_ge(unit_in[slot], i * 16 + (moe_base[l][slot] + 1) * 16)
                        return expert_view(slot, "wd" if k == 2 else "wg")

                    pe.wait_ge(hgT_dve[l], b * 4 + 4)
                    pe.wait_ge(hgT_act[l], b * 4 + 4)
                    for n, ps, done in ((0, gate_ps, gate_done[l]), (1, up_ps, up_done[l])):
                        w = landed(n)
                        for k in range(KD):
                            for h in range(2):
                                mm = T.matmul(ps[h * BLK:(h + 1) * BLK, 0:256], hgT[:, k, :], w[:, k, h * 256:(h + 1) * 256],
                                              start=(k == 0), stop=(k == KD - 1))
                        mm.then_inc(done, 1)
                    pe.wait_ge(act_ready[l], b + 1)
                    for j in range(2):
                        mm = T.transpose(at_ps[:, j * P:(j + 1) * P], act_sb[:, j * P:(j + 1) * P], ident)
                    mm.then_inc(act_turned[l], 1)
                    turn(b + 2)
                    pe.wait_ge(actT_ready[l], b + 1)
                    pe.wait_ge(y_read[l], b + 1)
                    wd = landed(2)
                    for k in range(4):
                        for h in range(2):
                            mm = T.matmul(y_ps[h * BLK:(h + 1) * BLK, :], actT[:, k % 2, (k // 2) * BLK:(k // 2 + 1) * BLK],
                                          wd[:, k, h * 512:(h + 1) * 512], start=(k == 0), stop=(k == 3))
                    mm.then_inc(down_done[l], 1)

                with pe.Fori(0, NE // 2) as i:
                    for par in range(2):
                        first = pe.value_load(block_start[0:1, bass.ds(i * 2 + par, 1)], min_val=0, max_val=MAXB)
                        end = pe.value_load(block_start[0:1, bass.ds(i * 2 + par + 1, 1)], min_val=1, max_val=MAXB)
                        with pe.Fori(first, end) as b:
                            block_of(b, i, par)
                total = pe.value_load(block_start[0:1, NE:NE + 1], min_val=NE, max_val=MAXB)
                pe.wait_ge(y_read[l], total + 1)
                pe.wait_ge(hgT_dve[l], total * 4 + 4)
                pe.wait_ge(hgT_act[l], total * 4 + 4)

            pe.wait_ge(attn_ready, 8)
            pe.wait_ge(cat_ready, 4)
            mixer_out(0, hT_cat, "wo")
            ffn(0)

            norm_turn("mix1", xhat, TT)
            hT_wait("mix1")
            for h in range(2):
                w = {n: unit_wait((n, h)) for n in ("gc", "v", "gb")}
                for i in range(4):
                    for n in ("gc", "v", "gb"):
                        ps = open_group((n, 4 * h + i))
                        for k in range(KD):
                            mm = T.matmul(ps[:, :], w[n][:, k, i * P:(i + 1) * P], hT_cat[:, k, :], start=(k == 0), stop=(k == KD - 1))
                        close(mm)
                for m in GATES[1][2 * h:2 * h + 2]:
                    mod_rows(*m)
                    mod_fin(*m)
            pe.wait_ge(mT_ready, KD)
            mixer_out(1, mT, "ow")
            ffn(1)
            assert at[0] == len(GROUPS)


_INS = ["x", "c", "ctx", "c_ctx", "w_mod", "b_mod", "norm_mix_g", "norm_ffn_g", "ev_w_in", "ev_q_norm_g", "ev_k_norm_g",
        "ev_dw_w", "ev_dw_b", "ev_ln_g", "ev_ln_b", "ev_w_out", "od_w_in", "od_conv_w", "od_w_out", "router_w",
        "router_bias", "moe_w_gate", "moe_w_up", "moe_w_down"]


def kernel(**inputs):
    import concourse.bacc as bacc
    from concourse.bass_utils import run_bass_kernel_spmd

    nc = bacc.Bacc("TRN2", target_bir_lowering=False, num_devices=1)
    arrays, args = {}, []
    values = {name: np.ascontiguousarray(inputs[name]) for name in _INS}
    values["consts"] = build_consts()
    for name, a in values.items():
        arrays[f"in_{name}"] = a
        args.append(nc.dram_tensor(f"in_{name}", a.shape, mybir.dt.from_np(a.dtype), kind="ExternalInput").ap())
    out = nc.dram_tensor("out_x", (1, SEQ, D), F32, kind="ExternalOutput").ap()
    hybrid_backbone_kernel(nc, *args, out)
    r = run_bass_kernel_spmd(nc, [arrays], core_ids=[0])
    return r.results[0]["out_x"]
```

```python
from contextlib import ExitStack

import numpy as np

import concourse.bass as bass
from concourse import mybir

F32 = mybir.dt.float32
I32 = mybir.dt.int32
ALU = mybir.AluOpType
ACT = mybir.ActivationFunctionType
AX_X = mybir.AxisListType.X

P = 128
D = 1024
KD = D // P
SEQ = 512
TT = SEQ // P
CTX = 256
CT = CTX // P
KT = TT + CT
HEADS, KVH, HD = 8, 2, 64
PAIRS = HEADS // 2
GRID_W = 64
CONV_K, CONV_C = 31, 512
PAD = CONV_K // 2
APAD = SEQ + 2 * PAD
SC_K = 3
NE, NG, EPG = 16, 4, 4
BLK = 64
MAXB = SEQ * 2 // BLK + NE
NB = MAXB + 3
NIDX = 4096
EPS = 1e-6
RING = 6
NBANK = 4

WITH_A = [(0, 6), (0, 7), (0, 8), (0, 9)]
WITH_AG = [(1, 0), (1, 1), (1, 2), (1, 3)]
WITH_Q = [(1, 6), (1, 7), (1, 8), (1, 9)]
LN_AT = {"mu": (6, 0), "var": (7, 0), "ln_rstd": (7, 3)}
GATE_AT = {(2, 1): ("mod", 0, 4), (2, 3): ("fin", 0, 4), (3, 1): ("mod", 0, 5), (3, 3): ("fin", 0, 5)}
GATES = [[(l, 4), (l, 5), (l, 10), (l, 11)] for l in range(2)]

CONSTS = {}


def build_consts():
    p = np.arange(P)
    parts = []

    def add(name, a):
        a = np.asarray(a, np.float32).reshape(P, -1)
        at = sum(x.shape[1] for x in parts)
        CONSTS[name] = (at, at + a.shape[1])
        parts.append(a)

    add("ident", np.eye(P))
    add("ones", np.ones((P, P)))
    add("before", p[:, None] < p[None, :])
    add("sel_both", np.stack([p % 32 == 0, p % 32 == 1], 1))
    add("sel_x", np.repeat((p % 32 == 0)[:, None], P, 1))
    add("sel_expert", p[:, None] % 32 == np.arange(NE)[None, :])
    add("slot_of_col", np.tile(p % BLK, (P, 1)))
    add("half", p // BLK)
    add("out_offset", p // BLK + 2 * NIDX)
    add("full_blocks", np.tile(np.arange(SEQ // BLK) * BLK - (np.arange(SEQ // BLK) == 0), (P, 1)))
    add("block_slots", np.tile(np.arange(NB + 1) * BLK, (P, 1)))
    add("group_key", np.tile(NG - np.arange(NG), (P, 1)))
    add("expert_key", np.tile(NE - np.arange(NE), (P, 1)))
    rank_at = [0, 1] + [r for k in range((NE - 2) // 2) for r in (NE - 1 - k, 2 + k)]
    add("rank_at", np.tile(rank_at, (P, 1)))
    tie = NE - 1 - np.arange(NE)
    tie[0:2] = NE * (MAXB + 1) * np.array([3, 2])
    add("rank_tie", np.tile(tie, (P, 1)))
    add("expert_id", np.tile(np.arange(NE), (P, 1)))
    add("expert_before", np.tile((np.arange(NE)[None, :] < np.arange(NE + 1)[:, None]).ravel(), (P, 1)))
    token = np.arange(TT)[None, :, None] * P + p[:, None, None] + np.zeros((1, 1, 2))
    token = token.transpose(0, 2, 1)
    add("token_row", 2 * token)
    add("out_row", 2 * (token + SEQ * np.arange(2)[None, :, None] - NIDX))
    add("minus_half", np.full((P, 1), -0.5))
    t = np.arange(SEQ)
    inv = (np.float32(10000.0) ** (-np.arange(HD // 4, dtype=np.float32) / np.float32(HD // 4))).astype(np.float32)
    ang = np.concatenate([(t // GRID_W).astype(np.float32)[:, None] * inv,
                          (t % GRID_W).astype(np.float32)[:, None] * inv], -1).astype(np.float32)
    for name, f in (("cos", np.cos), ("sin", np.sin)):
        add(name, f(ang.astype(np.float64)).reshape(TT, P, HD // 2).transpose(1, 0, 2))
    return np.ascontiguousarray(np.concatenate(parts, 1))


def plan_units():
    order = [("mod", 0, c) for c in range(4)] + [("kv",), ("a",)]
    order += [("mod",) + m for m in WITH_A] + [("ag",)] + [("mod",) + m for m in WITH_AG]
    order += [("q",)] + [("mod",) + m for m in WITH_Q] + [("mod",) + m for m in GATES[0][0:2]] + [("wo", 0), ("wo", 1)]
    order += [("mod",) + m for m in GATES[0][2:4]]
    return order


def plan_units_odd():
    return ([("mod", 1, 4), ("mod", 1, 5), ("gc", 0), ("v", 0), ("gb", 0), ("gc", 1), ("v", 1), ("gb", 1),
             ("ow", 0), ("ow", 1), ("mod", 1, 10), ("mod", 1, 11)])


def ffn_groups(l):
    a, b = GATES[l][2:4]
    return ([("norm", f"ffn{l}", j) for j in range(KD)] + [("route", l, 0), ("mod",) + a, ("route", l, 1), ("fin",) + a]
            + [("mod",) + b, ("fin",) + b, ("route", l, 2), ("route", l, 3)])


def plan_groups():
    g = [("params",), ("taps",), ("bias",)]
    for c in range(4):
        g += [("mod", 0, c), ("fin", 0, c)]
    g += [("norm", "ctx", j) for j in range(KD)] + [("norm", "mix0", j) for j in range(KD)]
    g += [("kvz", t) for t in range(CT)] + [("kvx", t) for t in range(TT)]
    last = None
    for w, units in (("a", WITH_A), ("ag", WITH_AG)):
        for i in range(4):
            g += [(w, i)] + ([("fin",) + last] if last else []) + [("mod",) + units[i]]
            last = units[i]
    g += [("kT", v, h) for v in range(KVH) for h in range(2)]
    g += [("q", 0), ("fin",) + last, ("q", 1), ("q", 2), ("q", 3)]
    for m in WITH_Q:
        g += [("mod",) + m, ("fin",) + m]
    g += [("qT", i) for i in range(PAIRS)]
    for s in range(8):
        for u in range(4):
            g += [("PT", s, u, 0), ("PT", s, u, 1)]
            if u == 0 and s:
                g += [("pv", s - 1)]
            g += [(name,) for name, at in LN_AT.items() if at == (s, u)]
            g += [GATE_AT[s, u]] if (s, u) in GATE_AT else []
    g += [("pv", 7)]
    g += [("out", 0, h, t) for h in range(2) for t in range(TT)]
    g += ffn_groups(0)
    for m in GATES[1][0:2]:
        g += [("mod",) + m, ("fin",) + m]
    g += [("norm", "mix1", j) for j in range(KD)]
    for m in range(KD):
        g += [(w, m) for w in ("gc", "v", "gb")]
    g += [("out", 1, h, t) for h in range(2) for t in range(TT)]
    g += ffn_groups(1)
    return g


GROUPS = plan_groups()
GROUP_AT = {name: n for n, name in enumerate(GROUPS)}
assert len(GROUP_AT) == len(GROUPS)


def hybrid_backbone_kernel(nc, x, c, ctx, c_ctx, w_mod, b_mod, norm_mix_g, norm_ffn_g, ev_w_in,
                           ev_q_norm_g, ev_k_norm_g, ev_dw_w, ev_dw_b, ev_ln_g, ev_ln_b, ev_w_out,
                           od_w_in, od_conv_w, od_w_out, router_w, router_bias, moe_w_gate, moe_w_up,
                           moe_w_down, consts, out):
    stack = ExitStack()
    with stack:
        def sb(name, shape, dt=F32):
            return stack.enter_context(nc.sbuf_tensor(name, shape, dt))

        def sem(name):
            return stack.enter_context(nc.semaphore(name))

        ring = sb("ring", [P, RING, KD, 512])
        xs = sb("xs", [P, TT, D])
        hT_cat = sb("hT_cat", [P, KD, SEQ])
        big = sb("big", [P, 4096])
        mid = sb("mid", [P, 4096])
        qT = sb("qT", [P, PAIRS, SEQ])
        kv_buf = sb("kv_buf", [P, 3 * KT * P])
        cact = sb("cact", [P, KD, 32])
        b_rows = sb("b_rows", [P, 512])
        prob = sb("prob", [P, 2, KT * P])
        apad = sb("apad", [P, 4, APAD])
        cst = sb("cst", [P, consts.shape[1]])
        modrow = sb("modrow", [P, 512])
        params = sb("params", [P, 44])
        taps = sb("taps", [P, KD, 34])
        modcol = sb("modcol", [P, 2, 12, 4, 2])
        mod_a = sb("mod_a", [P, 5, KD])
        stats = sb("stats", [P, 4, KT])
        qkg = sb("qkg", [P, 2, HD])
        head_stats = sb("head_stats", [P, 4, 32])
        softm = sb("softm", [P, 4, 2])
        bias_r = sb("bias_r", [P, NE])
        small = sb("small", [P, 6])
        block_start = sb("block_start", [P, NE + 1], I32)
        route_w = sb("route_w", [P, KD, 32])
        bias_col = sb("bias_col", [P, 4, 24])
        ln_col = sb("ln_col", [P, 2, TT])
        slot_w = sb("slot_w", [P, NB])
        order_i = sb("order_i", [P, NE], I32)
        row_i = sb("row_i", [P, 2, NB], I32)
        cur_idx = sb("cur_idx", [P, 2, 1], I32)
        tick = sb("tick", [P, 1])

        xhat = big[:, 0:4096].rearrange("p (t d) -> p t d", t=TT)
        ctx_x = kv_buf[:, 0:CT * D].rearrange("p (t d) -> p t d", t=CT)
        kT2 = kv_buf[:, 0:KVH * KT * P].rearrange("p (v k) -> p v k", v=KVH)
        vtok = kv_buf[:, KVH * KT * P:].rearrange("p (t d) -> p t d", t=KT)
        PT = [[v.rearrange("p (k q) -> p k q", k=KT) for v in pair] for pair in
              ((big[:, 0:1536], big[:, 1536:3072]),
               (hT_cat[:, 4:7, :].rearrange("p a b -> p (a b)"), mid[:, 0:1536]))]
        gate_mix = [big[:, 3072:4096], qT[:, 0:2, :].rearrange("p a b -> p (a b)")]
        gate_ffn = qT[:, 2, :]
        mT = xhat.rearrange("p t (j q) -> p (t j) q", q=512)
        hzT = mid[:, 0:2048].rearrange("p (j t) -> p j t", j=KD)
        ctx_hat = mid[:, 2048:4096].rearrange("p (t d) -> p t d", t=CT)
        qtok = mid[:, 0:2048].rearrange("p (t d) -> p t d", t=TT)
        ktok = prob[:, 0, :].rearrange("p (t d) -> p t d", t=KT)
        qtmp = prob[:, 1, :]
        conv_y = mid[:, 2048:4096].rearrange("p (t d) -> p t d", t=4)
        staging = qT[:, 0:2, :].rearrange("p a b -> p (a b)")
        craw = qT[:, 2, 0:16].rearrange("p (s k) -> p s k", s=2)
        gc_sb = [mid[:, 0:512], mid[:, 512:1024]]
        u_pad = [mid[:, 1024 + 520 * i:1024 + 520 * i + SEQ + 2] for i in range(2)]
        sc_y = [mid[:, 2560:3072], mid[:, 3072:3584]]
        work = apad[:, :, :].rearrange("p a b -> p (a b)")
        hg_raw = kv_buf[:, 512:1024]
        hg_next = work[:, 0:512]
        hgT = work[:, 512:1024].rearrange("p (j s) -> p j s", j=KD)
        silu_g = work[:, 1024:1280]
        act_sb = work[:, 1280:1536]
        actT = work[:, 1536:1792].rearrange("p (j s) -> p j s", j=2)
        y_blk = prob[:, 0, 0:512]
        y_out = kv_buf[:, 0:512]
        y_in = [buf[:, at:at + 2048].rearrange("p (k d) -> p k d", k=2) for buf in (big, mid) for at in (0, 2048)]
        router_rows = prob[:, 1, 0:512]
        tap_product = hT_cat[:, KD - 1, :]
        diag = hT_cat[:, KD - 1, :].rearrange("p (t q) -> p t q", t=TT)
        rt = work
        rt_at = [0]

        def rtmp(*shape):
            n = int(np.prod(shape))
            a = rt[:, rt_at[0]:rt_at[0] + n]
            rt_at[0] += n
            if len(shape) == 1:
                return a
            names = "abcd"[:len(shape)]
            return a.rearrange(f"p ({' '.join(names)}) -> p {' '.join(names)}", **dict(zip(names[1:], shape[1:])))

        aff, sel, selm = (rtmp(TT, NE) for _ in range(3))
        oh12 = rtmp(2, TT, NE)
        r32 = rtmp(2, TT, NE)
        r16, picked = (rtmp(TT, NE) for _ in range(2))
        g_a, g_b, g_c, g_d = (rtmp(TT, NG) for _ in range(4))
        r4, w_sum = rtmp(TT, 1), rtmp(TT, 1)
        before16, total16 = rtmp(TT, NE), rtmp(TT, NE)
        nblk16, key16, rank16, nblk_j, order_f, start_e = (rtmp(NE) for _ in range(6))
        cmp16 = rtmp(NE, SEQ // BLK)
        start_cmp = rtmp(NE + 1, NE)
        start_f = rtmp(NE + 1)
        place2, blk2, slot2, w2 = (rtmp(2, TT) for _ in range(4))
        assert rt_at[0] <= 4 * APAD
        mid_at = [0]

        def mtmp(**shape):
            n = int(np.prod(list(shape.values())))
            a = mid[:, mid_at[0]:mid_at[0] + n]
            mid_at[0] += n
            return a.rearrange(f"p ({' '.join(shape)}) -> p {' '.join(shape)}", **shape)

        oh_slot = mtmp(n=8, s=P)
        in_blk = mtmp(n=8, b=NB + 1)
        oh_blk = mtmp(n=8, b=NB)
        val_blk = mtmp(n=8, v=3, b=NB)
        ranks_above = mtmp(e=NE, o=NE)
        oh_order = mtmp(j=NE, e=NE)
        order_tmp = mtmp(j=NE, e=NE)
        assert mid_at[0] <= 4096

        def const(name):
            a, b = CONSTS[name]
            return cst[:, a:b]

        ident = const("ident")

        psum = [stack.enter_context(nc.psum_tensor(f"bank{i}", [P, 512], F32)) for i in range(4)]
        score_ps = [stack.enter_context(nc.psum_tensor(f"scores{i}", [P, 1024], F32)) for i in range(2)]
        gate_ps, up_ps, hg_dve_ps, at_ps = psum
        hg_act_ps = score_ps[1][:, 0:2 * P]
        y_ps = score_ps[0][:, 0:512]

        xhat_d = nc.dram_tensor("xhat_d", [SEQ * 2, 512], F32).ap()
        y_d = [nc.dram_tensor(f"y_d{l}", [SEQ * 4, 512], F32).ap() for l in range(2)]

        unit_in = [sem(f"unit_in{s}") for s in range(RING + 3)]
        consts_in, x_in, ctx_in, c_in, rows_in, bmod_in, qkg_in, router_in = (
            sem(n) for n in ("consts_in", "x_in", "ctx_in", "c_in", "rows_in", "bmod_in", "qkg_in", "router_in"))
        zeroed = sem("zeroed")
        cact_ready = sem("cact_ready")
        acc_done = sem("acc_done")
        bank_read = {}
        modrow_ready = sem("modrow_ready")
        modcol_ready = [sem(f"modcol_ready{i}") for i in range(4)]
        gates_ready = sem("gates_ready")
        gate_ffn_ready = [sem(f"gate_ffn_ready{l}") for l in range(2)]
        dve_step, pool_step = sem("dve_step"), sem("pool_step")
        MOD_OF = {"ctx": 0, "mix0": 0, "ffn0": 1, "mix1": 2, "ffn1": 3}
        norms = ("ctx", "mix0", "ffn0", "mix1", "ffn1")
        ssq_ready = {n: sem(f"ssq_{n}") for n in norms}
        rstd_ready = {n: sem(f"rstd_{n}") for n in norms}
        xhat_ready = {n: sem(f"xhat_{n}") for n in norms}
        hT_even = {n: sem(f"hT_even_{n}") for n in norms}
        hT_odd = {n: sem(f"hT_odd_{n}") for n in norms}
        kv_ready = sem("kv_ready")
        k_ssq, k_rstd, q_ssq, q_rstd = sem("k_ssq"), sem("k_rstd"), sem("q_ssq"), sem("q_rstd")
        k_roped, q_roped, q_ready = sem("k_roped"), sem("q_roped"), sem("q_ready")
        kT_ready, qT_ready = sem("kT_ready"), sem("qT_ready")
        a_ready, ag_ready, glu_ready = sem("a_ready"), sem("ag_ready"), sem("glu_ready")
        scores_done, max_ready, exp_ready, inv_ready, prob_ready = (
            sem(n) for n in ("scores_done", "max_ready", "exp_ready", "inv_ready", "prob_ready"))
        PT_ready, attn_ready = sem("PT_ready"), sem("attn_ready")
        tap_done, pool_tap_done = sem("tap_done"), sem("pool_tap_done")
        centred, sq_ready, var_ready, ln_rstd, diag_ready, ln_done, cat_ready = (
            sem(n) for n in ("centred", "sq_ready", "var_ready", "ln_rstd", "diag_ready", "ln_done", "cat_ready"))
        x_new = [sem(f"x_new{l}") for l in range(2)]
        xhat_stored = [sem(f"xhat_stored{l}") for l in range(2)]
        router_turned = [sem(f"router_turned{l}") for l in range(2)]
        aff_ready = [sem(f"aff_ready{l}") for l in range(2)]
        mask_ready = [sem(f"mask_ready{l}") for l in range(2)]
        table_in = [sem(f"table_in{l}") for l in range(2)]
        route_ready = [sem(f"route_ready{l}") for l in range(2)]
        idx_ready = [sem(f"idx_ready{l}") for l in range(2)]
        hg_in = [sem(f"hg_in{l}") for l in range(2)]
        hg_moved = [sem(f"hg_moved{l}") for l in range(2)]
        hg_turned = [sem(f"hg_turned{l}") for l in range(2)]
        hgT_dve = [sem(f"hgT_dve{l}") for l in range(2)]
        hgT_act = [sem(f"hgT_act{l}") for l in range(2)]
        gate_done = [sem(f"gate_done{l}") for l in range(2)]
        up_done = [sem(f"up_done{l}") for l in range(2)]
        silu_ready = [sem(f"silu_ready{l}") for l in range(2)]
        act_ready = [sem(f"act_ready{l}") for l in range(2)]
        act_turned = [sem(f"act_turned{l}") for l in range(2)]
        actT_ready = [sem(f"actT_ready{l}") for l in range(2)]
        down_done = [sem(f"down_done{l}") for l in range(2)]
        y_read = [sem(f"y_read{l}") for l in range(2)]
        y_moved = [sem(f"y_moved{l}") for l in range(2)]
        y_stored = [sem(f"y_stored{l}") for l in range(2)]
        ticked = [sem(f"ticked{l}") for l in range(2)]
        yin = [[sem(f"yin{l}_{i}") for i in range(TT)] for l in range(2)]
        y_added = [sem(f"y_added{l}") for l in range(2)]
        gc_ready, u_ready, mT_ready = sem("gc_ready"), sem("u_ready"), sem("mT_ready")
        out_done = sem("out_done")

        unit_slot, unit_count, loads = {}, {}, [0] * (RING + 3)
        prev_owner = [None] * (RING + 3)
        unit_prev = {}

        def place(name, slot):
            loads[slot] += 1
            unit_slot[name], unit_count[name] = slot, loads[slot] * 16
            unit_prev[name] = prev_owner[slot]
            prev_owner[slot] = name

        EXPERT_SETS = [[(0, 1, 2), (3, 4, 5), (6, 7, 8)], [(3, 4, 5), (0, 1, 2), (6, 7, 8)]]
        even_units = plan_units()
        odd_units = plan_units_odd()
        moe_base = []
        for l, units, start in ((0, even_units, 4), (1, odd_units, 3)):
            for n, name in enumerate(units):
                place(name, (n + start) % RING)
            moe_base.append(list(loads))
            for e in range(NE):
                for k, w in enumerate(("wg", "wu", "wd")):
                    place((w, l, e), EXPERT_SETS[l][e % 3][k])
        unit_last = {("kv",): ("kvx", TT - 1), ("a",): ("a", 3), ("ag",): ("ag", 3), ("q",): ("q", TT - 1)}
        for name in even_units + odd_units:
            if name[0] == "mod":
                unit_last[name] = name
            elif name[0] in ("wo", "ow"):
                unit_last[name] = ("out", 0 if name[0] == "wo" else 1, name[1], TT - 1)
            elif len(name) == 2:
                unit_last[name] = (name[0], 4 * name[1] + 3)

        wmod_v = [w_mod[l].rearrange("(p k) n -> p k n", k=KD) for l in range(2)]
        win_v = ev_w_in[0].rearrange("(k p) n -> p k n", p=P)
        wout_v = ev_w_out[0].rearrange("(k p) n -> p k n", p=P)
        oin_v = od_w_in[0].rearrange("(k p) n -> p k n", p=P)
        oout_v = od_w_out[0].rearrange("(k p) n -> p k n", p=P)
        kv_at = HEADS * HD
        a_at = kv_at + 2 * KVH * HD
        wg_v = moe_w_gate.rearrange("l e (k p) n -> (l e) p k n", p=P)
        wu_v = moe_w_up.rearrange("l e (k p) n -> (l e) p k n", p=P)
        wd_v = moe_w_down.rearrange("l e (k p) n -> (l e) p k n", p=P)

        def unit_source(name):
            w = name[0]
            if w == "mod":
                return wmod_v[name[1]][:, :, name[2] * 512:(name[2] + 1) * 512]
            if w == "kv":
                return win_v[:, :, kv_at:a_at]
            if w == "a":
                return win_v[:, :, a_at:a_at + 512]
            if w == "ag":
                return win_v[:, :, a_at + 512:a_at + 1024]
            if w == "q":
                return win_v[:, :, 0:512]
            if w == "wo":
                return wout_v[:, :, name[1] * 512:(name[1] + 1) * 512]
            if w == "ow":
                return oout_v[:, :, name[1] * 512:(name[1] + 1) * 512]
            at = {"gb": 0, "gc": D, "v": 2 * D}[w] + name[1] * 512
            return oin_v[:, :, at:at + 512]

        def unit(name):
            return ring[:, unit_slot[name]]

        def expert_view(slot, w):
            outside = (mid[:, :], hT_cat[:, :, :].rearrange("p k n -> p (k n)"), big[:, :])
            u = ring[:, slot] if slot < RING else outside[slot - RING].rearrange("p (k n) -> p k n", n=512)
            return u.rearrange("p k n -> p (k n)").rearrange("p (k n) -> p k n", n=D) if w == "wd" else u

        def bank(name):
            return psum[GROUP_AT[name] % NBANK]

        block = stack.enter_context(nc.Block())

        @block.sync
        def _(sp):
            def load_dense(name):
                prev = unit_prev[name]
                if prev in unit_last:
                    sp.wait_ge(acc_done, GROUP_AT[unit_last[prev]] + 1)
                src = unit_source(name)
                dst = unit(name)
                if name[0] == "kv":
                    dst = dst[:, :, 0:256]
                sp.dma_start(dst, src).then_inc(unit_in[unit_slot[name]], 16)

            def load_third(l, e, par, k):
                slot = EXPERT_SETS[l][par][k]
                src = (wg_v, wu_v, wd_v)[k][bass.ds(e + l * NE, 1)].rearrange("o p k n -> (o p) k n")
                sp.dma_start(expert_view(slot, "wd" if k == 2 else "wg"), src).then_inc(unit_in[slot], 16)

            def load_experts(l, next_units):
                def two_before(i, par, k):
                    if k < 2:
                        par, k = par - 1, k + 1
                    else:
                        k = 0
                    slot = EXPERT_SETS[l][par % 3][k]
                    sp.wait_ge(unit_in[slot], i * 16 + (moe_base[l][slot] + (1 if par >= 0 else 0)) * 16)

                for par in range(2):
                    for k, w in enumerate(("wg", "wu", "wd")):
                        prev = unit_prev[(w, l, par)]
                        sp.wait_ge(acc_done, GROUP_AT[unit_last[prev]] + 1)
                        load_third(l, par, par, k)
                sp.wait_ge(route_ready[l], 1)
                sp.wait_ge(xhat_stored[l], 16 * TT)
                sp.wait_ge(hg_in[l], 32)
                e = sp.value_load(order_i[0:1, 2:3], min_val=2, max_val=NE - 1)
                for k in range(3):
                    two_before(0, 2, k)
                    load_third(l, e, 2, k)
                used = (gate_done[l], up_done[l], down_done[l])

                def load_next(j, i, par):
                    e = sp.value_load(order_i[0:1, bass.ds(j, 1)], min_val=2, max_val=NE - 1)
                    end = sp.value_load(block_start[0:1, bass.ds(j - 2, 1)], min_val=1, max_val=MAXB)
                    for k in range(3):
                        two_before(i, par, k)
                        sp.wait_ge(used[k], end)
                        load_third(l, e, par, k)

                with sp.Fori(1, NE // 3) as i:
                    for par in range(3):
                        load_next(i * 3 + par, i, par)
                load_next(NE - 1, NE // 3, 0)
                end = sp.value_load(block_start[0:1, NE - 2:NE - 1], min_val=NE - 2, max_val=MAXB)
                total = sp.value_load(block_start[0:1, NE:NE + 1], min_val=NE, max_val=MAXB)
                for k, name in enumerate(next_units[0:3]):
                    sp.wait_ge(used[k], end)
                    load_dense(name)
                sp.wait_ge(down_done[l], total)
                sp.wait_ge(y_stored[l], total * 16 + 16)
                for t in range(TT):
                    for k in range(2):
                        rows = y_d[l][(k * SEQ + t * P) * 2:(k * SEQ + (t + 1) * P) * 2, :].rearrange("(p h) n -> p (h n)", h=2)
                        sp.dma_start(y_in[t][:, k, :], rows).then_inc(yin[l][t], 16)
                for name in next_units[3:]:
                    load_dense(name)

            sp.dma_start(cst[:, :], consts).then_inc(consts_in, 16)
            sp.dma_start(craw[:, 0, :], c.rearrange("o (p k) -> (o p) k", k=KD)).then_inc(c_in, 16)
            sp.dma_start(craw[:, 1, :], c_ctx.rearrange("(p k) -> p k", k=KD)).then_inc(c_in, 16)
            load_dense(even_units[0])
            sp.wait_ge(zeroed, 1)
            sp.dma_start(staging[0:16, 0:P], norm_mix_g.rearrange("l (j p) -> (l j) p", p=P)).then_inc(rows_in, 16)
            sp.dma_start(staging[16:32, 0:P], norm_ffn_g.rearrange("l (j p) -> (l j) p", p=P)).then_inc(rows_in, 16)
            for k, v in enumerate((ev_dw_b, ev_ln_g, ev_ln_b)):
                sp.dma_start(staging[32 + 4 * k:36 + 4 * k, 0:P], v.rearrange("o (j p) -> (o j) p", p=P)).then_inc(rows_in, 16)
            sp.dma_start(hT_cat[0:CONV_K, 0, :], ev_dw_w[0]).then_inc(rows_in, 16)
            sp.dma_start(hT_cat[CONV_K:CONV_K + SC_K, 0:2, :], od_conv_w[0].rearrange("k (a n) -> k a n", a=2)).then_inc(rows_in, 16)
            sp.dma_start(b_rows[0:24, :], b_mod.rearrange("l (c n) -> (l c) n", n=512)).then_inc(bmod_in, 16)
            load_dense(even_units[1])
            sp.dma_start(xs[:, :, :], x[0].rearrange("(t p) d -> p t d", p=P)).then_inc(x_in, 16)
            load_dense(even_units[2])
            load_dense(even_units[3])
            sp.dma_start(ctx_x, ctx[0].rearrange("(t p) d -> p t d", p=P)).then_inc(ctx_in, 16)
            for name in even_units[4:]:
                load_dense(name)
            load_experts(0, odd_units)
            load_experts(1, [])
            for t in range(TT):
                sp.wait_ge(y_added[1], t + 1)
                sp.dma_start(out[0, t * P:(t + 1) * P, :], xs[:, t, :]).then_inc(out_done, 16)
            sp.wait_ge(out_done, 16 * TT)

        @block.scalar
        def _(act):
            def acc_wait(name):
                act.wait_ge(acc_done, GROUP_AT[name] + 1)

            act.dma_start(qkg[:, 0, :], ev_q_norm_g.to_broadcast([P, HD])).then_inc(qkg_in, 16)
            act.dma_start(qkg[:, 1, :], ev_k_norm_g.to_broadcast([P, HD])).then_inc(qkg_in, 16)
            act.wait_ge(zeroed, 1)
            act.dma_start(route_w[:, :, 0:NE], router_w.rearrange("(k p) n -> p k n", p=P)).then_inc(router_in, 16)
            act.dma_start(bias_r[:, :], router_bias.rearrange("(o n) -> o n", o=1).to_broadcast([P, NE])).then_inc(router_in, 16)

            act.wait_ge(c_in, 32)
            for s in range(2):
                act.activation(cact[:, :, s], craw[:, s, :], ACT.Silu).then_inc(cact_ready, 1)

            mods = [0]

            def modrow_copy(l, c):
                acc_wait(("mod", l, c))
                if mods[0]:
                    act.wait_ge(acc_done, last_fin[0] + 1)
                act.activation(modrow[:, :], bank(("mod", l, c))[:, :], ACT.Copy).then_inc(modrow_ready, 1)
                mods[0] += 1
                bank_read[("mod", l, c)] = (modrow_ready, mods[0])
                last_fin[0] = GROUP_AT[("fin", l, c)]

            last_fin = [0]

            squared = []

            def squares(norm, src, tiles, wait):
                junk = hT_cat[:, 2:4, :].rearrange("p a b -> p (a b)") if norm == "mix1" else mid[:, 0:D]
                first = TT if norm == "ctx" else 0
                for t in range(tiles):
                    wait(t)
                    if squared:
                        act.wait_ge(*squared[-1])
                    act.activation(junk, src[:, t, :], ACT.Square,
                                   accum_out=stats[:, 0, first + t:first + t + 1]).then_inc(ssq_ready[norm], 1)
                    squared.append((ssq_ready[norm], t + 1))


            def modulate(norm, dst, n, scale, shift, chunks):
                act.wait_ge(modcol_ready[MOD_OF[norm]], 1)
                for j in chunks:
                    g = ("norm", norm, j)
                    acc_wait(g)
                    act.activation(dst[:, j, :], bank(g)[:, 0:n], ACT.Identity, bias=shift(j),
                                   scale=scale(j)).then_inc(hT_even[norm], 1)
                    bank_read[g] = (hT_even[norm], j // 2 + 1)

            def shift_of(l, which, s):
                return lambda j: modcol[:, l, 2 * which + j // 4, j % 4, s:s + 1]

            for c_ in range(4):
                modrow_copy(0, c_)
                if c_ == 1:
                    squares("mix0", xs, TT, lambda t: act.wait_ge(x_in, 16))
            squares("ctx", ctx_x, CT, lambda t: act.wait_ge(ctx_in, 16))
            modulate("ctx", hzT, CTX, lambda j: mod_a[:, 4, j:j + 1], shift_of(0, 0, 1), range(0, KD, 2))
            modulate("mix0", hT_cat, SEQ, lambda j: mod_a[:, 0, j:j + 1], shift_of(0, 0, 0), range(0, KD, 2))

            for t in range(KT):
                tile = ("kvz", t) if t < CT else ("kvx", t - CT)
                at = TT + t if t < CT else t - CT
                acc_wait(tile)
                act.activation(ktok[:, at, :], bank(tile)[:, 0:P], ACT.Copy).then_inc(kv_ready, 1)
                act.activation(vtok[:, at, :], bank(tile)[:, P:2 * P], ACT.Copy).then_inc(kv_ready, 1)
                bank_read[tile] = (kv_ready, 2 * t + 2)
            for i in range(4):
                acc_wait(("a", i))
                act.activation(apad[:, i, PAD:PAD + SEQ], bank(("a", i))[:, :], ACT.Copy).then_inc(a_ready, 1)
                bank_read[("a", i)] = (a_ready, i + 1)
                modrow_copy(*WITH_A[i])
            for i in range(4):
                acc_wait(("ag", i))
                if i >= 2:
                    act.wait_ge(glu_ready, i - 1)
                act.activation(qT[:, i % 2, :], bank(("ag", i))[:, :], ACT.Sigmoid).then_inc(ag_ready, 1)
                bank_read[("ag", i)] = (ag_ready, i + 1)
                modrow_copy(*WITH_AG[i])
            for v in range(KVH):
                for h in range(2):
                    g = ("kT", v, h)
                    acc_wait(g)
                    act.activation(kT2[:, v, h * 384:(h + 1) * 384], bank(g)[:, 0:384], ACT.Copy).then_inc(kT_ready, 1)
                    bank_read[g] = (kT_ready, 2 * v + h + 1)
            for t in range(TT):
                acc_wait(("q", t))
                act.activation(qtok[:, t, :], bank(("q", t))[:, :], ACT.Copy).then_inc(q_ready, 1)
                bank_read[("q", t)] = (q_ready, t + 1)
            for m in WITH_Q:
                modrow_copy(*m)
            for i in range(PAIRS):
                acc_wait(("qT", i))
                act.activation(qT[:, i, :], bank(("qT", i))[:, :], ACT.Copy).then_inc(qT_ready, 1)
                bank_read[("qT", i)] = (qT_ready, i + 1)


            def exps(n):
                act.wait_ge(max_ready, n + 1)
                if n >= 2:
                    acc_wait(("PT", (n - 2) // 4, (n - 2) % 4, 1))
                act.activation(prob[:, n % 2, :], score_ps[n % 2][:, 0:KT * P], ACT.Exp, bias=softm[:, 0, n % 2:n % 2 + 1],
                               scale=HD ** -0.5, accum_out=softm[:, 1, n % 2:n % 2 + 1]).then_inc(exp_ready, 1)

            def attn_out(s):
                acc_wait(("pv", s))
                act.activation(hT_cat[:, s // 2, (s % 2) * 256:(s % 2 + 1) * 256], bank(("pv", s))[:, 0:256],
                               ACT.Copy).then_inc(attn_ready, 1)
                bank_read[("pv", s)] = (attn_ready, s + 1)

            exps(0)
            for s in range(8):
                for u in range(4):
                    n = 4 * s + u
                    act.wait_ge(inv_ready, n + 1)
                    act.activation(prob[:, n % 2, :], prob[:, n % 2, :], ACT.Copy,
                                   scale=softm[:, 3, n % 2:n % 2 + 1]).then_inc(prob_ready, 1)
                    if n + 1 < 32:
                        exps(n + 1)
                    hh, qt = u // 2, u % 2
                    for g3 in range(2):
                        g = ("PT", s, u, g3)
                        acc_wait(g)
                        if s >= 2:
                            acc_wait(("pv", s - 2))
                        act.activation(PT[s % 2][hh][:, 3 * g3:3 * g3 + 3, qt * P:(qt + 1) * P],
                                       bank(g)[:, 0:384].rearrange("p (k q) -> p k q", k=3),
                                       ACT.Copy).then_inc(PT_ready, 1)
                        bank_read[g] = (PT_ready, 2 * n + g3 + 1)
                    if u == 0 and s:
                        attn_out(s - 1)
                    if GATE_AT.get((s, u), ("",))[0] == "mod":
                        modrow_copy(*GATE_AT[s, u][1:])
            attn_out(7)

            for i in range(4):
                act.wait_ge(ln_done, i + 1)
                act.activation(hT_cat[:, 4 + i, :], conv_y[:, i, :], ACT.Silu, bias=params[:, 40 + i:41 + i],
                               scale=params[:, 36 + i:37 + i]).then_inc(cat_ready, 1)

            def ffn(l):
                norm = f"ffn{l}"
                squares(norm, xs, TT, lambda t: act.wait_ge(x_new[l], TT + t + 1))
                for t in range(TT):
                    act.wait_ge(xhat_ready[norm], t + 1)
                    act.dma_start(xhat_d[t * 2 * P:(t + 1) * 2 * P, :].rearrange("(p h) n -> p (h n)", h=2),
                                  xhat[:, t, :]).then_inc(xhat_stored[l], 16)
                modulate(norm, hT_cat, SEQ, lambda j: mod_a[:, 1 + 2 * l, j:j + 1], shift_of(l, 3, 0), range(0, KD, 2))
                acc_wait(("route", l, 0))
                act.activation(router_rows, bank(("route", l, 0))[:, :], ACT.Copy).then_inc(router_turned[l], 1)
                bank_read[("route", l, 0)] = (router_turned[l], 1)
                modrow_copy(*GATES[l][2])
                acc_wait(("route", l, 1))
                act.activation(aff.rearrange("p a b -> p (a b)"), bank(("route", l, 1))[:, 0:TT * NE],
                               ACT.Sigmoid).then_inc(aff_ready[l], 1)
                bank_read[("route", l, 1)] = (aff_ready[l], 1)
                for h in range(2):
                    if h:
                        modrow_copy(*GATES[l][3])
                    g = ("fin",) + GATES[l][2 + h]
                    acc_wait(g)
                    act.activation(gate_ffn[h * 64:(h + 1) * 64, :], bank(g)[h * 64:(h + 1) * 64, :],
                                   ACT.Copy).then_inc(gate_ffn_ready[l], 1)
                    bank_read[g] = (gate_ffn_ready[l], h + 1)

                def turn_in():
                    for j in (2, 3, 6, 7):
                        at = (j % 4 - 2) * P + (j // 4) * BLK
                        act.activation(hgT[:, j, :], hg_act_ps[:, at:at + BLK], ACT.Identity,
                                       bias=shift_of(l, 3, 0)(j), scale=mod_a[:, 1 + 2 * l, j:j + 1]).then_inc(hgT_act[l], 1)

                act.wait_ge(route_ready[l], 1)
                total = act.value_load(block_start[0:1, NE:NE + 1], min_val=NE, max_val=MAXB)

                def move_on(b_plus_1):
                    act.wait_ge(hg_in[l], b_plus_1 * 16)
                    act.activation(hg_next, hg_raw, ACT.Copy).then_inc(hg_moved[l], 1)

                move_on(1)
                act.wait_ge(hg_turned[l], 1)
                turn_in()
                move_on(2)
                with act.Fori(0, total) as b:
                    act.wait_ge(gate_done[l], b + 1)
                    act.wait_ge(act_ready[l], b + 1)
                    act.activation(silu_g, gate_ps[:, 0:256], ACT.Silu).then_inc(silu_ready[l], 1)
                    act.wait_ge(hg_turned[l], b + 2)
                    act.wait_ge(up_done[l], b + 1)
                    turn_in()
                    move_on(b + 3)

            ffn(0)

            for m in GATES[1][0:2]:
                modrow_copy(*m)
            squares("mix1", xs, TT, lambda t: act.wait_ge(y_added[0], t + 1))
            modulate("mix1", hT_cat, SEQ, lambda j: mod_a[:, 2, j:j + 1], shift_of(1, 0, 0), range(0, KD, 2))
            for h in range(2):
                for i in range(4):
                    m = 4 * h + i
                    acc_wait(("gc", m))
                    if m >= 2:
                        act.wait_ge(u_ready, m - 1)
                    act.activation(gc_sb[m % 2], bank(("gc", m))[:, :], ACT.Copy).then_inc(gc_ready, 1)
                    bank_read[("gc", m)] = (gc_ready, m + 1)
            ffn(1)

        @block.vector
        def _(dve):
            steps = [0]

            def link(ins):
                steps[0] += 1
                ins.then_inc(dve_step, 1)
                dve.wait_ge(dve_step, steps[0])

            def acc_wait(name):
                dve.wait_ge(acc_done, GROUP_AT[name] + 1)

            V = nc.vector
            V.memset(b_rows[:, :], 0.0)
            V.memset(staging[:, 0:P], 0.0)
            V.memset(route_w[:, :, :].rearrange("p k m -> p (k m)"), 0.0)
            V.memset(cact[:, :, :].rearrange("p k m -> p (k m)"), 0.0)
            V.memset(apad[:, :, 0:PAD], 0.0)
            V.memset(apad[:, :, PAD + SEQ:APAD], 0.0)
            for l in range(2):
                V.memset(small[:, l:l + 1], 0.0).then_inc(y_read[l], 1)
                V.memset(small[:, 2 + l:3 + l], 0.0).then_inc(ticked[l], 1)
                V.memset(small[:, 4 + l:5 + l], 0.0).then_inc(act_ready[l], 1)
            V.memset(hT_cat[0:34, 1, :], 0.0).then_inc(zeroed, 1)

            acc_wait(("params",))
            link(V.tensor_copy(params[:, :], bank(("params",))[:, 0:44]))
            bank_read[("params",)] = (dve_step, steps[0])
            acc_wait(("taps",))
            link(V.tensor_copy(taps[:, :, :], bank(("taps",))[:, 0:KD * 34].rearrange("p (j k) -> p j k", j=KD)))
            bank_read[("taps",)] = (dve_step, steps[0])

            acc_wait(("bias",))
            link(V.tensor_copy(bias_col[:, :, :], bank(("bias",))[:, 0:4 * 24].rearrange("p (j c) -> p j c", j=4)))
            bank_read[("bias",)] = (dve_step, steps[0])

            gates = [0]

            def fin(l, c):
                g = ("fin", l, c)
                acc_wait(g)
                if c in (4, 5):
                    gates[0] += 1
                    bank_read[g] = (gates_ready, gates[0])
                if c in (4, 5):
                    V.tensor_copy(gate_mix[l][:, (c - 4) * 512:(c - 3) * 512], bank(g)[:, :]).then_inc(gates_ready, 1)
                else:
                    link(V.tensor_tensor(modcol[:, l, c, :, :], bank(g)[:, 0:8].rearrange("p (j s) -> p j s", s=2),
                                         bias_col[:, :, 12 * l + c].unsqueeze(2).to_broadcast([P, 4, 2]), ALU.add))
                    bank_read[g] = (dve_step, steps[0])
                if c in (3, 9):
                    first = c - 1
                    gcol = (0 if c == 3 else 16) + 8 * l
                    at = 2 * l + (0 if c == 3 else 1)
                    for s in range(1 if (l, c) == (0, 3) else 0, -1, -1):
                        ins = V.scalar_tensor_tensor(out=mod_a[:, 4 if s else at, :].rearrange("p (h j) -> p h j", h=2),
                                                     in0=modcol[:, l, first:first + 2, :, s], scalar=1.0,
                                                     in1=params[:, gcol:gcol + 8].rearrange("p (h j) -> p h j", h=2),
                                                     op0=ALU.add, op1=ALU.mult)
                    ins.then_inc(modcol_ready[at], 1)

            def normalise(norm, src, tiles):
                dst = xhat if norm != "ctx" else ctx_hat
                for t in tiles:
                    dve.wait_ge(rstd_ready[norm], t + 1)
                    V.tensor_scalar(dst[:, t, :], src[:, t, :], stats[:, 1 if norm != "ctx" else 2, t:t + 1], None,
                                    ALU.mult).then_inc(xhat_ready[norm], 1)

            def modulate(norm, dst, n, scale, shift):
                dve.wait_ge(modcol_ready[MOD_OF[norm]], 1)
                for j in range(1, KD, 2):
                    g = ("norm", norm, j)
                    acc_wait(g)
                    V.tensor_scalar(dst[:, j, :], bank(g)[:, 0:n], scale(j), shift(j), ALU.mult,
                                    ALU.add).then_inc(hT_odd[norm], 1)
                    bank_read[g] = (hT_odd[norm], j // 2 + 1)

            def shift_of(l, which, s):
                return lambda j: modcol[:, l, 2 * which + j // 4, j % 4, s:s + 1]

            fin(0, 0)
            fin(0, 1)
            normalise("mix0", xs, range(TT))
            fin(0, 2)
            fin(0, 3)
            normalise("ctx", ctx_x, range(CT))
            modulate("ctx", hzT, CTX, lambda j: mod_a[:, 4, j:j + 1], shift_of(0, 0, 1))
            modulate("mix0", hT_cat, SEQ, lambda j: mod_a[:, 0, j:j + 1], shift_of(0, 0, 0))

            def head_norm(v, tmp, n, nh, g, stat, ssq, rstd, count):
                link(V.tensor_tensor(tmp, v, v, ALU.mult))
                V.tensor_reduce(head_stats[:, stat, 0:n * nh], tmp.rearrange("p (m d) -> p m d", d=HD), AX_X,
                                ALU.add).then_inc(ssq, 1)
                if nh == HEADS:
                    conv(3)
                dve.wait_ge(rstd, count)
                v3 = v.rearrange("p (m d) -> p m d", d=HD)
                link(V.tensor_tensor(v3, v3, head_stats[:, stat, 0:n * nh].unsqueeze(2).to_broadcast([P, n * nh, HD]), ALU.mult))
                link(V.tensor_tensor(v3, v3, qkg[:, g, :].unsqueeze(1).to_broadcast([P, n * nh, HD]), ALU.mult))

            def rope(v, tmp, tile, nh, done):
                x12 = v.rearrange("p (h i two) -> p two h i", h=nh, two=2)
                half = nh * HD // 2
                t1 = tmp[:, 0:half].rearrange("p (h i) -> p h i", h=nh)
                t2 = tmp[:, half:2 * half].rearrange("p (h i) -> p h i", h=nh)
                cs = const("cos")[:, tile * 32:(tile + 1) * 32].unsqueeze(1).to_broadcast([P, nh, 32])
                sn = const("sin")[:, tile * 32:(tile + 1) * 32].unsqueeze(1).to_broadcast([P, nh, 32])
                x1, x2 = x12[:, 0], x12[:, 1]
                V.tensor_tensor(t1, x1, sn, ALU.mult)
                link(V.tensor_tensor(t2, x2, sn, ALU.mult))
                V.tensor_tensor(x1, x1, cs, ALU.mult)
                link(V.tensor_tensor(x2, x2, cs, ALU.mult))
                link(V.tensor_tensor(x2, x2, t1, ALU.add))
                V.tensor_tensor(x1, x1, t2, ALU.subtract).then_inc(done, 1)

            dve.wait_ge(kv_ready, 2 * KT)
            dve.wait_ge(qkg_in, 32)
            head_norm(ktok.rearrange("p t d -> p (t d)"), qtmp, KT, KVH, 1, 0, k_ssq, k_rstd, 1)
            for t in range(TT):
                rope(ktok[:, t, :], qtmp[:, t * P:(t + 1) * P], t, KVH, k_roped)

            tap_list = [(k, i) for k in range(CONV_K) for i in (0, 1)] + [(k, 2) for k in range(CONV_K)]
            tap_at = [0]

            def conv(n):
                for _ in range(min(n, len(tap_list) - tap_at[0])):
                    at, (k, i) = tap_at[0], tap_list[tap_at[0]]
                    src = apad[:, i, k:k + SEQ]
                    w = taps[:, i, k:k + 1]
                    if k == 0:
                        dve.wait_ge(glu_ready, i + 1)
                        ins = V.tensor_scalar(conv_y[:, i, :], src, w, params[:, 32 + i:33 + i], ALU.mult, ALU.add)
                    else:
                        dve.wait_ge(tap_done, at - (1 if i < 2 else 0))
                        ins = V.scalar_tensor_tensor(out=conv_y[:, i, :], in0=src, scalar=w, in1=conv_y[:, i, :],
                                                     op0=ALU.mult, op1=ALU.add)
                    ins.then_inc(tap_done, 1)
                    tap_at[0] += 1

            for m in WITH_A[0:3]:
                fin(*m)
            for i in range(4):
                dve.wait_ge(ag_ready, i + 1)
                a_in = apad[:, i, PAD:PAD + SEQ]
                V.tensor_tensor(a_in, a_in, qT[:, i % 2, :], ALU.mult).then_inc(glu_ready, 1)
                fin(*([WITH_A[3]] + WITH_AG)[i])
                if i:
                    conv(10)

            for t in range(TT):
                if t == 1:
                    fin(*WITH_AG[3])
                dve.wait_ge(q_ready, t + 1)
                if t:
                    dve.wait_ge(q_roped, t)
                head_norm(qtok[:, t, :], qtmp[:, 0:512], 1, HEADS, 0, 1, q_ssq, q_rstd, t + 1)
                rope(qtok[:, t, :], qtmp[:, 0:512], t, HEADS, q_roped)
                if t < TT - 1:
                    conv(3)
            for m in WITH_Q:
                fin(*m)

            def row_max(n):
                dve.wait_ge(scores_done, n + 1)
                link(V.tensor_reduce(softm[:, 2, n % 2:n % 2 + 1], score_ps[n % 2][:, 0:KT * P], AX_X, ALU.max))
                V.tensor_scalar(softm[:, 0, n % 2:n % 2 + 1], softm[:, 2, n % 2:n % 2 + 1], -HD ** -0.5, None,
                                ALU.mult).then_inc(max_ready, 1)

            def layer_norm(s, u):
                if (s, u) == (6, 1):
                    acc_wait(("mu",))
                    for i in range(4):
                        V.scalar_tensor_tensor(out=conv_y[:, i, :], in0=bank(("mu",))[:, :], scalar=-1.0 / CONV_C,
                                               in1=conv_y[:, i, :], op0=ALU.mult, op1=ALU.add).then_inc(centred, 1)
                    bank_read[("mu",)] = (centred, 4)
                if (s, u) in ((6, 2), (6, 3)):
                    for i in (0, 1) if u == 2 else (2, 3):
                        dve.wait_ge(centred, i + 1)
                        V.tensor_tensor(apad[:, i, 0:SEQ], conv_y[:, i, :], conv_y[:, i, :], ALU.mult).then_inc(sq_ready, 1)
                ident_t = ident.unsqueeze(1).to_broadcast([P, TT, P])
                if (s, u) == (7, 1):
                    acc_wait(("var",))
                    link(V.tensor_tensor(diag, bank(("var",))[:, :].rearrange("p (t q) -> p t q", t=TT), ident_t, ALU.mult))
                    bank_read[("var",)] = (dve_step, steps[0])
                    V.tensor_reduce(ln_col[:, 0, :], diag, AX_X, ALU.add).then_inc(var_ready, 1)
                if (s, u) == (7, 2):
                    dve.wait_ge(ln_rstd, 1)
                    V.tensor_tensor(diag, ident_t, ln_col[:, 1, :].unsqueeze(2).to_broadcast([P, TT, P]), ALU.mult).then_inc(diag_ready, 1)

            row_max(0)
            for s in range(8):
                for u in range(4):
                    n = 4 * s + u
                    dve.wait_ge(exp_ready, n + 1)
                    V.reciprocal(softm[:, 3, n % 2:n % 2 + 1], softm[:, 1, n % 2:n % 2 + 1]).then_inc(inv_ready, 1)
                    if n + 1 < 32:
                        row_max(n + 1)
                    conv(2)
                    if GATE_AT.get((s, u), ("",))[0] == "fin":
                        fin(*GATE_AT[s, u][1:])
                    layer_norm(s, u)

            acc_wait(("ln_rstd",))
            for i in range(4):
                V.tensor_tensor(conv_y[:, i, :], conv_y[:, i, :], bank(("ln_rstd",))[:, :], ALU.mult).then_inc(ln_done, 1)
            bank_read[("ln_rstd",)] = (ln_done, 4)

            def mixer_out(l):
                for h in range(2):
                    for t in range(TT):
                        g = ("out", l, h, t)
                        tmp = prob[:, 0, 0:512] if t % 2 else prob[:, 1, 0:512]
                        acc_wait(g)
                        link(V.tensor_tensor(tmp, bank(g)[:, :], gate_mix[l][:, h * 512:(h + 1) * 512], ALU.mult))
                        bank_read[g] = (dve_step, steps[0])
                        xh = xs[:, t, h * 512:(h + 1) * 512]
                        V.tensor_tensor(xh, xh, tmp, ALU.add).then_inc(x_new[l], 1)
                        if l == 0 and h == 1 and t >= 1:
                            normalise("ffn0", xs, [t - 1])
                normalise(f"ffn{l}", xs, [TT - 1] if l == 0 else range(TT))

            def route(l):
                key = const("expert_key").unsqueeze(1).to_broadcast([P, TT, NE])
                gkey = const("group_key").unsqueeze(1).to_broadcast([P, TT, NG])

                def b16(v):
                    return v.to_broadcast([P, TT, NE])

                dve.wait_ge(aff_ready[l], 1)
                link(V.tensor_tensor(sel, aff, bias_r[:, :].unsqueeze(1).to_broadcast([P, TT, NE]), ALU.add))
                s4 = sel.rearrange("p t (g k) -> p t g k", g=NG)
                e = [s4[:, :, :, k] for k in range(EPG)]
                V.tensor_tensor(g_a, e[0], e[1], ALU.max)
                V.tensor_tensor(g_b, e[0], e[1], ALU.min)
                V.tensor_tensor(g_c, e[2], e[3], ALU.max)
                link(V.tensor_tensor(g_d, e[2], e[3], ALU.min))
                link(V.tensor_tensor(g_b, g_b, g_d, ALU.max))
                link(V.tensor_tensor(g_d, g_a, g_c, ALU.min))
                link(V.tensor_tensor(g_b, g_b, g_d, ALU.max))
                link(V.tensor_tensor(g_a, g_a, g_c, ALU.max))
                link(V.tensor_tensor(g_a, g_a, g_b, ALU.add))
                link(V.tensor_reduce(r4, g_a, AX_X, ALU.max))
                link(V.tensor_tensor(g_b, g_a, r4.to_broadcast([P, TT, NG]), ALU.is_equal))
                link(V.tensor_tensor(g_b, g_b, gkey, ALU.mult))
                link(V.tensor_reduce(r4, g_b, AX_X, ALU.max))
                link(V.tensor_tensor(g_b, g_b, r4.to_broadcast([P, TT, NG]), ALU.is_equal))
                link(V.tensor_scalar(g_c, g_b, 1e30, -1e30, ALU.mult, ALU.add))
                m4 = selm.rearrange("p t (g k) -> p t g k", g=NG)
                link(V.tensor_tensor(m4, s4, g_b.unsqueeze(3).to_broadcast([P, TT, NG, EPG]), ALU.mult))
                link(V.tensor_tensor(m4, m4, g_c.unsqueeze(3).to_broadcast([P, TT, NG, EPG]), ALU.add))
                for n in range(2):
                    oh = oh12[:, n]
                    link(V.tensor_reduce(r4, selm, AX_X, ALU.max))
                    link(V.tensor_tensor(r16, selm, b16(r4), ALU.is_equal))
                    link(V.tensor_tensor(r16, r16, key, ALU.mult))
                    link(V.tensor_reduce(r4, r16, AX_X, ALU.max))
                    link(V.tensor_tensor(oh, r16, b16(r4), ALU.is_equal))
                    if n == 0:
                        link(V.scalar_tensor_tensor(out=selm, in0=oh, scalar=-3e38, in1=selm, op0=ALU.mult, op1=ALU.add))
                V.tensor_tensor(picked, oh12[:, 0], oh12[:, 1], ALU.add).then_inc(mask_ready[l], 1)
                link(V.tensor_tensor(r32, oh12, aff.unsqueeze(1).to_broadcast([P, 2, TT, NE]), ALU.mult))
                link(V.tensor_reduce(w2, r32, AX_X, ALU.add))
                link(V.tensor_tensor(w_sum[:, :, 0], w2[:, 0, :], w2[:, 1, :], ALU.add))
                link(V.reciprocal(w_sum, w_sum))
                link(V.tensor_tensor(w2, w2, w_sum[:, :, 0].unsqueeze(1).to_broadcast([P, 2, TT]), ALU.mult))
                g = ("route", l, 2)
                acc_wait(g)
                V.tensor_copy(before16, bank(g)[:, 0:TT * NE].rearrange("p (t e) -> p t e", e=NE))
                link(V.tensor_copy(total16, bank(g)[:, TT * NE:2 * TT * NE].rearrange("p (t e) -> p t e", e=NE)))
                bank_read[g] = (dve_step, steps[0])
                for t in range(1, TT):
                    V.tensor_tensor(before16[:, t, :], before16[:, t, :], total16[:, t - 1, :], ALU.add)
                    link(V.tensor_tensor(total16[:, t, :], total16[:, t, :], total16[:, t - 1, :], ALU.add))
                n_full = SEQ // BLK
                link(V.tensor_tensor(cmp16, total16[:, TT - 1, :].unsqueeze(2).to_broadcast([P, NE, n_full]),
                                     const("full_blocks").unsqueeze(1).to_broadcast([P, NE, n_full]), ALU.is_gt))
                link(V.tensor_reduce(nblk16, cmp16, AX_X, ALU.add))
                link(V.scalar_tensor_tensor(out=key16, in0=nblk16, scalar=float(NE), in1=const("rank_tie"), op0=ALU.mult,
                                            op1=ALU.add))
                by_e = [P, NE, NE]
                link(V.tensor_tensor(ranks_above, key16.unsqueeze(1).to_broadcast(by_e), key16.unsqueeze(2).to_broadcast(by_e),
                                     ALU.is_gt))
                link(V.tensor_reduce(rank16, ranks_above, AX_X, ALU.add))
                link(V.tensor_tensor(oh_order, rank16.unsqueeze(1).to_broadcast(by_e),
                                     const("rank_at").unsqueeze(2).to_broadcast(by_e), ALU.is_equal))
                link(V.tensor_tensor(order_tmp, oh_order, nblk16.unsqueeze(1).to_broadcast(by_e), ALU.mult))
                link(V.tensor_reduce(nblk_j, order_tmp, AX_X, ALU.add))
                link(V.tensor_tensor(start_cmp, nblk_j.unsqueeze(1).to_broadcast([P, NE + 1, NE]),
                                     const("expert_before").rearrange("p (a b) -> p a b", b=NE), ALU.mult))
                link(V.tensor_reduce(start_f, start_cmp, AX_X, ALU.add))
                V.tensor_copy(block_start[:, :], start_f)
                link(V.tensor_tensor(order_tmp, oh_order.rearrange("p j e -> p e j"),
                                     start_f[:, 0:NE].unsqueeze(1).to_broadcast(by_e), ALU.mult))
                link(V.tensor_reduce(start_e, order_tmp, AX_X, ALU.add))
                link(V.scalar_tensor_tensor(out=before16, in0=start_e.unsqueeze(1).to_broadcast([P, TT, NE]),
                                            scalar=float(BLK), in1=before16, op0=ALU.mult, op1=ALU.add))
                link(V.tensor_tensor(r32, oh12, before16.unsqueeze(1).to_broadcast([P, 2, TT, NE]), ALU.mult))
                link(V.tensor_reduce(place2, r32, AX_X, ALU.add))
                flat = lambda v: v.rearrange("p a b -> p (a b)")
                link(V.tensor_tensor(in_blk, flat(place2).unsqueeze(2).to_broadcast([P, 2 * TT, NB + 1]),
                                     const("block_slots").unsqueeze(1).to_broadcast([P, 2 * TT, NB + 1]), ALU.is_ge))
                V.tensor_tensor(oh_blk, in_blk[:, :, 0:NB], in_blk[:, :, 1:NB + 1], ALU.subtract)
                link(V.tensor_reduce(flat(blk2), in_blk[:, :, 1:NB + 1], AX_X, ALU.add))
                link(V.scalar_tensor_tensor(out=slot2, in0=blk2, scalar=-float(BLK), in1=place2, op0=ALU.mult, op1=ALU.add))
                V.tensor_tensor(oh_slot, flat(slot2).unsqueeze(2).to_broadcast([P, 2 * TT, P]),
                                const("slot_of_col").unsqueeze(1).to_broadcast([P, 2 * TT, P]), ALU.is_equal)
                for n, v in enumerate((const("token_row"), const("out_row"), flat(w2))):
                    V.tensor_tensor(val_blk[:, :, n, :], oh_blk, v.unsqueeze(2).to_broadcast([P, 2 * TT, NB]),
                                    ALU.mult).then_inc(table_in[l], 1)
                link(V.tensor_tensor(order_tmp, oh_order, const("expert_id").unsqueeze(1).to_broadcast(by_e), ALU.mult))
                link(V.tensor_reduce(order_f, order_tmp, AX_X, ALU.add))
                V.tensor_copy(order_i[:, :], order_f)
                g = ("route", l, 3)
                acc_wait(g)
                tab = bank(g)[:, 0:3 * NB].rearrange("p (v b) -> p v b", v=3)
                V.tensor_copy(slot_w[:, :], tab[:, 2, :])
                V.tensor_scalar(row_i[:, 0, :], tab[:, 0, :], const("half"), None, ALU.add)
                V.tensor_scalar(row_i[:, 1, :], tab[:, 1, :], const("out_offset"), None, ALU.add).then_inc(route_ready[l], 1)
                bank_read[g] = (route_ready[l], 1)

            def ffn(l):
                norm = f"ffn{l}"
                modulate(norm, hT_cat, SEQ, lambda j: mod_a[:, 1 + 2 * l, j:j + 1], shift_of(l, 3, 0))
                if l == 0:
                    dve.wait_ge(router_in, 32)
                route(l)

                def turn_in():
                    for j in (0, 1, 4, 5):
                        at = j % 4 * P + (j // 4) * BLK
                        V.tensor_scalar(hgT[:, j, :], hg_dve_ps[:, at:at + BLK], mod_a[:, 1 + 2 * l, j:j + 1],
                                        shift_of(l, 3, 0)(j), ALU.mult, ALU.add).then_inc(hgT_dve[l], 1)

                dve.wait_ge(route_ready[l], 1)
                dve.wait_ge(gate_ffn_ready[l], 2)
                total = dve.value_load(block_start[0:1, NE:NE + 1], min_val=NE, max_val=MAXB)
                dve.wait_ge(hg_turned[l], 1)
                turn_in()

                def product(b):
                    dve.wait_ge(silu_ready[l], b + 1)
                    dve.wait_ge(up_done[l], b + 1)
                    V.tensor_tensor(act_sb, silu_g, up_ps[:, 0:256], ALU.mult).then_inc(act_ready[l], 1)

                def product_turned(b_plus_1):
                    dve.wait_ge(act_turned[l], b_plus_1)
                    V.tensor_copy(actT, at_ps[:, 0:256].rearrange("p (j s) -> p j s", j=2)).then_inc(actT_ready[l], 1)

                def result(b):
                    dve.wait_ge(down_done[l], b + 1)
                    dve.wait_ge(y_moved[l], b + 1)
                    V.scalar_tensor_tensor(out=y_blk, in0=y_ps, scalar=slot_w[:, bass.ds(b, 1)], in1=gate_ffn[:, :],
                                           op0=ALU.mult, op1=ALU.mult).then_inc(y_read[l], 1)

                product(0)
                dve.wait_ge(hg_turned[l], 2)
                turn_in()
                with dve.Fori(1, total) as b:
                    product_turned(b)
                    product(b)
                    dve.wait_ge(hg_turned[l], b + 2)
                    turn_in()
                    result(b - 1)
                product_turned(total)
                result(total - 1)
                if l == 0:
                    for m in GATES[1][0:2]:
                        fin(*m)
                for t in range(TT):
                    dve.wait_ge(yin[l][t], 32)
                    link(V.tensor_tensor(xs[:, t, :], xs[:, t, :], y_in[t][:, 0, :], ALU.add))
                    V.tensor_tensor(xs[:, t, :], xs[:, t, :], y_in[t][:, 1, :], ALU.add).then_inc(y_added[l], 1)

            dve.wait_ge(gates_ready, 2)
            mixer_out(0)
            ffn(0)

            normalise("mix1", xs, range(TT))
            modulate("mix1", hT_cat, SEQ, lambda j: mod_a[:, 2, j:j + 1], shift_of(1, 0, 0))
            for u in u_pad:
                V.memset(u[:, 0:1], 0.0)
                link(V.memset(u[:, SEQ + 1:SEQ + 2], 0.0))
            for h in range(2):
                for i in range(4):
                    m = 4 * h + i
                    up, y = u_pad[m % 2], sc_y[m % 2]
                    dve.wait_ge(gc_ready, m + 1)
                    acc_wait(("v", m))
                    V.tensor_tensor(up[:, 1:SEQ + 1], gc_sb[m % 2], bank(("v", m))[:, :], ALU.mult).then_inc(u_ready, 1)
                    bank_read[("v", m)] = (u_ready, m + 1)
                    dve.wait_ge(u_ready, m + 1)
                    link(V.tensor_scalar(y, up[:, 0:SEQ], taps[:, m, 31:32], None, ALU.mult))
                    for k in range(1, SC_K):
                        link(V.scalar_tensor_tensor(out=y, in0=up[:, k:k + SEQ], scalar=taps[:, m, 31 + k:32 + k], in1=y,
                                                    op0=ALU.mult, op1=ALU.add))
                    acc_wait(("gb", m))
                    V.tensor_tensor(mT[:, m, :], y, bank(("gb", m))[:, :], ALU.mult).then_inc(mT_ready, 1)
                    bank_read[("gb", m)] = (mT_ready, m + 1)
            dve.wait_ge(gates_ready, 4)
            mixer_out(1)
            ffn(1)

        @block.gpsimd
        def _(pool):
            G = nc.gpsimd
            pool.wait_ge(zeroed, 1)
            pool.wait_ge(consts_in, 16)
            half = const("minus_half")
            steps = [0]

            def passed(l, n):
                pool.wait_ge(ticked[l], n)
                G.tensor_tensor(tick[:, :], half, half, ALU.add).then_inc(ticked[l], 1)

            def link(ins):
                steps[0] += 1
                ins.then_inc(pool_step, 1)
                pool.wait_ge(pool_step, steps[0])

            def rsqrt(dst, src, n, scale):
                link(G.tensor_scalar(dst, src, scale, EPS, ALU.mult, ALU.add))
                return G.tensor_tensor(dst, dst, half.to_broadcast([P, n]), ALU.pow)

            def norm_rstd(norm, tiles):
                row, first = (2, TT) if norm == "ctx" else (1, 0)
                for t in range(tiles):
                    pool.wait_ge(ssq_ready[norm], t + 1)
                    rsqrt(stats[:, row, t:t + 1], stats[:, 0, first + t:first + t + 1], 1, 1.0 / D).then_inc(rstd_ready[norm], 1)

            norm_rstd("mix0", TT)
            norm_rstd("ctx", CT)
            pool.wait_ge(k_ssq, 1)
            rsqrt(head_stats[:, 0, 0:KT * KVH], head_stats[:, 0, 0:KT * KVH], KT * KVH, 1.0 / HD).then_inc(k_rstd, 1)
            for t in range(TT):
                pool.wait_ge(q_ssq, t + 1)
                rsqrt(head_stats[:, 1, 0:HEADS], head_stats[:, 1, 0:HEADS], HEADS, 1.0 / HD).then_inc(q_rstd, 1)
            for k in range(CONV_K):
                src, w = apad[:, 3, k:k + SEQ], taps[:, 3, k:k + 1]
                if k == 0:
                    pool.wait_ge(glu_ready, 4)
                    G.tensor_scalar(conv_y[:, 3, :], src, w, params[:, 35:36], ALU.mult, ALU.add).then_inc(pool_tap_done, 1)
                else:
                    pool.wait_ge(pool_tap_done, k)
                    link(G.tensor_scalar(tap_product, src, w, None, ALU.mult))
                    G.tensor_tensor(conv_y[:, 3, :], conv_y[:, 3, :], tap_product, ALU.add).then_inc(pool_tap_done, 1)
            pool.wait_ge(var_ready, 1)
            rsqrt(ln_col[:, 1, :], ln_col[:, 0, :], TT, 1.0 / CONV_C).then_inc(ln_rstd, 1)

            def ffn(l):
                norm_rstd(f"ffn{l}", TT)
                pool.wait_ge(route_ready[l], 1)
                total = pool.value_load(block_start[0:1, NE:NE + 1], min_val=NE, max_val=MAXB)
                pool.wait_ge(xhat_stored[l], 16 * TT)

                def gather(b, count):
                    G.tensor_copy(cur_idx[:, 0, :], row_i[:, 0, bass.ds(b, 1)]).then_inc(idx_ready[l], 1)
                    pool.wait_ge(idx_ready[l], count)
                    passed(l, count)
                    G.indirect_dma_start(out=hg_raw, out_offset=None, in_=xhat_d,
                                         in_offset=bass.IndirectOffsetOnAxis(ap=cur_idx[:, 0, :], axis=0),
                                         bounds_check=2 * SEQ - 1, oob_is_err=False).then_inc(hg_in[l], 16)

                def scatter(b, count, moved):
                    G.tensor_tensor(y_out, y_blk, const("ones")[:, 0:1].to_broadcast([P, 512]), ALU.mult).then_inc(y_moved[l], 1)
                    G.tensor_copy(cur_idx[:, 1, :], row_i[:, 1, bass.ds(b, 1)]).then_inc(idx_ready[l], 1)
                    pool.wait_ge(idx_ready[l], count)
                    pool.wait_ge(y_moved[l], moved)
                    passed(l, count)
                    G.indirect_dma_start(out=y_d[l], out_offset=bass.IndirectOffsetOnAxis(ap=cur_idx[:, 1, :], axis=0),
                                         in_=y_out, in_offset=None, bounds_check=4 * SEQ - 1,
                                         oob_is_err=False).then_inc(y_stored[l], 16)

                gather(0, 1)
                scatter(NB - 1, 2, 1)
                for n in range(1, 3):
                    pool.wait_ge(hg_moved[l], n)
                    gather(n, 2 + n)
                pool.wait_ge(hg_moved[l], 3)
                gather(3, 5)

                def store(b, count):
                    pool.wait_ge(y_read[l], b + 2)
                    pool.wait_ge(y_stored[l], b * 16 + 16)
                    scatter(b, count, b + 2)

                with pool.Fori(1, total) as b:
                    pool.wait_ge(hg_moved[l], b + 3)
                    gather(b + 3, b * 2 + 4)
                    store(b - 1, b * 2 + 5)
                store(total - 1, total * 2 + 4)
                pool.wait_ge(hg_in[l], total * 16 + 48)
                passed(l, total * 2 + 5)

            ffn(0)
            norm_rstd("mix1", TT)
            ffn(1)

        @block.tensor
        def _(pe):
            T = nc.tensor
            at = [0]

            def open_group(name):
                n = at[0]
                assert GROUPS[n] == name, (GROUPS[n], name)
                at[0] += 1
                if n >= NBANK:
                    pe.wait_ge(*bank_read[GROUPS[n - NBANK]])
                return psum[n % NBANK]

            def unit_wait(name):
                pe.wait_ge(unit_in[unit_slot[name]], unit_count[name])
                return unit(name)

            def close(mm):
                mm.then_inc(acc_done, 1)

            pe.wait_ge(consts_in, 16)
            pe.wait_ge(zeroed, 1)
            pe.wait_ge(rows_in, 16 * 7)
            ps = open_group(("params",))
            close(T.transpose(ps[:, 0:44], staging[0:44, 0:P], ident[0:44, 0:44]))
            ps = open_group(("taps",))
            for j in range(KD):
                mm = T.transpose(ps[:, j * 34:(j + 1) * 34], hT_cat[0:34, j // 4, (j % 4) * P:(j % 4 + 1) * P], ident[0:34, 0:34])
            close(mm)

            ps = open_group(("bias",))
            pe.wait_ge(bmod_in, 16)
            for j in range(4):
                mm = T.transpose(ps[:, j * 24:(j + 1) * 24], b_rows[0:24, j * P:(j + 1) * P], ident[0:24, 0:24])
            close(mm)

            mods = [0]

            def mod_rows(l, c):
                ps = open_group(("mod", l, c))
                w = unit_wait(("mod", l, c))
                if not mods[0]:
                    pe.wait_ge(cact_ready, 2)
                for k in range(KD):
                    q = k % 4
                    mm = T.matmul(ps[32 * q:32 * q + 32, :], cact[:, k, :], w[:, k, :], start=(k < 4), stop=(k >= 4))
                close(mm)

            def mod_fin(l, c):
                mods[0] += 1
                ps = open_group(("fin", l, c))
                pe.wait_ge(modrow_ready, mods[0])
                bias_row = ident[:, 12 * l + c:12 * l + c + 1]
                if c in (4, 5):
                    T.matmul(ps[:, :], const("sel_x"), modrow[:, :], start=True, stop=False)
                    mm = T.matmul(ps[:, :], bias_row.to_broadcast([P, P]), b_rows[:, :], start=False, stop=True)
                elif c in (10, 11):
                    h = c - 10
                    T.matmul(ps[h * 64:(h + 1) * 64, :], const("sel_x")[:, 0:64], modrow[:, :], start=True, stop=False)
                    mm = T.matmul(ps[h * 64:(h + 1) * 64, :], bias_row.to_broadcast([P, 64]), b_rows[:, :], start=False, stop=True)
                else:
                    for j in range(4):
                        mm = T.matmul(ps[:, 2 * j:2 * j + 2], modrow[:, j * P:(j + 1) * P], const("sel_both"), start=True, stop=True)
                close(mm)

            def norm_turn(norm, src, tiles):
                pe.wait_ge(xhat_ready[norm], tiles)
                for j in range(KD):
                    ps = open_group(("norm", norm, j))
                    for t in range(tiles):
                        mm = T.transpose(ps[:, t * P:(t + 1) * P], src[:, t, j * P:(j + 1) * P], ident)
                    close(mm)

            for c_ in range(4):
                mod_rows(0, c_)
                mod_fin(0, c_)
            norm_turn("ctx", ctx_hat, CT)
            norm_turn("mix0", xhat, TT)
            def hT_wait(norm):
                pe.wait_ge(hT_even[norm], KD // 2)
                pe.wait_ge(hT_odd[norm], KD // 2)


            def tokens_out(name, lhs, t, w, n):
                ps = open_group(name)
                for k in range(KD):
                    mm = T.matmul(ps[:, 0:n], lhs[:, k, t * P:(t + 1) * P], w[:, k, 0:n], start=(k == 0), stop=(k == KD - 1))
                close(mm)

            def channels_out(name, i, w):
                ps = open_group(name)
                for k in range(KD):
                    mm = T.matmul(ps[:, :], w[:, k, i * P:(i + 1) * P], hT_cat[:, k, :], start=(k == 0), stop=(k == KD - 1))
                close(mm)

            w = unit_wait(("kv",))
            hT_wait("ctx")
            for t in range(CT):
                tokens_out(("kvz", t), hzT, t, w, 256)
            hT_wait("mix0")
            for t in range(TT):
                tokens_out(("kvx", t), hT_cat, t, w, 256)
            w = unit_wait(("a",))
            for i in range(4):
                channels_out(("a", i), i, w)
                if i:
                    mod_fin(*WITH_A[i - 1])
                mod_rows(*WITH_A[i])
            w = unit_wait(("ag",))
            for i in range(4):
                channels_out(("ag", i), i, w)
                mod_fin(*([WITH_A[3]] + WITH_AG)[i])
                mod_rows(*WITH_AG[i])
            for v in range(KVH):
                for h in range(2):
                    ps = open_group(("kT", v, h))
                    pe.wait_ge(k_roped, TT)
                    for t in range(3):
                        for half in range(2):
                            mm = T.matmul(ps[half * 64:(half + 1) * 64, t * P:(t + 1) * P], ktok[:, 3 * h + t, v * HD:(v + 1) * HD],
                                          ident, start=True, stop=True)
                    close(mm)
            w = unit_wait(("q",))
            for t in range(TT):
                tokens_out(("q", t), hT_cat, t, w, 512)
                if t == 0:
                    mod_fin(*WITH_AG[3])
            for m in WITH_Q:
                mod_rows(*m)
                mod_fin(*m)
            for i in range(PAIRS):
                ps = open_group(("qT", i))
                pe.wait_ge(q_roped, TT)
                for t in range(TT):
                    mm = T.transpose(ps[:, t * P:(t + 1) * P], qtok[:, t, i * P:(i + 1) * P], ident)
                close(mm)

            def scores(n):
                s, u = n // 4, n % 4
                pair, qt = s // 2, (s % 2) * 2 + u % 2
                r = slice((u // 2) * 64, (u // 2) * 64 + 64)
                pe.wait_ge(qT_ready, pair + 1)
                if n >= 2:
                    pe.wait_ge(exp_ready, n - 1)
                for a, b in ((0, 512), (512, KT * P)):
                    mm = T.matmul(score_ps[n % 2][:, a:b], qT[r, pair, qt * P:(qt + 1) * P], kT2[r, pair // 2, a:b],
                                  start=True, stop=True)
                mm.then_inc(scores_done, 1)

            def values(s):
                ps = open_group(("pv", s))
                pe.wait_ge(PT_ready, 8 * s + 8)
                kvh = s // 4
                for k in range(KT):
                    for hh in range(2):
                        mm = T.matmul(ps[hh * 64:(hh + 1) * 64, 0:256], vtok[:, k, kvh * HD:(kvh + 1) * HD], PT[s % 2][hh][:, k, :],
                                      start=(k == 0), stop=(k == KT - 1))
                close(mm)

            def layer_norm(s, u):
                for name, at in LN_AT.items():
                    if at != (s, u):
                        continue
                    ps = open_group((name,))
                    if name == "ln_rstd":
                        pe.wait_ge(diag_ready, 1)
                        close(T.matmul(ps[:, :], const("ones"), diag.rearrange("p t q -> p (t q)"), start=True, stop=True))
                        continue
                    if name == "mu":
                        pe.wait_ge(tap_done, 3 * CONV_K)
                        pe.wait_ge(pool_tap_done, CONV_K)
                    else:
                        pe.wait_ge(sq_ready, 4)
                    src = conv_y if name == "mu" else apad[:, :, 0:SEQ]
                    for i in range(4):
                        mm = T.matmul(ps[:, :], const("ones"), src[:, i, :], start=(i == 0), stop=(i == 3))
                    close(mm)

            pe.wait_ge(kT_ready, 2 * KVH)
            scores(0)
            for s in range(8):
                for u in range(4):
                    n = 4 * s + u
                    if n + 1 < 32:
                        scores(n + 1)
                    pe.wait_ge(prob_ready, n + 1)
                    for g3 in range(2):
                        ps = open_group(("PT", s, u, g3))
                        for k in range(3):
                            mm = T.transpose(ps[:, k * P:(k + 1) * P], prob[:, n % 2, (3 * g3 + k) * P:(3 * g3 + k + 1) * P], ident)
                        close(mm)
                    if u == 0 and s:
                        values(s - 1)
                    layer_norm(s, u)
                    if (s, u) in GATE_AT:
                        kind, l, c = GATE_AT[s, u]
                        (mod_rows if kind == "mod" else mod_fin)(l, c)
            values(7)

            def mixer_out(l, lhs, unit_name):
                def product(ps, t, w, chunks):
                    for k in chunks:
                        mm = T.matmul(ps[:, :], lhs[:, k, t * P:(t + 1) * P], w[:, k, :], start=(k == 0), stop=(k == KD - 1))
                    return mm

                for h in range(2):
                    w = unit_wait((unit_name, h))
                    if l == 0 and h == 0:
                        banks = [open_group(("out", l, h, t)) for t in range(TT)]
                        for t in range(TT):
                            product(banks[t], t, w, range(KD // 2))
                        pe.wait_ge(cat_ready, 4)
                        for t in range(TT):
                            close(product(banks[t], t, w, range(KD // 2, KD)))
                        continue
                    for t in range(TT):
                        ps = open_group(("out", l, h, t))
                        close(product(ps, t, w, range(KD)))

            def ffn(l):
                norm_turn(f"ffn{l}", xhat, TT)
                ps = open_group(("route", l, 0))
                hT_wait(f"ffn{l}")
                if l == 0:
                    pe.wait_ge(router_in, 32)
                for k in range(KD):
                    q = k % 4
                    mm = T.matmul(ps[32 * q:32 * q + 32, :], route_w[:, k, :], hT_cat[:, k, :], start=(k < 4), stop=(k >= 4))
                close(mm)
                mod_rows(*GATES[l][2])
                ps = open_group(("route", l, 1))
                pe.wait_ge(router_turned[l], 1)
                for t in range(TT):
                    mm = T.matmul(ps[:, t * NE:(t + 1) * NE], router_rows[:, t * P:(t + 1) * P], const("sel_expert"),
                                  start=True, stop=True)
                close(mm)
                mod_fin(*GATES[l][2])
                mod_rows(*GATES[l][3])
                mod_fin(*GATES[l][3])
                ps = open_group(("route", l, 2))
                pe.wait_ge(mask_ready[l], 1)
                rows = picked.rearrange("p t e -> p (t e)")
                T.matmul(ps[:, 0:TT * NE], const("before"), rows, start=True, stop=True)
                close(T.matmul(ps[:, TT * NE:2 * TT * NE], const("ones"), rows, start=True, stop=True))
                ps = open_group(("route", l, 3))
                pe.wait_ge(table_in[l], 3)
                for n in range(2 * TT):
                    mm = T.matmul(ps[:, 0:3 * NB], oh_slot[:, n, :], val_blk[:, n, :, :].rearrange("p v b -> p (v b)"),
                                  start=(n == 0), stop=(n == 2 * TT - 1))
                close(mm)

                pe.wait_ge(route_ready[l], 1)

                def turn(count):
                    pe.wait_ge(hg_moved[l], count)
                    for j in range(4):
                        mm = T.transpose((hg_dve_ps, hg_act_ps)[j // 2][:, j % 2 * P:(j % 2 + 1) * P], hg_next[:, j * P:(j + 1) * P], ident)
                    mm.then_inc(hg_turned[l], 1)

                turn(1)

                def landed(i, par, k):
                    slot = EXPERT_SETS[l][par][k]
                    pe.wait_ge(unit_in[slot], i * 16 + (moe_base[l][slot] + 1) * 16)
                    return expert_view(slot, "wd" if k == 2 else "wg")

                def half_columns(ps, w, done):
                    for k in range(KD):
                        for h in range(2):
                            mm = T.matmul(ps[h * BLK:(h + 1) * BLK, 0:256], hgT[:, k, :], w[:, k, h * 256:(h + 1) * 256],
                                          start=(k == 0), stop=(k == KD - 1))
                    mm.then_inc(done, 1)

                def turn_product(b_plus_1):
                    pe.wait_ge(act_ready[l], b_plus_1 + 1)
                    for j in range(2):
                        mm = T.transpose(at_ps[:, j * P:(j + 1) * P], act_sb[:, j * P:(j + 1) * P], ident)
                    mm.then_inc(act_turned[l], 1)

                def down(b_plus_1, i, par):
                    wd = landed(i, par, 2)
                    pe.wait_ge(actT_ready[l], b_plus_1)
                    pe.wait_ge(y_read[l], b_plus_1)
                    for k in range(4):
                        for h in range(2):
                            mm = T.matmul(y_ps[h * BLK:(h + 1) * BLK, :], actT[:, k % 2, (k // 2) * BLK:(k // 2 + 1) * BLK],
                                          wd[:, k, h * 512:(h + 1) * 512], start=(k == 0), stop=(k == 3))
                    mm.then_inc(down_done[l], 1)

                def block_of(b, i, par, i_before, par_before):
                    pe.wait_ge(hgT_dve[l], b * 4 + 4)
                    pe.wait_ge(hgT_act[l], b * 4 + 4)
                    half_columns(gate_ps, landed(i, par, 0), gate_done[l])
                    turn_product(b)
                    half_columns(up_ps, landed(i, par, 1), up_done[l])
                    turn(b + 2)
                    down(b, i_before, par_before)

                def later_blocks(e, i, par):
                    first = pe.value_load(block_start[0:1, bass.ds(e, 1)], min_val=0, max_val=MAXB)
                    end = pe.value_load(block_start[0:1, bass.ds(e + 1, 1)], min_val=1, max_val=MAXB)
                    with pe.If(first + 1 < end):
                        with pe.Fori(first + 1, end) as b:
                            block_of(b, i, par, i, par)

                pe.wait_ge(hgT_dve[l], 4)
                pe.wait_ge(hgT_act[l], 4)
                half_columns(gate_ps, landed(0, 0, 0), gate_done[l])
                half_columns(up_ps, landed(0, 0, 1), up_done[l])
                turn(2)
                later_blocks(0, 0, 0)
                with pe.Fori(0, NE // 3) as i:
                    for n in range(1, 4):
                        i_own, par = (i, n) if n < 3 else (i + 1, 0)
                        b = pe.value_load(block_start[0:1, bass.ds(i * 3 + n, 1)], min_val=1, max_val=MAXB)
                        block_of(b, i_own, par, i, n - 1)
                        later_blocks(i * 3 + n, i_own, par)
                total = pe.value_load(block_start[0:1, NE:NE + 1], min_val=NE, max_val=MAXB)
                turn_product(total)
                down(total, NE // 3, 0)
                pe.wait_ge(y_read[l], total + 1)
                pe.wait_ge(hgT_dve[l], total * 4 + 4)
                pe.wait_ge(hgT_act[l], total * 4 + 4)

            pe.wait_ge(attn_ready, 8)
            mixer_out(0, hT_cat, "wo")
            ffn(0)

            for m in GATES[1][0:2]:
                mod_rows(*m)
                mod_fin(*m)
            norm_turn("mix1", xhat, TT)
            hT_wait("mix1")
            for h in range(2):
                w = {n: unit_wait((n, h)) for n in ("gc", "v", "gb")}
                for i in range(4):
                    for n in ("gc", "v", "gb"):
                        ps = open_group((n, 4 * h + i))
                        for k in range(KD):
                            mm = T.matmul(ps[:, :], w[n][:, k, i * P:(i + 1) * P], hT_cat[:, k, :], start=(k == 0), stop=(k == KD - 1))
                        close(mm)
            pe.wait_ge(mT_ready, KD)
            mixer_out(1, mT, "ow")
            ffn(1)
            assert at[0] == len(GROUPS)


_INS = ["x", "c", "ctx", "c_ctx", "w_mod", "b_mod", "norm_mix_g", "norm_ffn_g", "ev_w_in", "ev_q_norm_g", "ev_k_norm_g",
        "ev_dw_w", "ev_dw_b", "ev_ln_g", "ev_ln_b", "ev_w_out", "od_w_in", "od_conv_w", "od_w_out", "router_w",
        "router_bias", "moe_w_gate", "moe_w_up", "moe_w_down"]


def kernel(**inputs):
    import concourse.bacc as bacc
    from concourse.bass_utils import run_bass_kernel_spmd

    nc = bacc.Bacc("TRN2", target_bir_lowering=False, num_devices=1)
    arrays, args = {}, []
    values = {name: np.ascontiguousarray(inputs[name]) for name in _INS}
    values["consts"] = build_consts()
    for name, a in values.items():
        arrays[f"in_{name}"] = a
        args.append(nc.dram_tensor(f"in_{name}", a.shape, mybir.dt.from_np(a.dtype), kind="ExternalInput").ap())
    out = nc.dram_tensor("out_x", (1, SEQ, D), F32, kind="ExternalOutput").ap()
    hybrid_backbone_kernel(nc, *args, out)
    r = run_bass_kernel_spmd(nc, [arrays], core_ids=[0])
    return r.results[0]["out_x"]
```
